# Optimizing a Trainium2 kernel written in Bass

```python
import math
import jax, jax.numpy as jnp
from jax import lax
import numpy as np
import jax
import jax.numpy as jnp

D_MODEL = 1024
BATCH = 1
SEQ = 256
DEPTH = 2

CHUNK = 64
N_MEM = 256
D_MIX = D_MODEL
D_GLA = D_MIX // 2
D_SGU = D_MIX - D_GLA
GLA_HEADS = 4
D_QK = D_GLA // 2
GLA_DK = D_QK // GLA_HEADS
GLA_DV = D_GLA // GLA_HEADS
GATE_RANK = 16
GATE_TEMP = 16.0
SGU_GROUPS = 4
SGU_BLOCK = 128
SGU_CH = D_SGU // SGU_GROUPS
XATTN_HEADS = 4
XATTN_DH = D_MODEL // XATTN_HEADS
N_EXPERTS = 16
N_EXPERT_GROUPS = 4
EXPERTS_PER_GROUP = N_EXPERTS // N_EXPERT_GROUPS
TOP_K = 2
D_EXPERT = D_MODEL // 2
DN_ALPHA = (2.0 * DEPTH) ** 0.25
DN_BETA = (8.0 * DEPTH) ** -0.25
LN_EPS = 1e-5
RMS_EPS = 1e-6
D_IN = 2 * D_QK + 2 * D_GLA + GATE_RANK + 2 * D_SGU


def layer_norm(x, g, b):
    xf = x.astype(jnp.float32)
    mu = jnp.mean(xf, axis=-1, keepdims=True)
    var = jnp.mean(jnp.square(xf - mu), axis=-1, keepdims=True)
    y = (xf - mu) * lax.rsqrt(var + LN_EPS)
    return (y * g.astype(jnp.float32) + b.astype(jnp.float32)).astype(x.dtype)

def split_proj(p):
    sizes = (D_QK, D_QK, D_GLA, D_GLA, GATE_RANK, D_SGU, D_SGU)
    outs, start = [], 0
    for s in sizes:
        outs.append(p[..., start:start + s])
        start += s
    return outs

def gla_group(q, k, v, r, a_low, w_a2, b_a, gn_g):
    B, S, _ = q.shape
    nc = S // CHUNK
    log_a = jax.nn.log_sigmoid((a_low @ w_a2 + b_a).astype(jnp.float32)) / GATE_TEMP

    def to_chunks(t, d):
        return t.astype(jnp.float32).reshape(B, nc, CHUNK, GLA_HEADS, d).transpose(1, 0, 3, 2, 4)

    qc = to_chunks(q, GLA_DK) * (GLA_DK ** -0.5)
    kc = to_chunks(k, GLA_DK)
    vc = to_chunks(v, GLA_DV)
    gc = to_chunks(log_a, GLA_DK)

    def step(state, inp):
        q_c, k_c, v_c, g_c = inp
        bcum = jnp.cumsum(g_c, axis=2)
        b_last = bcum[:, :, -1:, :]
        k_dec = k_c * jnp.exp(b_last - bcum)
        state = jnp.exp(b_last[:, :, 0, :])[..., None] * state + jnp.einsum('bhck,bhcv->bhkv', k_dec, v_c)
        o = jnp.einsum('bhck,bhkv->bhcv', q_c, state)
        return state, o

    s0 = jnp.zeros((B, GLA_HEADS, GLA_DK, GLA_DV), jnp.float32)
    _, o = lax.scan(step, s0, (qc, kc, vc, gc))
    o = o.transpose(1, 0, 3, 2, 4).reshape(B, S, GLA_HEADS, GLA_DV)
    o = o * lax.rsqrt(jnp.mean(jnp.square(o), axis=-1, keepdims=True) + RMS_EPS)
    o = o.reshape(B, S, D_GLA) * gn_g.astype(jnp.float32)
    out = o * jax.nn.silu(r.astype(jnp.float32))
    return out.astype(q.dtype)

def sgu_group(u, v, w_s, b_s, ln_g, ln_b):
    B, S, _ = u.shape
    nb = S // SGU_BLOCK
    u = jax.nn.gelu(u)
    v = jax.nn.gelu(v).reshape(B, S, SGU_GROUPS, SGU_CH)
    v = layer_norm(v, ln_g.reshape(SGU_GROUPS, SGU_CH), ln_b.reshape(SGU_GROUPS, SGU_CH))
    v = v.reshape(B, nb, SGU_BLOCK, SGU_GROUPS, SGU_CH)
    pos = jnp.arange(SGU_BLOCK)
    mask = (pos[None, :] // CHUNK) <= (pos[:, None] // CHUNK)
    w_m = jnp.where(mask[None], w_s, jnp.zeros_like(w_s))
    mixed = jnp.einsum('gts,bnsgc->bntgc', w_m, v) + b_s.T[None, None, :, :, None]
    out = u.reshape(B, nb, SGU_BLOCK, SGU_GROUPS, SGU_CH) * mixed
    return out.reshape(B, S, D_SGU)

def mem_xattn(x, mem, wq, wk, wv, wo):
    B, S, _ = x.shape
    M = mem.shape[1]
    q = (x @ wq).reshape(B, S, XATTN_HEADS, XATTN_DH)
    k = (mem @ wk).reshape(B, M, XATTN_HEADS, XATTN_DH)
    v = (mem @ wv).reshape(B, M, XATTN_HEADS, XATTN_DH)
    s = jnp.einsum('bshd,bmhd->bhsm', q, k).astype(jnp.float32) * (XATTN_DH ** -0.5)
    p = jax.nn.softmax(s, axis=-1).astype(v.dtype)
    o = jnp.einsum('bhsm,bmhd->bshd', p, v).reshape(B, S, D_MODEL)
    return o @ wo

def grouped_moe(x, w_router, b_router, w_gate, w_up, w_down):
    B, S, D = x.shape
    xt = x.reshape(B * S, D)
    scores = jax.nn.softmax((xt @ w_router + b_router).astype(jnp.float32), axis=-1)
    grp = scores.reshape(-1, N_EXPERT_GROUPS, EXPERTS_PER_GROUP)
    group_score = jnp.sum(lax.top_k(grp, TOP_K)[0], axis=-1)
    g_sel = jnp.argmax(group_score, axis=-1)
    in_grp = jnp.sum(grp * jax.nn.one_hot(g_sel, N_EXPERT_GROUPS, dtype=jnp.float32)[:, :, None], axis=1)
    top_w, top_i = lax.top_k(in_grp, TOP_K)
    top_w = top_w / jnp.sum(top_w, axis=-1, keepdims=True)
    eid = g_sel[:, None] * EXPERTS_PER_GROUP + top_i
    gate = jnp.sum(jax.nn.one_hot(eid, N_EXPERTS, dtype=jnp.float32) * top_w[..., None], axis=1)
    gate = gate.astype(x.dtype)
    y = jnp.zeros_like(xt)
    for e in range(N_EXPERTS):
        h = jax.nn.silu(xt @ w_gate[e]) * (xt @ w_up[e])
        y = y + gate[:, e:e + 1] * (h @ w_down[e])
    return y.reshape(B, S, D)

def first_inputs(seed: int = 0) -> dict:
    key = jax.random.key(seed)
    ks = jax.random.split(key, 24)
    f32 = jnp.float32

    def nrm(k, shape, fan_in, scale=1.0):
        return jax.random.normal(k, shape, f32) * (scale * fan_in ** -0.5)

    def gain(k, shape):
        return 1.0 + 0.02 * jax.random.normal(k, shape, f32)

    return {
        "x": jax.random.normal(ks[0], (BATCH, SEQ, D_MODEL), f32),
        "mem": jax.random.normal(ks[1], (BATCH, N_MEM, D_MODEL), f32),
        "w_in": nrm(ks[2], (DEPTH, D_MODEL, D_IN), D_MODEL),
        "w_a2": nrm(ks[3], (DEPTH, GATE_RANK, D_QK), GATE_RANK),
        "b_a": 1.0 + 0.5 * jax.random.normal(ks[4], (DEPTH, D_QK), f32),
        "gla_norm_g": gain(ks[5], (DEPTH, D_GLA)),
        "w_s": nrm(ks[6], (DEPTH, SGU_GROUPS, SGU_BLOCK, SGU_BLOCK), SGU_BLOCK),
        "b_s": gain(ks[7], (DEPTH, SGU_GROUPS, SGU_BLOCK)),
        "sgu_ln_g": gain(ks[8], (DEPTH, D_SGU)),
        "sgu_ln_b": 0.02 * jax.random.normal(ks[9], (DEPTH, D_SGU), f32),
        "w_out": nrm(ks[10], (DEPTH, D_MIX, D_MODEL), D_MIX, DN_BETA),
        "wq_x": nrm(ks[11], (DEPTH, D_MODEL, D_MODEL), D_MODEL),
        "wk_x": nrm(ks[12], (DEPTH, D_MODEL, D_MODEL), D_MODEL),
        "wv_x": nrm(ks[13], (DEPTH, D_MODEL, D_MODEL), D_MODEL),
        "wo_x": nrm(ks[14], (DEPTH, D_MODEL, D_MODEL), D_MODEL, DN_BETA),
        "w_router": nrm(ks[15], (D_MODEL, N_EXPERTS), D_MODEL),
        "b_router": 0.01 * jax.random.normal(ks[16], (N_EXPERTS,), f32),
        "w_gate": nrm(ks[17], (DEPTH, N_EXPERTS, D_MODEL, D_EXPERT), D_MODEL),
        "w_up": nrm(ks[18], (DEPTH, N_EXPERTS, D_MODEL, D_EXPERT), D_MODEL),
        "w_down": nrm(ks[19], (DEPTH, N_EXPERTS, D_EXPERT, D_MODEL), D_EXPERT, DN_BETA),
        "ln_g": gain(ks[20], (DEPTH, 3, D_MODEL)),
        "ln_b": 0.02 * jax.random.normal(ks[21], (DEPTH, 3, D_MODEL), f32),
    }

def first_block(x, mem, w_in, w_a2, b_a, gla_norm_g, w_s, b_s, sgu_ln_g, sgu_ln_b, w_out,
              wq_x, wk_x, wv_x, wo_x, w_router, b_router, w_gate, w_up, w_down, ln_g, ln_b):
    for l in range(DEPTH):
        q, k, v, r, a_low, u, v_sgu = split_proj(x @ w_in[l])
        y_gla = gla_group(q, k, v, r, a_low, w_a2[l], b_a[l], gla_norm_g[l])
        y_sgu = sgu_group(u, v_sgu, w_s[l], b_s[l], sgu_ln_g[l], sgu_ln_b[l])
        h = jnp.concatenate([y_gla, y_sgu], axis=-1) @ w_out[l]
        x = layer_norm(DN_ALPHA * x + h, ln_g[l, 0], ln_b[l, 0])
        h = mem_xattn(x, mem, wq_x[l], wk_x[l], wv_x[l], wo_x[l])
        x = layer_norm(DN_ALPHA * x + h, ln_g[l, 1], ln_b[l, 1])
        h = grouped_moe(x, w_router, b_router, w_gate[l], w_up[l], w_down[l])
        x = layer_norm(DN_ALPHA * x + h, ln_g[l, 2], ln_b[l, 2])
    return x


N_EVEN = (DEPTH + 1) // 2
N_ODD = DEPTH // 2

HEAD_DIM = 64
NEG = -1e30
BIG = 1e30
NORM_EPS = 1e-6

N_BUCKETS = 32
MAX_DISTANCE = 1024
N_BIAS_HEADS = 8

NSA_HEADS = 8
NSA_KV_HEADS = 2
NSA_GROUP = NSA_HEADS // NSA_KV_HEADS
CMP_LEN = 32
CMP_STRIDE = 16
CMP_HIDDEN = 256
SLC_BLOCK = 64
SLC_TOPN = 16
NSA_WINDOW = 512
NSA_QBLOCK = 128

MOBA_HEADS = 8
MOBA_BLOCK = 256
MOBA_TOPK = 3
MOBA_QBLOCK = 32

MLA_HEADS = 4
MLA_Q_RANK = 256
MLA_KV_RANK = 128
MLA_NOPE = 128
MLA_ROPE = 64
MLA_V = 128
ROPE_THETA = 10000.0
DENSE_QBLOCK = 128

SWA_HEADS = 8
SWA_KV_HEADS = 2
SWA_GROUP = SWA_HEADS // SWA_KV_HEADS
SWA_WINDOW = 128
SWA_QBLOCK = 128

N_GROUPS = 4
EXPERTS_PER_GROUP_2 = N_EXPERTS // N_GROUPS
D_EXPERT_2 = 512
MOE_BLOCK = 256

ADA_INIT = 0.5

EVEN_WIDTHS = (NSA_HEADS * HEAD_DIM,) + (NSA_KV_HEADS * HEAD_DIM,) * 6 + (3 * NSA_HEADS,) + (MOBA_HEADS * HEAD_DIM,) * 3
EVEN_IN = sum(EVEN_WIDTHS)
EVEN_OUT = NSA_HEADS * HEAD_DIM + MOBA_HEADS * HEAD_DIM
ODD_WIDTHS = (MLA_Q_RANK, MLA_KV_RANK, MLA_ROPE, SWA_HEADS * HEAD_DIM, SWA_KV_HEADS * HEAD_DIM, SWA_KV_HEADS * HEAD_DIM)
ODD_IN = sum(ODD_WIDTHS)
ODD_OUT = MLA_HEADS * MLA_V + SWA_HEADS * HEAD_DIM


def rmsnorm(x, g):
    xf = x.astype(jnp.float32)
    y = xf * lax.rsqrt(jnp.mean(xf * xf, axis=-1, keepdims=True) + NORM_EPS)
    return (y * g.astype(jnp.float32)).astype(x.dtype)

def split_cols(x, widths):
    idx, acc = [], 0
    for w in widths[:-1]:
        acc += w
        idx.append(acc)
    return jnp.split(x, idx, axis=-1)

def masked_softmax(s, mask):
    s = jnp.where(mask, s.astype(jnp.float32), NEG)
    p = jax.nn.softmax(s, axis=-1)
    return jnp.where(mask, p, 0.0)

def rel_bucket(dist):
    exact = N_BUCKETS // 2
    d = jnp.maximum(dist, 0)
    log_part = exact + (jnp.log(jnp.maximum(d, 1).astype(jnp.float32) / exact)
                        / math.log(MAX_DISTANCE / exact) * (N_BUCKETS - exact)).astype(jnp.int32)
    return jnp.where(d < exact, d, jnp.minimum(log_part, N_BUCKETS - 1))

def shared_bias(rel_table, dist, n_kv):
    b = jnp.moveaxis(rel_table[rel_bucket(dist)], -1, 0).astype(jnp.float32)
    return b.reshape(n_kv, -1, *dist.shape)

def gathered_bias(rel_table, dist, n_kv):
    table = rel_table.reshape(N_BUCKETS, n_kv, -1)
    kv = jnp.arange(n_kv)[None, :, None, None]
    return jnp.moveaxis(table[rel_bucket(dist), kv], -1, 2).astype(jnp.float32)

def rope_tables(S, dim):
    inv = ROPE_THETA ** (-jnp.arange(0, dim, 2, dtype=jnp.float32) / dim)
    ang = jnp.arange(S, dtype=jnp.float32)[:, None] * inv[None, :]
    return jnp.cos(ang), jnp.sin(ang)

def apply_rope(x, cos, sin):
    half = x.shape[-1] // 2
    x1 = x[..., :half].astype(jnp.float32)
    x2 = x[..., half:].astype(jnp.float32)
    return jnp.concatenate([x1 * cos - x2 * sin, x1 * sin + x2 * cos], axis=-1).astype(x.dtype)

def adaln(c, w, b):
    m = jax.nn.silu(c) @ w + b
    return jnp.split(m[:, None, :], 6, axis=-1)

def nsa_attention(q, kc, vc, ks, vs, kw, vw, gates, pos_k, pos_v, ck_w1, ck_w2, cv_w1, cv_w2, rel_table):
    B, S, _ = q.shape
    Hk, G, dh, QB = NSA_KV_HEADS, NSA_GROUP, HEAD_DIM, NSA_QBLOCK
    scale = dh ** -0.5
    q = q.reshape(B, S, Hk, G, dh).transpose(0, 2, 3, 1, 4)
    to_kv = lambda t: t.reshape(B, S, Hk, dh).transpose(0, 2, 1, 3)
    kc, vc, ks, vs, kw, vw = (to_kv(t) for t in (kc, vc, ks, vs, kw, vw))
    g = jax.nn.sigmoid(gates.astype(jnp.float32)).reshape(B, S, Hk, G, 3).transpose(0, 2, 3, 1, 4)

    n_cmp = (S - CMP_LEN) // CMP_STRIDE + 1
    cmp_start = np.arange(n_cmp, dtype=np.int32) * CMP_STRIDE
    win_idx = cmp_start[:, None] + np.arange(CMP_LEN, dtype=np.int32)[None, :]
    cmp_end = cmp_start + CMP_LEN - 1

    def compress(t, pos, w1, w2):
        blocks = t[:, :, win_idx, :] + pos
        flat = blocks.reshape(B, Hk, n_cmp, CMP_LEN * dh)
        return jax.nn.gelu(flat @ w1) @ w2

    k_cmp = compress(kc, pos_k, ck_w1, ck_w2)
    v_cmp = compress(vc, pos_v, cv_w1, cv_w2)

    n_slc = S // SLC_BLOCK
    slc_lo = np.arange(n_slc, dtype=np.int32) * SLC_BLOCK
    overlap = ((cmp_start[:, None] <= slc_lo[None, :] + SLC_BLOCK - 1)
               & (cmp_end[:, None] >= slc_lo[None, :])).astype(np.float32)
    n_sel = min(SLC_TOPN, n_slc)
    ks_blocks = ks.reshape(B, Hk, n_slc, SLC_BLOCK, dh)
    vs_blocks = vs.reshape(B, Hk, n_slc, SLC_BLOCK, dh)

    pad = ((0, 0), (0, 0), (NSA_WINDOW, 0), (0, 0))
    kw_pad, vw_pad = jnp.pad(kw, pad), jnp.pad(vw, pad)

    nq = S // QB
    q_blocks = jnp.moveaxis(q.reshape(B, Hk, G, nq, QB, dh), 3, 0)
    g_blocks = jnp.moveaxis(g.reshape(B, Hk, G, nq, QB, 3), 3, 0)
    b_idx = jnp.arange(B)[:, None, None, None]
    kv_idx = jnp.arange(Hk)[None, :, None, None]

    def block(args):
        qb, gb, i = args
        start = i * QB
        t = start + jnp.arange(QB)
        s_c = jnp.einsum('bkgqd,bknd->bkgqn', qb, k_cmp).astype(jnp.float32) * scale \
            + shared_bias(rel_table, t[:, None] - cmp_end[None, :], Hk)
        p_c = masked_softmax(s_c, cmp_end[None, :] <= t[:, None])
        o_c = jnp.einsum('bkgqn,bknd->bkgqd', p_c.astype(v_cmp.dtype), v_cmp)
        imp = jnp.einsum('bkgqn,nm->bkqm', p_c, overlap)
        blk_t = (t // SLC_BLOCK)[:, None]
        j = jnp.arange(n_slc)[None, :]
        forced = (j == 0) | (j == blk_t) | (j == blk_t - 1)
        score = jnp.where(forced, BIG, jnp.where(j <= blk_t, imp, NEG))
        sel = lax.top_k(score, n_sel)[1]
        k_sel = ks_blocks[b_idx, kv_idx, sel].reshape(B, Hk, QB, n_sel * SLC_BLOCK, dh)
        v_sel = vs_blocks[b_idx, kv_idx, sel].reshape(B, Hk, QB, n_sel * SLC_BLOCK, dh)
        pos_sel = (sel[..., None] * SLC_BLOCK + jnp.arange(SLC_BLOCK)).reshape(B, Hk, QB, -1)
        dist_s = t[:, None] - pos_sel
        s_s = jnp.einsum('bkgqd,bkqsd->bkgqs', qb, k_sel).astype(jnp.float32) * scale \
            + gathered_bias(rel_table, dist_s, Hk)
        p_s = masked_softmax(s_s, (dist_s >= 0)[:, :, None])
        o_s = jnp.einsum('bkgqs,bkqsd->bkgqd', p_s.astype(v_sel.dtype), v_sel)
        k_w = lax.dynamic_slice_in_dim(kw_pad, start, QB + NSA_WINDOW, axis=2)
        v_w = lax.dynamic_slice_in_dim(vw_pad, start, QB + NSA_WINDOW, axis=2)
        dist_w = t[:, None] - (start - NSA_WINDOW + jnp.arange(QB + NSA_WINDOW))[None, :]
        s_w = jnp.einsum('bkgqd,bksd->bkgqs', qb, k_w).astype(jnp.float32) * scale \
            + shared_bias(rel_table, dist_w, Hk)
        p_w = masked_softmax(s_w, (dist_w >= 0) & (dist_w < NSA_WINDOW))
        o_w = jnp.einsum('bkgqs,bksd->bkgqd', p_w.astype(v_w.dtype), v_w)
        return (gb[..., 0:1] * o_c + gb[..., 1:2] * o_s + gb[..., 2:3] * o_w).astype(qb.dtype)

    o = lax.map(block, (q_blocks, g_blocks, jnp.arange(nq)))
    return o.transpose(1, 0, 4, 2, 3, 5).reshape(B, S, NSA_HEADS * dh)

def moba_attention(q, k, v, rel_table):
    B, S, _ = q.shape
    H, dh, QB = MOBA_HEADS, HEAD_DIM, MOBA_QBLOCK
    scale = dh ** -0.5
    q, k, v = (t.reshape(B, S, H, dh).transpose(0, 2, 1, 3) for t in (q, k, v))
    n_blk = -(-S // MOBA_BLOCK)
    pad = ((0, 0), (0, 0), (0, n_blk * MOBA_BLOCK - S), (0, 0))
    k_pad, v_pad = jnp.pad(k, pad), jnp.pad(v, pad)
    k_blocks = k_pad.reshape(B, H, n_blk, MOBA_BLOCK, dh)
    v_blocks = v_pad.reshape(B, H, n_blk, MOBA_BLOCK, dh)
    k_mean = jnp.mean(k_blocks.astype(jnp.float32), axis=3)
    n_top = min(MOBA_TOPK, n_blk)
    n_s = n_top * MOBA_BLOCK
    nq = S // QB
    q_blocks = jnp.moveaxis(q.reshape(B, H, nq, QB, dh), 2, 0)
    b_idx = jnp.arange(B)[:, None, None, None]
    h_idx = jnp.arange(H)[None, :, None, None]

    def block(args):
        qb, i = args
        start = i * QB
        t = start + jnp.arange(QB)
        own = start // MOBA_BLOCK
        gate = jnp.einsum('bhqd,bhnd->bhqn', qb.astype(jnp.float32), k_mean)
        gate = jnp.where(jnp.arange(n_blk) < own, gate, NEG)
        sel = lax.top_k(gate, n_top)[1]
        k_sel = k_blocks[b_idx, h_idx, sel].reshape(B, H, QB, n_s, dh)
        v_sel = v_blocks[b_idx, h_idx, sel].reshape(B, H, QB, n_s, dh)
        pos_sel = (sel[..., None] * MOBA_BLOCK + jnp.arange(MOBA_BLOCK)).reshape(B, H, QB, n_s)
        mask_sel = pos_sel < own * MOBA_BLOCK
        k_own = lax.dynamic_slice_in_dim(k_pad, own * MOBA_BLOCK, MOBA_BLOCK, axis=2)
        v_own = lax.dynamic_slice_in_dim(v_pad, own * MOBA_BLOCK, MOBA_BLOCK, axis=2)
        dist_own = t[:, None] - (own * MOBA_BLOCK + jnp.arange(MOBA_BLOCK))[None, :]
        s_sel = jnp.einsum('bhqd,bhqsd->bhqs', qb, k_sel).astype(jnp.float32) * scale \
            + gathered_bias(rel_table, t[:, None] - pos_sel, H)[:, :, 0]
        s_own = jnp.einsum('bhqd,bhsd->bhqs', qb, k_own).astype(jnp.float32) * scale \
            + shared_bias(rel_table, dist_own, H)[:, 0]
        s = jnp.concatenate([s_sel, s_own], axis=-1)
        mask = jnp.concatenate([mask_sel, jnp.broadcast_to(dist_own >= 0, s_own.shape)], axis=-1)
        p = masked_softmax(s, mask).astype(v.dtype)
        return jnp.einsum('bhqs,bhqsd->bhqd', p[..., :n_s], v_sel) \
            + jnp.einsum('bhqs,bhsd->bhqd', p[..., n_s:], v_own)

    o = lax.map(block, (q_blocks, jnp.arange(nq)))
    return o.transpose(1, 0, 3, 2, 4).reshape(B, S, H * dh)

def mla_attention(c_q, c_kv, k_rope, q_norm, kv_norm, w_q_up, w_kv_up):
    B, S, _ = c_q.shape
    H, QB = MLA_HEADS, DENSE_QBLOCK
    q = (rmsnorm(c_q, q_norm) @ w_q_up).reshape(B, S, H, MLA_NOPE + MLA_ROPE)
    kv = (rmsnorm(c_kv, kv_norm) @ w_kv_up).reshape(B, S, H, MLA_NOPE + MLA_V)
    cos, sin = rope_tables(S, MLA_ROPE)
    q_nope = q[..., :MLA_NOPE]
    q_rope = apply_rope(q[..., MLA_NOPE:], cos[:, None, :], sin[:, None, :])
    k_rope = apply_rope(k_rope, cos, sin)
    k_nope = kv[..., :MLA_NOPE].transpose(0, 2, 1, 3)
    v = kv[..., MLA_NOPE:].transpose(0, 2, 1, 3)
    scale = (MLA_NOPE + MLA_ROPE) ** -0.5
    nq = S // QB
    qn_b = q_nope.reshape(B, nq, QB, H, MLA_NOPE).transpose(1, 0, 3, 2, 4)
    qr_b = q_rope.reshape(B, nq, QB, H, MLA_ROPE).transpose(1, 0, 3, 2, 4)
    kpos = jnp.arange(S)

    def block(args):
        qn, qr, i = args
        t = i * QB + jnp.arange(QB)
        s = (jnp.einsum('bhqd,bhkd->bhqk', qn, k_nope)
             + jnp.einsum('bhqd,bkd->bhqk', qr, k_rope)).astype(jnp.float32) * scale
        s = jnp.where(kpos[None, :] <= t[:, None], s, NEG)
        p = jax.nn.softmax(s, axis=-1).astype(v.dtype)
        return jnp.einsum('bhqk,bhkd->bhqd', p, v)

    o = lax.map(block, (qn_b, qr_b, jnp.arange(nq)))
    return o.transpose(1, 0, 3, 2, 4).reshape(B, S, H * MLA_V)

def swa_sink_attention(q, k, v, sinks, rel_table):
    B, S, _ = q.shape
    Hk, G, dh, QB, W = SWA_KV_HEADS, SWA_GROUP, HEAD_DIM, SWA_QBLOCK, SWA_WINDOW
    scale = dh ** -0.5
    q = q.reshape(B, S, Hk, G, dh).transpose(0, 2, 3, 1, 4)
    k = k.reshape(B, S, Hk, dh).transpose(0, 2, 1, 3)
    v = v.reshape(B, S, Hk, dh).transpose(0, 2, 1, 3)
    pad = ((0, 0), (0, 0), (W, 0), (0, 0))
    k_pad, v_pad = jnp.pad(k, pad), jnp.pad(v, pad)
    nq = S // QB
    q_blocks = jnp.moveaxis(q.reshape(B, Hk, G, nq, QB, dh), 3, 0)
    sink = sinks.astype(jnp.float32).reshape(Hk, G, 1, 1)

    def block(args):
        qb, i = args
        start = i * QB
        t = start + jnp.arange(QB)
        k_w = lax.dynamic_slice_in_dim(k_pad, start, QB + W, axis=2)
        v_w = lax.dynamic_slice_in_dim(v_pad, start, QB + W, axis=2)
        dist = t[:, None] - (start - W + jnp.arange(QB + W))[None, :]
        mask = (dist >= 0) & (dist < W)
        s = jnp.einsum('bkgqd,bksd->bkgqs', qb, k_w).astype(jnp.float32) * scale \
            + shared_bias(rel_table, dist, Hk)
        s = jnp.where(mask, s, NEG)
        m = jnp.maximum(jnp.max(s, axis=-1, keepdims=True), sink)
        e = jnp.exp(s - m)
        p = e / (jnp.sum(e, axis=-1, keepdims=True) + jnp.exp(sink - m))
        return jnp.einsum('bkgqs,bksd->bkgqd', p.astype(v_w.dtype), v_w)

    o = lax.map(block, (q_blocks, jnp.arange(nq)))
    return o.transpose(1, 0, 4, 2, 3, 5).reshape(B, S, SWA_HEADS * dh)

def even_mixer(h, w_in, w_out, pos_k, pos_v, ck_w1, ck_w2, cv_w1, cv_w2, rel_table):
    q_a, kc, vc, ks, vs, kw, vw, gates, q_b, k_b, v_b = split_cols(h @ w_in, EVEN_WIDTHS)
    o_a = nsa_attention(q_a, kc, vc, ks, vs, kw, vw, gates, pos_k, pos_v, ck_w1, ck_w2, cv_w1, cv_w2, rel_table)
    o_b = moba_attention(q_b, k_b, v_b, rel_table)
    return jnp.concatenate([o_a, o_b.astype(o_a.dtype)], axis=-1) @ w_out

def odd_mixer(h, w_in, w_out, q_norm, kv_norm, w_q_up, w_kv_up, sinks, rel_table):
    c_q, c_kv, k_rope, q_d, k_d, v_d = split_cols(h @ w_in, ODD_WIDTHS)
    o_c = mla_attention(c_q, c_kv, k_rope, q_norm, kv_norm, w_q_up, w_kv_up)
    o_d = swa_sink_attention(q_d, k_d, v_d, sinks, rel_table)
    return jnp.concatenate([o_c, o_d.astype(o_c.dtype)], axis=-1) @ w_out

def grouped_moe_2(h, router_w, router_b, w_gate, w_up, w_down):
    B, S, D = h.shape
    T = B * S
    E = N_EXPERTS
    xf = h.reshape(T, D)
    aff = jax.nn.sigmoid((xf @ router_w).astype(jnp.float32))
    biased = (aff + router_b.astype(jnp.float32)).reshape(T, N_GROUPS, EXPERTS_PER_GROUP_2)
    grp_score = jnp.sum(lax.top_k(biased, TOP_K)[0], axis=-1)
    g_sel = jnp.argmax(grp_score, axis=-1)
    tok = jnp.arange(T)
    local = lax.top_k(biased[tok, g_sel], TOP_K)[1]
    expert = g_sel[:, None] * EXPERTS_PER_GROUP_2 + local
    w = aff[tok[:, None], expert]
    w = w / jnp.sum(w, axis=-1, keepdims=True)

    A = T * TOP_K
    flat_e = expert.reshape(A)
    flat_tok = jnp.repeat(tok, TOP_K)
    flat_w = w.reshape(A)
    order = jnp.argsort(flat_e)
    se, stok, sw = flat_e[order], flat_tok[order], flat_w[order]
    counts = jnp.zeros((E,), jnp.int32).at[flat_e].add(1)
    padded = (counts + MOE_BLOCK - 1) // MOE_BLOCK * MOE_BLOCK
    start = jnp.cumsum(counts) - counts
    pend = jnp.cumsum(padded)
    pstart = pend - padded
    dest = pstart[se] + jnp.arange(A) - start[se]
    n_blocks = (A + E * (MOE_BLOCK - 1) + MOE_BLOCK - 1) // MOE_BLOCK
    P = n_blocks * MOE_BLOCK
    tok_buf = jnp.zeros((P,), jnp.int32).at[dest].set(stok)
    w_buf = jnp.zeros((P,), jnp.float32).at[dest].set(sw)
    blk_expert = jnp.minimum(jnp.searchsorted(pend, jnp.arange(n_blocks) * MOE_BLOCK, side='right'), E - 1)
    xs = xf[tok_buf].reshape(n_blocks, MOE_BLOCK, D)

    def expert_block(args):
        xb, e = args
        hid = jax.nn.silu(xb @ w_gate[e]) * (xb @ w_up[e])
        return hid @ w_down[e]

    ys = lax.map(expert_block, (xs, blk_expert)).reshape(P, D)
    out = jnp.zeros((T, D), ys.dtype).at[tok_buf].add(ys * w_buf[:, None].astype(ys.dtype))
    return out.reshape(B, S, D).astype(h.dtype)

def second_inputs(seed: int = 0) -> dict:
    key = jax.random.key(seed)
    ks = iter(jax.random.split(key, 40))
    D = D_MODEL

    def nrm(shape, std):
        return jax.random.normal(next(ks), shape, jnp.float32) * std

    def gain(shape):
        return 1.0 + nrm(shape, 0.02)

    return {
        "x": nrm((BATCH, SEQ, D), 1.0),
        "c": nrm((BATCH, D), 1.0),
        "rel_table": nrm((N_BUCKETS, N_BIAS_HEADS), 0.5),
        "router_w": nrm((D, N_EXPERTS), D ** -0.5),
        "router_b": nrm((N_EXPERTS,), 0.01),
        "final_norm": gain((D,)),
        "norm_mix": gain((DEPTH, D)),
        "norm_ffn": gain((DEPTH, D)),
        "ada_w": nrm((DEPTH, D, 6 * D), ADA_INIT * D ** -0.5),
        "ada_b": nrm((DEPTH, 6 * D), 0.02),
        "moe_w_gate": nrm((DEPTH, N_EXPERTS, D, D_EXPERT_2), D ** -0.5),
        "moe_w_up": nrm((DEPTH, N_EXPERTS, D, D_EXPERT_2), D ** -0.5),
        "moe_w_down": nrm((DEPTH, N_EXPERTS, D_EXPERT_2, D), D_EXPERT_2 ** -0.5),
        "ev_w_in": nrm((N_EVEN, D, EVEN_IN), D ** -0.5),
        "ev_w_out": nrm((N_EVEN, EVEN_OUT, D), EVEN_OUT ** -0.5),
        "nsa_pos_k": nrm((N_EVEN, CMP_LEN, HEAD_DIM), 0.1),
        "nsa_pos_v": nrm((N_EVEN, CMP_LEN, HEAD_DIM), 0.1),
        "nsa_ck_w1": nrm((N_EVEN, CMP_LEN * HEAD_DIM, CMP_HIDDEN), (CMP_LEN * HEAD_DIM) ** -0.5),
        "nsa_ck_w2": nrm((N_EVEN, CMP_HIDDEN, HEAD_DIM), CMP_HIDDEN ** -0.5),
        "nsa_cv_w1": nrm((N_EVEN, CMP_LEN * HEAD_DIM, CMP_HIDDEN), (CMP_LEN * HEAD_DIM) ** -0.5),
        "nsa_cv_w2": nrm((N_EVEN, CMP_HIDDEN, HEAD_DIM), CMP_HIDDEN ** -0.5),
        "od_w_in": nrm((N_ODD, D, ODD_IN), D ** -0.5),
        "od_w_out": nrm((N_ODD, ODD_OUT, D), ODD_OUT ** -0.5),
        "mla_q_norm": gain((N_ODD, MLA_Q_RANK)),
        "mla_kv_norm": gain((N_ODD, MLA_KV_RANK)),
        "mla_w_q_up": nrm((N_ODD, MLA_Q_RANK, MLA_HEADS * (MLA_NOPE + MLA_ROPE)), MLA_Q_RANK ** -0.5),
        "mla_w_kv_up": nrm((N_ODD, MLA_KV_RANK, MLA_HEADS * (MLA_NOPE + MLA_V)), MLA_KV_RANK ** -0.5),
        "swa_sinks": nrm((N_ODD, SWA_HEADS), 1.0),
    }

def second_block(x, c, rel_table, router_w, router_b, final_norm, norm_mix, norm_ffn, ada_w, ada_b,
              moe_w_gate, moe_w_up, moe_w_down, ev_w_in, ev_w_out, nsa_pos_k, nsa_pos_v,
              nsa_ck_w1, nsa_ck_w2, nsa_cv_w1, nsa_cv_w2, od_w_in, od_w_out, mla_q_norm,
              mla_kv_norm, mla_w_q_up, mla_w_kv_up, swa_sinks):
    for layer in range(DEPTH):
        shift_m, scale_m, gate_m, shift_f, scale_f, gate_f = adaln(c, ada_w[layer], ada_b[layer])
        h = rmsnorm(x, norm_mix[layer]) * (1.0 + scale_m) + shift_m
        i = layer // 2
        if layer % 2 == 0:
            mix = even_mixer(h, ev_w_in[i], ev_w_out[i], nsa_pos_k[i], nsa_pos_v[i], nsa_ck_w1[i],
                             nsa_ck_w2[i], nsa_cv_w1[i], nsa_cv_w2[i], rel_table)
        else:
            mix = odd_mixer(h, od_w_in[i], od_w_out[i], mla_q_norm[i], mla_kv_norm[i],
                            mla_w_q_up[i], mla_w_kv_up[i], swa_sinks[i], rel_table)
        x = x + gate_m * mix.astype(x.dtype)
        h = rmsnorm(x, norm_ffn[layer]) * (1.0 + scale_f) + shift_f
        x = x + gate_f * grouped_moe_2(h, router_w, router_b, moe_w_gate[layer], moe_w_up[layer],
                                     moe_w_down[layer]).astype(x.dtype)
    return rmsnorm(x, final_norm)


def setup_inputs(seed=0):
    out = dict(first_inputs(seed))
    for name, value in second_inputs(seed + 1).items():
        if name != "x":
            out[name + "_2"] = value
    return out


def reference(
    x, mem, w_in, w_a2, b_a, gla_norm_g, w_s, b_s, sgu_ln_g, sgu_ln_b, w_out, wq_x, wk_x, wv_x,
    wo_x, w_router, b_router, w_gate, w_up, w_down, ln_g, ln_b, c_2, rel_table_2, router_w_2,
    router_b_2, final_norm_2, norm_mix_2, norm_ffn_2, ada_w_2, ada_b_2, moe_w_gate_2,
    moe_w_up_2, moe_w_down_2, ev_w_in_2, ev_w_out_2, nsa_pos_k_2, nsa_pos_v_2, nsa_ck_w1_2,
    nsa_ck_w2_2, nsa_cv_w1_2, nsa_cv_w2_2, od_w_in_2, od_w_out_2, mla_q_norm_2, mla_kv_norm_2,
    mla_w_q_up_2, mla_w_kv_up_2, swa_sinks_2,
):
    x = first_block(
        x, mem, w_in, w_a2, b_a, gla_norm_g, w_s, b_s, sgu_ln_g, sgu_ln_b, w_out, wq_x, wk_x,
        wv_x, wo_x, w_router, b_router, w_gate, w_up, w_down, ln_g, ln_b,
    )
    return second_block(
        x, c_2, rel_table_2, router_w_2, router_b_2, final_norm_2, norm_mix_2, norm_ffn_2,
        ada_w_2, ada_b_2, moe_w_gate_2, moe_w_up_2, moe_w_down_2, ev_w_in_2, ev_w_out_2,
        nsa_pos_k_2, nsa_pos_v_2, nsa_ck_w1_2, nsa_ck_w2_2, nsa_cv_w1_2, nsa_cv_w2_2, od_w_in_2,
        od_w_out_2, mla_q_norm_2, mla_kv_norm_2, mla_w_q_up_2, mla_w_kv_up_2, swa_sinks_2,
    )


_drawn_inputs = setup_inputs


def setup_inputs(seed=0):
    import zlib

    import numpy as np

    out = dict(_drawn_inputs(seed))
    spreads = {}
    factors = {'final_norm_2': 2.877,
     'norm_mix_2': 3.256,
     'nsa_pos_k_2': 8.0,
     'mla_q_norm_2': 6.135,
     'mla_kv_norm_2': 6.065,
     'swa_sinks_2': 8.0}
    for name, (base, spread) in spreads.items():
        noise = np.random.default_rng([zlib.crc32(name.encode()), seed]).standard_normal(out[name].shape)
        drawn = base * np.exp(spread * noise) if base else spread * noise
        out[name] = jnp.asarray(drawn.astype(out[name].dtype))
    for name, factor in factors.items():
        out[name] = (out[name] * factor).astype(out[name].dtype)
    return out
```

```python
from contextlib import ExitStack

import numpy as np

import concourse.bass as bass
from concourse import mybir

F32 = mybir.dt.float32
ALU = mybir.AluOpType
ACT = mybir.ActivationFunctionType
AX = mybir.AxisListType

P = 128
S = 256
NT = S // P
D = 1024
DC = D // P
DEPTH = 2
CHUNK = 64
NCHUNK = S // CHUNK
GLA_HEADS = 4
SGU_GROUPS = 4
GATE_RANK = 16
NEXP = 16
NGRP = 4
EPG = NEXP // NGRP
HID = 512
HC = HID // P
ALPHA = (2.0 * DEPTH) ** 0.25
LN_EPS = 1e-5
RMS_EPS = 1e-6
NEG = -1e30
LOW = -3.0e38

RING = 6
PIECE = 4096
NBANK = 8
EXP_PER_BODY = 2
BODIES = NEXP // EXP_PER_BODY

N_CMP = (S - 32) // 16 + 1
CMP_L = 32
DH = 64
PAIRS = 4
MLA_H = 4
MLA_SCALE = 192.0 ** -0.5
ADA_COLS = 6 * D // NEXP
ADA_ROW = (DC + 1) * ADA_COLS
NLIN1 = 5 + 2 + 2 + 2 + 2 + 2
NLIN_EVEN = 8 + 2
NLIN_ODD = 4 + 2
NMOE = 3 * NEXP
NPIECES = 2 * (NLIN1 + NMOE) + NLIN_EVEN + NMOE + NLIN_ODD + NMOE
UROW = 512


def layout(fields):
    at, out = 0, {}
    for name, n in fields:
        out[name] = (at, at + n)
        at += n
    return out, at


CONST, CONST_N = layout([
    ("ident", P), ("later", P), ("inch16", 2), ("inch", 2), ("blocks", 256), ("rank4", 4),
    ("valid", NT), ("causal", NT * S), ("cos", NT * 32), ("sin", NT * 32), ("onehot", UROW),
    ("lncount", 2 * NT * 33), ("ones", 2), ("half", 16)])
PARAM, PARAM_N = layout([
    ("w_alow", 2 * DC * 16), ("w_router", DC * 16), ("router_w_2", DC * 16), ("w_gates", DC * 24),
    ("b_s", 8), ("w_s", 2 * 4 * P), ("w_a2", 2 * 256), ("c", DC), ("norm_mix", 2 * DC),
    ("norm_ffn", 2 * DC), ("q_norm", 2), ("kv_norm", 1), ("pos_k", 16), ("pos_v", 16),
    ("ck_w2", 2 * DH), ("cv_w2", 2 * DH), ("rel_table", 8), ("rel_rows", 8 * 33), ("b_router", 16),
    ("router_b_2", 16)])


NSA_WINDOW = 512
SWA_WINDOW = 128


def buckets(n):
    d = np.arange(n)
    bounds = [np.ceil(16 * 2.0 ** (3 * k / 8) - 1e-9) for k in range(16)]
    log_part = 15 + np.sum(d[:, None] >= np.array(bounds)[None, :], axis=1)
    return np.where(d < 16, d, np.minimum(log_part, 31))


def constants():
    c = np.zeros((P, CONST_N), np.float32)

    def put(name, a):
        a = np.asarray(a, np.float32)
        c[:a.shape[0], CONST[name][0]:CONST[name][1]] = a.reshape(a.shape[0], -1)

    p = np.arange(P)
    put("ident", np.eye(P))
    same = p[:, None] // CHUNK == p[None, :] // CHUNK
    put("later", np.where(same & (p[:, None] > p[None, :]), 1.0 / 16.0, 0.0))
    inch = p[:, None] // CHUNK == np.arange(2)[None, :]
    put("inch16", inch / 16.0)
    put("inch", inch)
    put("blocks", p[:, None] // 64 == np.arange(256)[None, :] // P)
    put("rank4", np.tile(np.array([4.0, 3.0, 2.0, 1.0]), (P, 1)))
    t = np.arange(NT)[None, :] * P + p[:, None]
    put("valid", t >= CMP_L - 1)
    put("causal", np.where(np.arange(S)[None, None, :] <= t[:, :, None], 0.0, NEG))
    ang = t[:, :, None].astype(np.float32) * (10000.0 ** (-np.arange(0, 64, 2) / 64.0)).astype(np.float32)
    put("cos", np.cos(ang))
    put("sin", np.sin(ang))
    u = np.arange(UROW)
    dist = 255 - u
    hot = np.zeros((33, UROW), np.float32)
    ok = (dist >= 0)
    hot[buckets(S)[dist[ok]], u[ok]] = 1.0
    hot[32, ~ok] = NEG
    put("onehot", hot)
    lncount = np.full((P, 2, NT, 33), NEG)
    for k, window in enumerate((NSA_WINDOW, SWA_WINDOW)):
        of = buckets(window)
        for b in range(32):
            n = np.sum((of == b) & (np.arange(window) > t[:, :, None]), axis=2)
            lncount[:, k, :, b] = np.where(n > 0, np.log(np.maximum(n, 1)), NEG)
    lncount[:, 1, :, 32] = 0.0
    put("lncount", lncount)
    put("ones", np.ones((P, 2)))
    put("half", np.full((P, 16), -0.5))
    return c


class Banks:

    def __init__(self, full, drained):
        self.full, self.drained = full, drained
        self.count = [0] * NBANK
        self.next = 0
        self.jobs = {}

    def add(self, name):
        b = self.next % NBANK
        self.next += 1
        self.count[b] += 1
        self.jobs[name] = (b, self.count[b], 0)

    def add_loop(self, names, rounds):
        banks = [(self.next + k) % NBANK for k in range(len(names))]
        self.next += len(names)
        for k, (name, b) in enumerate(zip(names, banks)):
            self.jobs[name] = (b, self.count[b] + banks[:k + 1].count(b), banks.count(b))
        for b in range(NBANK):
            self.count[b] += rounds * banks.count(b)

    def number(self, name, it):
        b, n, per = self.jobs[name]
        return b, (n if it is None else it * per + n)

    def wait_full(self, eng, name, it=None):
        b, n = self.number(name, it)
        eng.wait_ge(self.full[b], n)

    def wait_drained(self, eng, name, it=None, rounds=None):
        b, n, per = self.jobs[name]
        if rounds is not None:
            n += (rounds - 1) * per
        eng.wait_ge(self.drained[b], n if it is None else it * per + n)

    def wait_drained_round_before(self, eng, name, it):
        b, n, per = self.jobs[name]
        assert n > per
        eng.wait_ge(self.drained[b], it * per + (n - per))

    def wait_free(self, eng, name, it=None):
        b, n, per = self.jobs[name]
        if it is not None:
            eng.wait_ge(self.drained[b], it * per + (n - 1))
        elif n > 1:
            eng.wait_ge(self.drained[b], n - 1)


class Steps:

    def __init__(self, eng, sem):
        self.eng, self.sem, self.n, self.it = eng, sem, 0, None

    def __call__(self, ins):
        self.n += 1
        ins.then_inc(self.sem, 1)
        self.eng.wait_ge(self.sem, self.n if self.it is None else self.it * self.per + self.n)

    def enter(self, it, per):
        self.it, self.per, self.start = it, per, self.n

    def leave(self, rounds):
        assert self.n - self.start == self.per, self.n - self.start
        self.n = self.start + rounds * self.per
        self.it = None


def program(nc, weights, ada, cst, prm, vecs, x_in, xT_in, memT_in, out, scratch):
    ctx = ExitStack()
    with ctx:
        def sb(name, *shape):
            return ctx.enter_context(nc.sbuf_tensor(name, [P, *shape], F32))

        def sem(name):
            return ctx.enter_context(nc.semaphore(name))

        ring = sb("ring", RING, PIECE)
        x = sb("x", NT, D)
        xT = sb("xT", DC, S)
        oT = sb("oT", DC, S)
        mix = sb("mix", NT, D)
        consts = sb("consts", CONST_N)
        params = sb("params", PARAM_N)
        work = sb("work", 14336)
        small = sb("small", 560)
        psum = [ctx.enter_context(nc.psum_tensor(f"bank{b}", [P, 512], F32)) for b in range(NBANK)]

        def cut(t, at, *shape):
            n = int(np.prod(shape))
            ap = t[:, at:at + n]
            if len(shape) == 2:
                return ap.rearrange("p (a b) -> p a b", a=shape[0])
            if len(shape) == 3:
                return ap.rearrange("p (a b c) -> p a b c", a=shape[0], b=shape[1])
            return ap

        def cs(name, *shape):
            return cut(consts, CONST[name][0], *(shape or (CONST[name][1] - CONST[name][0],)))

        def pr(name, *shape):
            return cut(params, PARAM[name][0], *(shape or (PARAM[name][1] - PARAM[name][0],)))

        ident = cs("ident")
        later, inch16, inch = cs("later"), cs("inch16"), cs("inch")
        blocks = cs("blocks")

        memT = cut(work, 0, DC, S)
        xkT = cut(work, 2048, DC, S)
        xv = cut(work, 4096, NT, D)
        ada_in = cut(work, 2048, DC + 1, ADA_COLS)
        GL = 6144
        gqT = cut(work, GL, 2, S)
        gk = cut(work, GL + 512, NT, 256)
        gv = cut(work, GL + 1024, NT, 512)
        gr = cut(work, GL + 2048, NT, 512)
        su = cut(work, GL + 3072, NT, 512)
        sv = cut(work, GL + 4096, NT, 512)
        xqT = cut(work, GL, DC, S)
        gg = cut(oT[:, :, :].rearrange("p a b -> p (a b)"), 0, NT, 256)
        gE = cut(oT[:, :, :].rearrange("p a b -> p (a b)"), 512, NT, 256)
        gkd = cut(oT[:, :, :].rearrange("p a b -> p (a b)"), 1024, NCHUNK, 256)
        states = cut(xT[:, :, :].rearrange("p a b -> p (a b)"), 0, NCHUNK, 2, 256)
        LNV = GL + 5120
        lnv = cut(work, LNV, 2, D)
        mixv = cut(work, LNV, 3, 512)
        EX = GL
        esig = cut(work, EX, 2, HID)
        eh = cut(work, EX + 1024, 2, HID)
        ehT = cut(work, EX + 2048, 2, HC, P)
        ada_acc = cut(work, EX + 3072, ADA_COLS)
        gtmp = cut(work, EX + 3456, 512)
        aS = cut(mix[:, :, :].rearrange("p a b -> p (a b)"), 0, 2, 2, S)
        aP = cut(mix[:, :, :].rearrange("p a b -> p (a b)"), 1024, 2, 2, S)
        aPT = cut(work, 13312, 2, 4, P)
        bias = cut(work, 0, 8, NT, S)
        NS = 4096
        nq = cut(work, NS, PAIRS, S)
        nk = [cut(work, NS + 1024 + 512 * j, 2, S) for j in range(2)]
        nv = [cut(work, NS + 2048 + 512 * j, NT, 2, P) for j in range(2)]
        kcz = cut(work, NS + 3072, 2, 16)
        vcz = cut(work, NS + 3104, 2, P)
        MB = NS + 3360
        mq = cut(work, MB, PAIRS, S)
        mk = cut(work, MB + 1024, 8, S)
        mv = cut(work, MB + 3072, NT, 8, P)
        flat = cut(work, MB + 1024, 2, 16, 2 * N_CMP)
        h1T = cut(work, MB + 2048, 2, 2, 2 * N_CMP)
        gate_row = cut(work, MB, D)
        rowbuf = [cut(t[:, :, :].rearrange("p a b -> p (a b)"), 0, 4, UROW) for t in (mix, oT)]
        cq = cut(work, NS, NT, 448)
        cT = cut(work, NS + 896, 3, S)
        kr2 = cut(work, NS + 1664, NT, P)
        rt = cut(work, NS + 1920, 512)
        swq = cut(work, NS, PAIRS, S)
        swk = cut(work, NS + 7552, 2, S)
        swv = cut(work, NS + 8064, NT, 2, P)
        qn = cut(work, NS + 2432, MLA_H, S)
        kn = cut(work, NS + 3456, MLA_H, S)
        lv = cut(work, NS + 4480, NT, 512)
        qrn = cut(work, NS + 5504, NT, 256)
        qro = cut(work, NS + 6016, NT, 256)
        qrT = cut(work, NS + 6528, 2, S)
        krz = cut(work, NS + 7040, 2, S)
        assert NS + 8576 <= 13312 and MB + 5120 <= 13312

        SM, _n = layout([("stat_in", 16), ("stat_out", 16), ("bn", 2 * 12), ("mv", 4), ("nm", 4),
                         ("den", 4), ("modc", 96), ("gate", 32), ("sc", 8), ("decay", 8), ("gates", 48),
                         ("modg", 16), ("bnb", 48), ("mvb", 16), ("es", 4), ("mx", 4), ("pads", 2 * NT * 8), ("padmax", 2 * NT * 8), ("sig", 8)])
        assert _n <= 560

        def sm(name, *shape):
            return cut(small, SM[name][0], *(shape or (SM[name][1] - SM[name][0],)))

        stat_in, stat_out = sm("stat_in"), sm("stat_out")
        gate = sm("gate", NT, NEXP)
        gates = sm("gates", NT, 24)
        nm, den = sm("nm", 2, 2), sm("den", 2, 2)
        decay = sm("decay", 2, NCHUNK)
        alow = sb("alow", S)

        pad_w = cut(work, GL + 3072, 2 * NT, 8, 33)

        R, _n = layout([("A", 32), ("B", 32), ("hi", 16), ("lo", 16), ("8a", 8), ("8b", 8), ("8c", 8), ("2a", 2),
                        ("g", 8), ("a", 8), ("b", 8), ("1", 8), ("2", 8), ("tmp", 32)])

        def ro(name, *shape):
            return cut(gtmp, R[name][0], *(shape or (R[name][1] - R[name][0],)))

        rA, rB = ro("A", 2, 16), ro("B", 2, 16)
        r_hi, r_lo, r8a, r8b, r8c = ro("hi", 8, 2), ro("lo", 8, 2), ro("8a"), ro("8b"), ro("8c")
        r2a, r_g, r_a, r_b, r_1, r_2 = ro("2a"), ro("g", 2, 4), ro("a", 2, 4), ro("b", 2, 4), ro("1", 2, 4), ro("2", 2, 4)
        r_tmp = ro("tmp", 2, 4, 4)

        def skewed(first):
            flat_ = scratch[:, :]
            return bass.AP(flat_.tensor, flat_.offset + first, [[UROW, P], [P * (UROW + 1), 8], [1, S]])

        slot_full = [sem(f"slot_full{i}") for i in range(RING)]
        pieces_done = sem("pieces_done")
        banks = Banks([sem(f"bank_full{i}") for i in range(NBANK)],
                      [sem(f"bank_drained{i}") for i in range(NBANK)])
        setup_loaded = sem("setup_loaded")
        xT_loaded = sem("xT_loaded")
        vecs_loaded = sem("vecs_loaded")
        vecs_used = sem("vecs_used")
        var_ready = sem("var_ready")
        rstd_ready = sem("rstd_ready")
        dve_steps, act_steps, pool_steps = sem("dve_steps"), sem("act_steps"), sem("pool_steps")
        att_max, att_exp, att_prob = sem("att_max"), sem("att_exp"), sem("att_prob")
        ada_loaded, ada_summed = sem("ada_loaded"), sem("ada_summed")
        x_ready = sem("x_ready")
        gla_abs, gla_log, gla_g, gla_kd = sem("gla_abs"), sem("gla_log"), sem("gla_g"), sem("gla_kd")
        gla_state = sem("gla_state")
        sgu_ready = sem("sgu_ready")
        ws_masked = sem("ws_masked")
        silu_c = sem("silu_c")
        router_in, router_exp = sem("router_in"), sem("router_exp")
        ones_set = sem("ones_set")
        pads_in, pads_fn = sem("pads_in"), sem("pads_fn")
        rows_out, bias_back = sem("rows_out"), sem("bias_back")
        bias_ready = sem("bias_ready")
        zeros_set = sem("zeros_set")
        lat_ready = sem("lat_ready")
        rope_ready = sem("rope_ready")
        out_ready, out_stored = sem("out_ready"), sem("out_stored")

        OUTS = [(T, n) for n in range(2) for T in range(NT)]

        def cross_units(tag):
            out = []
            for hp in range(2):
                for T in range(NT):
                    t = slice(T * P, (T + 1) * P)
                    out.append(dict(
                        name=f"{tag}.{hp}.{T}", nk=S, tiles=2, kp=P, bias=None, sink=None, gate=None,
                        scores=[[(xqT[:, 4 * hp + 2 * a + j, t], xkT[:, 4 * hp + 2 * a + j, :])
                                 for j in range(2)] for a in range(2)],
                        pv=[(2 * a + j, a, kt, xv[:, kt, (4 * hp + 2 * a + j) * P:(4 * hp + 2 * a + j + 1) * P])
                            for a in range(2) for j in range(2) for kt in range(2)],
                        first=True, last=True, o=f"{tag}.o.{hp}.{T}", regions=4,
                        dest=oT[:, 4 * hp:4 * hp + 4, t]))
            return out

        def pair_units(tag, q, branches, chunk0):
            out = []
            for i in range(PAIRS):
                for T in range(NT):
                    t = slice(T * P, (T + 1) * P)
                    for b, (kf, vf, n, g, biases, sink) in enumerate(branches):
                        nk_ = n or (T + 1) * P
                        tiles = 1 if n else T + 1
                        out.append(dict(
                            name=f"{tag}.{i}.{T}.{b}", nk=nk_, tiles=tiles, kp=min(nk_, P),
                            bias=biases(i, T), sink=sink and sink(i, T),
                            gate=None if g is None else g(i, T),
                            scores=[[(q[:, i, t], kf(i, a)[:, 0:nk_])] for a in range(2)],
                            pv=[(0, a, kt, vf(i, a, kt)) for a in range(2) for kt in range(tiles)],
                            first=b == 0, last=b == len(branches) - 1, o=f"{tag}.o.{i}.{T}",
                            regions=1, dest=oT[:, chunk0 + i:chunk0 + i + 1, t]))
            return out

        def causal_bias(i, T):
            return [bias[:, i + 4 * a, T, 0:(T + 1) * P] for a in range(2)]

        def cmp_bias(i, T):
            return [bias[:, i + 4 * a, T, CMP_L - 1:S:16] for a in range(2)]

        def nsa_gate(b):
            return lambda i, T: gates[:, T, :].rearrange("p (a i b) -> p a i b", a=2, b=3)[:, :, i, b]

        def before(k):
            return lambda i, T: sm("pads", 2 * NT, 2, 4)[:, NT * k + T, :, i]

        def nsa_units():
            return pair_units("nsa", nq, [
                (lambda i, a: kcz[:, a, :], lambda i, a, kt: vcz[0:N_CMP, a, :], N_CMP, nsa_gate(0), cmp_bias, None),
                (lambda i, a: nk[0][:, a, :], lambda i, a, kt: nv[0][:, kt, a, :], None, nsa_gate(1), causal_bias, None),
                (lambda i, a: nk[1][:, a, :], lambda i, a, kt: nv[1][:, kt, a, :], None, nsa_gate(2), causal_bias,
                 before(0)),
            ], 0)

        def moba_units():
            return pair_units("moba", mq, [
                (lambda i, a: mk[:, i + 4 * a, :], lambda i, a, kt: mv[:, kt, i + 4 * a, :], None, None, causal_bias,
                 None),
            ], 4)

        def swa_units():
            return pair_units("swa", swq, [
                (lambda i, a: swk[:, a, :], lambda i, a, kt: swv[:, kt, a, :], None, None, causal_bias,
                 before(1)),
            ], 4)

        def mla_units():
            out = []
            for i in range(2):
                for T in range(NT):
                    t = slice(T * P, (T + 1) * P)
                    n = (T + 1) * P
                    out.append(dict(
                        name=f"mla.{i}.{T}", nk=n, tiles=T + 1, kp=P, sink=None, gate=None,
                        bias=[cs("causal", NT, S)[:, T, 0:n]] * 2,
                        scores=[[(qn[:, 2 * i + a, t], kn[:, 2 * i + a, 0:n]),
                                 (qrT[:, i, t], krz[:, a, 0:n])] for a in range(2)],
                        pv=[(a, a, kt, lv[:, kt, (2 * i + a) * P:(2 * i + a + 1) * P])
                            for a in range(2) for kt in range(T + 1)],
                        first=True, last=True, o=f"mla.o.{i}.{T}", regions=2,
                        dest=oT[:, 2 * i:2 * i + 2, t]))
            return out

        def numbered(units, first):
            for k, u in enumerate(units):
                u["n"] = first + k
            return units

        ATT = {"0.x": 0, "1.x": 4, "nsa": 8, "moba": 32, "mla": 40, "swa": 44}

        MOE_ORDER = [("gu", 0), ("gu", 1), ("td", 0), ("ada", 0), ("gu", 2), ("td", 1), ("gu", 3),
                     ("td", 2), ("ada", 1), ("td", 3)]

        def moe_jobs(tag, with_ada):
            out = []
            for what, k in MOE_ORDER:
                if what == "gu":
                    out += [f"{tag}.g{k}", f"{tag}.u{k}"]
                elif what == "td":
                    out += [f"{tag}.hT{k}", f"{tag}.y{k}.0", f"{tag}.y{k}.1"]
                elif with_ada:
                    out.append(f"{tag}.ada{k}")
            return out

        block = ctx.enter_context(nc.Block())

        @block.tensor
        def _(pe):
            taken = [0]
            release = [False]

            def piece(it=None):
                m = taken[0]
                taken[0] += 1
                n = 16 * (m // RING + 1)
                pe.wait_ge(slot_full[m % RING], n if it is None else it * 16 + n)
                if m and it is None:
                    release[0] = True
                return ring[:, m % RING, :]

            def mm(o, lhsT, rhs, start, stop):
                ins = nc.tensor.matmul(o, lhsT, rhs, start=start, stop=stop)
                if release[0] and not stop:
                    ins.then_inc(pieces_done, 1)
                    release[0] = False
                return ins

            def begin(name, it=None):
                if it is None:
                    banks.add(name)
                banks.wait_free(pe, name, it)
                return psum[banks.jobs[name][0]]

            def end(name, ins):
                ins.then_inc(banks.full[banks.jobs[name][0]], 1)

            def ready(name, it=None):
                banks.wait_drained(pe, name, it)

            def product(name, parts, it=None):
                bank = begin(name, it)
                for c0, c1, rows, pairs in parts:
                    for k, (a, b) in enumerate(pairs):
                        ins = mm(bank[0:rows, c0:c1], a, b, k == 0, k == len(pairs) - 1)
                end(name, ins)

            def transposes(name, pairs, it=None):
                bank = begin(name, it)
                for c0, c1, rows, src in pairs:
                    k = src.shape[0]
                    ins = nc.tensor.transpose(bank[0:rows, c0:c1], src, ident[0:k, 0:k])
                end(name, ins)

            def columns(w, n=512):
                return w[:, 0:DC * n].rearrange("p (c n) -> p c n", c=DC)

            def natural(name, T, rhs, src=xT, n=512, at=0):
                product(name, [(at, at + n, P, [(src[:, c, T * P:(T + 1) * P], rhs(c)) for c in range(DC)])])

            def transposed(name, cols, src=xT):
                product(name, [(k * S, (k + 1) * S, f(0).shape[-1] if len(f(0).shape) == 2 else P,
                                [(f(c), src[:, c, :]) for c in range(DC)]) for k, f in enumerate(cols)])

            def turn(tag, src):
                for q in range(DC // 2):
                    transposes(f"{tag}.{q}", [(j * S + T * P, j * S + (T + 1) * P, P,
                                               src[:, T, (2 * q + j) * P:(2 * q + j + 1) * P])
                                              for j in range(2) for T in range(NT)])

            def project_out(tag):
                for q in range(2):
                    w = columns(piece())
                    for T in range(NT):
                        natural(f"{tag}.{T}.{q}", T, lambda c: w[:, c, :], src=oT)

            def attention(units):
                n = len(units)
                for k in range(n + 2):
                    if k < n:
                        u = units[k]
                        product(u["name"] + ".s", [(a * S, a * S + u["nk"], P, u["scores"][a]) for a in range(2)])
                    if 1 <= k <= n:
                        u = units[k - 1]
                        pe.wait_ge(att_prob, u["n"] + 1)
                        src = aP[:, u["n"] % 2, :, :]
                        transposes(u["name"] + ".t", [
                            ((2 * a + kt) * P, (2 * a + kt + 1) * P, u["kp"], src[:, a, kt * P:kt * P + u["kp"]])
                            for a in range(2) for kt in range(u["tiles"])])
                    if k >= 2:
                        u = units[k - 2]
                        if u["first"]:
                            begin(u["o"])
                        bank = psum[banks.jobs[u["o"]][0]]
                        ready(u["name"] + ".t")
                        src = aPT[:, u["n"] % 2, :, :]
                        for j, (r, a, kt, v) in enumerate(u["pv"]):
                            fresh = u["first"] and (j == 0 or u["pv"][j - 1][0] != r)
                            done = u["last"] and (j == len(u["pv"]) - 1 or u["pv"][j + 1][0] != r)
                            ins = mm(bank[:, r * P:(r + 1) * P], v, src[0:u["kp"], 2 * a + kt, :], fresh, done)
                        if u["last"]:
                            end(u["o"], ins)

            def experts(tag, with_ada):
                banks.add_loop(moe_jobs(tag, with_ada), BODIES)
                first = taken[0]
                with pe.Fori(0, BODIES) as it:
                    w = {}

                    def gate_up(k):
                        e, T = divmod(k, 2)
                        for what in "gu":
                            if T == 0:
                                w[what, e] = columns(piece(it))
                            if what == "g" and k in (0, 3):
                                release[0] = True
                            product(f"{tag}.{what}{k}", [(0, HID, P, [
                                (xT[:, c, T * P:(T + 1) * P], w[what, e][:, c, :]) for c in range(DC)])], it)

                    def down(k):
                        e, T = divmod(k, 2)
                        ready(f"{tag}.u{k}", it)
                        transposes(f"{tag}.hT{k}", [(j * P, (j + 1) * P, P, eh[:, k % 2, j * P:(j + 1) * P])
                                                    for j in range(HC)], it)
                        if T == 0:
                            w["d", e] = piece(it).rearrange("p (c n) -> p c n", c=HC)
                        ready(f"{tag}.hT{k}", it)
                        for n in range(2):
                            if T == 0:
                                release[0] = True
                            product(f"{tag}.y{k}.{n}", [(0, 512, P, [
                                (ehT[:, k % 2, j, :], w["d", e][:, j, n * 512:(n + 1) * 512])
                                for j in range(HC)])], it)

                    for what, k in MOE_ORDER:
                        if what == "gu":
                            gate_up(k)
                        elif what == "td":
                            down(k)
                        elif with_ada:
                            pe.wait_ge(ada_summed, it * 2 + (2 * BODIES * with_ada[0] + k + 1))
                            product(f"{tag}.ada{k}", [(j, j + 1, P, [(ada_acc[:, j * P:(j + 1) * P], cs("ones")[:, 0:1])])
                                                      for j in range(ADA_COLS // P)], it)
                taken[0] = first + NMOE

            pe.wait_ge(setup_loaded, 32)
            for h in range(8):
                product(f"row.{h}", [(0, UROW, P, [(pr("rel_table")[0:33, h:h + 1].broadcast_to([33, P]), cs("onehot")[0:33, :])])])

            def first_layer(l):
                if l == 0:
                    pe.wait_ge(xT_loaded, 48)
                else:
                    for q in range(DC // 2):
                        ready(f"{l - 1}.turn3.{q}")
                tg = f"{l}"
                w = columns(piece())
                transposed(f"{tg}.q", [lambda c, m=m: w[:, c, m * P:(m + 1) * P] for m in range(2)])
                product(f"{tg}.k", [(T * 256, (T + 1) * 256, P, [(xT[:, c, T * P:(T + 1) * P], w[:, c, 256:512])
                                                               for c in range(DC)]) for T in range(NT)])
                wl = pr("w_alow", 2, DC * 16)[:, l, :].rearrange("p (c n) -> p c n", c=DC)
                product(f"{tg}.alow", [(0, S, GATE_RANK, [(wl[:, c, :], xT[:, c, :]) for c in range(DC)])])
                w = columns(piece())
                for T in range(NT):
                    natural(f"{tg}.v.{T}", T, lambda c: w[:, c, :])
                ready(f"{tg}.alow")
                wa = pr("w_a2", 2, 256)[0:GATE_RANK + 1, l, :]
                product(f"{tg}.z", [(T * 256, (T + 1) * 256, P, [(alow[0:GATE_RANK + 1, T * P:(T + 1) * P], wa)])
                                    for T in range(NT)])
                for n in ("r", "u", "sv"):
                    w = columns(piece())
                    for T in range(NT):
                        natural(f"{tg}.{n}.{T}", T, lambda c: w[:, c, :])
                pe.wait_ge(gla_g, l + 1)
                product(f"{tg}.rem", [(T * 256, (T + 1) * 256, P, [(later, gg[:, T, :])]) for T in range(NT)])
                product(f"{tg}.dec", [(m * 4 + 2 * T, m * 4 + 2 * T + 2, P,
                                       [(gg[:, T, m * P:(m + 1) * P], inch16)])
                                      for m in range(2) for T in range(NT)])
                for q in range(2):
                    w = columns(piece())
                    for j in range(2):
                        transposed(f"{tg}.xk.{2 * q + j}",
                                   [lambda c, m=m: w[:, c, m * P:(m + 1) * P] for m in (2 * j, 2 * j + 1)], src=memT)
                pe.wait_ge(gla_kd, l + 1)
                for T in range(NT):
                    ready(f"{tg}.v.{T}")
                for c in range(NCHUNK):
                    T = c // 2
                    product(f"{tg}.kv.{c}", [(m * 256, (m + 1) * 256, P,
                                              [(gkd[:, c, m * P:(m + 1) * P], gv[:, T, m * 256:(m + 1) * 256])])
                                             for m in range(2)])
                for q in range(2):
                    w = columns(piece())
                    for T in range(NT):
                        natural(f"{tg}.xv.{T}.{q}", T, lambda c: w[:, c, :], src=memT)
                ready(f"{tg}.q")
                for c in range(NCHUNK):
                    T = c // 2
                    pe.wait_ge(gla_state, NCHUNK * l + c + 1)
                    product(f"{tg}.o.{c}", [(m * 256, (m + 1) * 256, P,
                                             [(gqT[:, m, T * P:(T + 1) * P], states[:, c, m, :])]) for m in range(2)])
                pe.wait_ge(sgu_ready, l + 1)
                pe.wait_ge(ws_masked, 2)
                ws = pr("w_s", 2, 4, P)
                for T in range(NT):
                    product(f"{tg}.mix.{T}", [(g * P, (g + 1) * P, P, [(ws[:, l, g, :], sv[:, T, g * P:(g + 1) * P])])
                                              for g in range(SGU_GROUPS)])
                for T in range(NT):
                    ready(f"{tg}.mix.{T}")
                turn(f"{tg}.turn0", mix)
                for q in range(DC // 2):
                    ready(f"{tg}.turn0.{q}")
                project_out(f"{tg}.out")
                pe.wait_ge(x_ready, 3 * l + 1)
                turn(f"{tg}.turn1", x)
                for q in range(DC // 2):
                    ready(f"{tg}.turn1.{q}")
                for q in range(2):
                    w = columns(piece())
                    for j in range(2):
                        transposed(f"{tg}.xq.{2 * q + j}",
                                   [lambda c, m=m: w[:, c, m * P:(m + 1) * P] for m in (2 * j, 2 * j + 1)])
                for q in range(4):
                    ready(f"{tg}.xq.{q}")
                    ready(f"{tg}.xk.{q}")
                for q in range(2):
                    for T in range(NT):
                        ready(f"{tg}.xv.{T}.{q}")
                us = numbered(cross_units(f"{tg}.x"), ATT[f"{tg}.x"])
                attention(us)
                for u in us:
                    ready(u["o"])
                project_out(f"{tg}.xo")
                pe.wait_ge(x_ready, 3 * l + 2)
                turn(f"{tg}.turn2", x)
                for q in range(DC // 2):
                    ready(f"{tg}.turn2.{q}")
                route(f"{tg}.logits", "w_router")
                experts(f"{tg}.moe", (l,))
                if l == 0:
                    pe.wait_ge(x_ready, 3 * l + 3)
                    turn(f"{tg}.turn3", x)

            def route(name, weights):
                wr = pr(weights, DC, 16)
                product(name, [(T * 16, (T + 1) * 16, P, [(xT[:, c, T * P:(T + 1) * P], wr[:, c, :])
                                                         for c in range(DC)]) for T in range(NT)])

            def gate_rows(tag, cols):
                for q in range(2):
                    product(f"{tag}.{q}", [(j * P, (j + 1) * P, P,
                                            [(cols[:, 4 * q + j:4 * q + j + 1].broadcast_to([P, P]), ident)])
                                           for j in range(4)])

            first_layer(0)
            first_layer(1)

            def normed(tag, n):
                pe.wait_ge(x_ready, n)
                turn(tag, mix)
                for q in range(DC // 2):
                    ready(f"{tag}.{q}")

            normed("e.turn0", 6)
            w = columns(piece())
            for j in range(2):
                transposed(f"e.q.{j}", [lambda c, i=i: w[:, c, i * P:(i + 1) * P] for i in (2 * j, 2 * j + 1)])
            w = columns(piece())
            transposed("e.c", [lambda c, i=i: w[:, c, i * P:(i + 1) * P] for i in range(2)])
            transposed("e.ks", [lambda c: w[:, c, 256:384]])
            product("e.vs", [(T * P, (T + 1) * P, P, [(xT[:, c, T * P:(T + 1) * P], w[:, c, 384:512])
                                                     for c in range(DC)]) for T in range(NT)])
            w = columns(piece())
            transposed("e.kw", [lambda c: w[:, c, 0:P]])
            product("e.vw", [(T * P, (T + 1) * P, P, [(xT[:, c, T * P:(T + 1) * P], w[:, c, P:2 * P])
                                                     for c in range(DC)]) for T in range(NT)])
            wg = pr("w_gates", DC, 24)
            product("e.gates", [(T * 24, (T + 1) * 24, P, [(xT[:, c, T * P:(T + 1) * P], wg[:, c, :])
                                                          for c in range(DC)]) for T in range(NT)])
            ready("e.c")
            for j, n in enumerate("kv"):
                w1 = piece().rearrange("p (c n) -> p c n", c=16)
                product(f"e.h1{n}", [(m * 2 * N_CMP, (m + 1) * 2 * N_CMP, P,
                                      [(w1[:, c, m * P:(m + 1) * P], flat[:, j, c, :]) for c in range(16)])
                                     for m in range(2)])
            ready("e.h1k")
            wk2 = pr("ck_w2", 2, DH)
            product("e.kc", [(0, 2 * N_CMP, DH, [(wk2[:, m, :], h1T[:, 0, m, :]) for m in range(2)])])
            ready("e.h1v")
            wv2 = pr("cv_w2", 2, DH)
            product("e.vc", [(a * DH, (a + 1) * DH, N_CMP,
                              [(h1T[:, 1, m, a * N_CMP:(a + 1) * N_CMP], wv2[:, m, :]) for m in range(2)])
                             for a in range(2)])
            for n in ("e.q.0", "e.q.1", "e.ks", "e.kw", "e.vs", "e.vw", "e.kc", "e.vc"):
                ready(n)
            attention(numbered(nsa_units(), ATT["nsa"]))
            w = columns(piece())
            for j in range(2):
                transposed(f"e.mq.{j}", [lambda c, i=i: w[:, c, i * P:(i + 1) * P] for i in (2 * j, 2 * j + 1)])
            w = columns(piece())
            for j in range(2):
                transposed(f"e.mk.{j}", [lambda c, i=i: w[:, c, i * P:(i + 1) * P] for i in (2 * j, 2 * j + 1)])
            w = columns(piece())
            for T in range(NT):
                natural(f"e.mv.{T}", T, lambda c: w[:, c, :])
            for n in ("e.mq.0", "e.mq.1", "e.mk.0", "e.mk.1", "e.mv.0", "e.mv.1"):
                ready(n)
            attention(numbered(moba_units(), ATT["moba"]))
            for i in range(PAIRS):
                for T in range(NT):
                    ready(f"nsa.o.{i}.{T}")
                    ready(f"moba.o.{i}.{T}")
            gate_rows("e.gm", sm("modc", 2, 48)[:, 0, 16:24])
            project_out("e.out")
            normed("e.turn1", 7)
            route("e.logits", "router_w_2")
            experts("e.moe", None)
            gate_rows("e.gf", sm("modc", 2, 48)[:, 0, 40:48])

            normed("o.turn0", 8)
            w = columns(piece())
            for T in range(NT):
                natural(f"o.c.{T}", T, lambda c: w[:, c, 0:448], n=448)
            pe.wait_ge(lat_ready, 1)
            transposes("o.cqT", [(j * S + T * P, j * S + (T + 1) * P, P, cq[:, T, j * P:(j + 1) * P])
                                 for j in range(2) for T in range(NT)])
            transposes("o.ckvT", [(T * P, (T + 1) * P, P, cq[:, T, 2 * P:3 * P]) for T in range(NT)])
            w = piece()
            wq = w[:, 0:1536].rearrange("p (c n) -> p c n", c=2)
            wkv = w[:, 1536:2560]
            ready("o.cqT")
            ready("o.ckvT")
            for j in range(2):
                product(f"o.qn.{j}", [(a * S, (a + 1) * S, P,
                                       [(wq[:, c, (2 * j + a) * 192:(2 * j + a) * 192 + P], cT[:, c, :]) for c in range(2)])
                                      for a in range(2)])
                product(f"o.kn.{j}", [(a * S, (a + 1) * S, P, [(wkv[:, (2 * j + a) * 256:(2 * j + a) * 256 + P], cT[:, 2, :])])
                                      for a in range(2)])
            wqr = wq.rearrange("p c (h n) -> p c h n", h=MLA_H)
            wv_ = wkv.rearrange("p (h n) -> p h n", h=MLA_H)
            product("o.qr", [(T * 256, (T + 1) * 256, P, [(cT[:, c, T * P:(T + 1) * P], wqr[:, c, :, P:192]) for c in range(2)])
                             for T in range(NT)])
            for T in range(NT):
                product(f"o.v.{T}", [(0, 512, P, [(cT[:, 2, T * P:(T + 1) * P], wv_[:, :, P:256])])])
            pe.wait_ge(rope_ready, 1)
            transposes("o.krT", [(T * P, (T + 1) * P, P, kr2[:, T, :]) for T in range(NT)])
            pe.wait_ge(rope_ready, 2)
            transposes("o.qrT", [(i * S + T * P, i * S + (T + 1) * P, P, qro[:, T, i * P:(i + 1) * P])
                                 for i in range(2) for T in range(NT)])
            for n in ("o.qn.0", "o.qn.1", "o.kn.0", "o.kn.1", "o.v.0", "o.v.1", "o.krT", "o.qrT"):
                ready(n)
            attention(numbered(mla_units(), ATT["mla"]))
            w = columns(piece())
            for j in range(2):
                transposed(f"o.sq.{j}", [lambda c, i=i: w[:, c, i * P:(i + 1) * P] for i in (2 * j, 2 * j + 1)])
            w = columns(piece())
            transposed("o.sk", [lambda c: w[:, c, 0:P]])
            product("o.sv", [(T * P, (T + 1) * P, P, [(xT[:, c, T * P:(T + 1) * P], w[:, c, P:2 * P])
                                                     for c in range(DC)]) for T in range(NT)])
            for n in ("o.sq.0", "o.sq.1", "o.sk", "o.sv"):
                ready(n)
            attention(numbered(swa_units(), ATT["swa"]))
            for i in range(PAIRS):
                for T in range(NT):
                    ready(f"swa.o.{i}.{T}")
            for i in range(2):
                for T in range(NT):
                    ready(f"mla.o.{i}.{T}")
            gate_rows("o.gm", sm("modc", 2, 48)[:, 1, 16:24])
            project_out("o.out")
            normed("o.turn1", 9)
            route("o.logits", "router_w_2")
            experts("o.moe", None)
            gate_rows("o.gf", sm("modc", 2, 48)[:, 1, 40:48])
            assert taken[0] == NPIECES, taken[0]

        @block.scalar
        def _(act):
            step = Steps(act, act_steps)

            def fn(o, i, f, **kw):
                return nc.scalar.activation(o, i, f, **kw)

            def carry(name, ops, f=ACT.Identity, it=None, **kw):
                banks.wait_full(act, name, it)
                b = banks.jobs[name][0]
                for k, (o, c) in enumerate(ops):
                    ins = fn(o, c(psum[b]), f, **kw)
                    if k < len(ops) - 1:
                        step(ins)
                ins.then_inc(banks.drained[b], 1)

            def whole(o, name, f=ACT.Identity, it=None, **kw):
                a, b = o.shape[1:] if len(o.shape) == 3 else (1, o.shape[1])
                n = a * b
                view = (lambda t: t[:, 0:n].rearrange("p (a b) -> p a b", a=a)) if len(o.shape) == 3 \
                    else (lambda t: t[0:o.shape[0], 0:n])
                carry(name, [(o, view)], f, it, **kw)

            def turned(tag):
                for q in (0, 2):
                    whole(xT[:, 2 * q:2 * q + 2, :], f"{tag}.{q}")

            def modulated(tag, layer, shift):
                for q in (0, 2):
                    banks.wait_full(act, f"{tag}.{q}")
                    b = banks.jobs[f"{tag}.{q}"][0]
                    for j in range(2):
                        c = 2 * q + j
                        ins = fn(xT[:, c, :], psum[b][:, j * S:(j + 1) * S], ACT.Identity,
                                 scale=sm("modg")[:, c:c + 1],
                                 bias=sm("modc", 2, 48)[:, layer, shift + c:shift + c + 1])
                        if j == 0:
                            step(ins)
                    ins.then_inc(banks.drained[b], 1)

            def attention(units):
                def exps(u):
                    act.wait_ge(att_max, u["n"] + 1)
                    i = u["n"] % 2
                    b = banks.jobs[u["name"] + ".s"][0]
                    for a in range(2):
                        src = psum[b][:, a * S:a * S + u["nk"]] if u["bias"] is None else aS[:, i, a, 0:u["nk"]]
                        ins = fn(aP[:, i, a, 0:u["nk"]], src, ACT.Exp, bias=nm[:, i, a:a + 1],
                                 accum_out=den[:, i, a:a + 1])
                        if a == 0 or u["sink"] is not None:
                            step(ins)
                    if u["sink"] is not None:
                        es = sm("es", 2, 2)[:, i, :]
                        ins = fn(es, es, ACT.Exp)
                    if u["bias"] is None:
                        ins.then_inc(banks.drained[b], 1)
                    else:
                        ins.then_inc(att_exp, 1)

                def turned_probs(u):
                    o, kp = aPT[:, u["n"] % 2, :, :], u["kp"]
                    if u["tiles"] == 2:
                        carry(u["name"] + ".t", [(o[0:kp], lambda t: t[0:kp, :].rearrange("p (a b) -> p a b", a=4))])
                    else:
                        carry(u["name"] + ".t", [(o[0:kp, 0:4:2, :],
                                                  lambda t: t[0:kp, :].rearrange("p (a b) -> p a b", a=4)[:, 0:4:2, :])])

                for k in range(len(units) + 1):
                    if k < len(units):
                        exps(units[k])
                    if k >= 1:
                        turned_probs(units[k - 1])

            def experts(tag):
                with act.Fori(0, BODIES) as it:
                    def sig(k):
                        whole(esig[:, k % 2, :], f"{tag}.g{k}", ACT.Silu, it)

                    def hT(k):
                        whole(ehT[:, k % 2, :, :], f"{tag}.hT{k}", it=it)

                    sig(0)
                    sig(1)
                    hT(0)
                    sig(2)
                    hT(1)
                    sig(3)
                    hT(2)
                    hT(3)

            act.dma_start(consts[:, :], cst).then_inc(setup_loaded, 16)
            act.dma_start(params[:, :], prm).then_inc(setup_loaded, 16)
            act.dma_start(xT[:, :, :], xT_in).then_inc(xT_loaded, 16)
            act.dma_start(memT, memT_in).then_inc(xT_loaded, 16)
            act.dma_start(x[:, :, :], x_in).then_inc(xT_loaded, 16)
            act.wait_ge(setup_loaded, 32)
            fn(sm("sc"), pr("c"), ACT.Silu).then_inc(silu_c, 1)
            for h in range(8):
                whole(rowbuf[h // 4][:, h % 4, :], f"row.{h}")
                banks.wait_drained(act, f"row.{h}")
                act.dma_start(scratch[h, 0:P * (UROW + 1)].rearrange("(p u) -> p u", p=P)[:, 0:UROW],
                              rowbuf[h // 4][:, h % 4, :]).then_inc(rows_out, 16)
            act.wait_ge(pads_in, 1)
            fn(pad_w, pad_w, ACT.Exp).then_inc(pads_fn, 1)
            act.wait_ge(pads_in, 2)
            fn(sm("pads"), sm("pads"), ACT.Ln).then_inc(pads_fn, 1)
            act.wait_ge(ones_set, 1)

            for l in range(DEPTH):
                tg = f"{l}"
                if l:
                    turned(f"{l - 1}.turn3")
                whole(gqT, f"{tg}.q", scale=0.125)
                whole(alow[0:GATE_RANK, :], f"{tg}.alow")
                for T in range(NT):
                    whole(gv[:, T, :], f"{tg}.v.{T}")
                act.wait_ge(gla_abs, l + 1)
                step(fn(gE, gE, ACT.Exp, scale=-1.0))
                fn(gE, gE, ACT.Ln, bias=1.0).then_inc(gla_log, 1)
                for T in range(NT):
                    whole(gr[:, T, :], f"{tg}.r.{T}", ACT.Silu)
                for T in range(NT):
                    whole(su[:, T, :], f"{tg}.u.{T}", ACT.Gelu_apprx_tanh)
                for T in range(NT):
                    whole(sv[:, T, :], f"{tg}.sv.{T}", ACT.Gelu_apprx_tanh)
                whole(gE, f"{tg}.rem", ACT.Exp)
                whole(decay, f"{tg}.dec", ACT.Exp)
                for j in range(4):
                    whole(xkT[:, 2 * j:2 * j + 2, :], f"{tg}.xk.{j}")
                for T, q in OUTS:
                    whole(xv[:, T, q * 512:(q + 1) * 512], f"{tg}.xv.{T}.{q}")
                for q in (0, 2):
                    whole(oT[:, 2 * q:2 * q + 2, :], f"{tg}.turn0.{q}")
                turned(f"{tg}.turn1")
                for j in range(4):
                    whole(xqT[:, 2 * j:2 * j + 2, :], f"{tg}.xq.{j}", scale=0.0625)
                attention(numbered(cross_units(f"{tg}.x"), ATT[f"{tg}.x"]))
                turned(f"{tg}.turn2")
                act.wait_ge(router_in, l + 1)
                fn(rA, rA, ACT.Exp).then_inc(router_exp, 1)
                experts(f"{tg}.moe")

            act.wait_ge(rows_out, 128)
            act.wait_ge(x_ready, 6)
            for T in range(NT):
                act.dma_start(bias[:, :, T, :], skewed(255 - P * T)).then_inc(bias_back, 16)
            modulated("e.turn0", 0, 0)
            for j in range(2):
                whole(nq[:, 2 * j:2 * j + 2, :], f"e.q.{j}", scale=0.125)
            act.wait_ge(zeros_set, 1)
            for n, t in (("ks", nk[0]), ("kw", nk[1])):
                carry(f"e.{n}", [(t[a * DH:(a + 1) * DH, a, :], lambda t_, a=a: t_[a * DH:(a + 1) * DH, 0:S])
                                 for a in range(2)]) if n == "ks" else None
                if n == "ks":
                    carry("e.vs", [(nv[0][:, :, a, a * DH:(a + 1) * DH],
                                    lambda t_, a=a: t_[:, 0:256].rearrange("p (t c) -> p t c", t=2)[:, :, a * DH:(a + 1) * DH])
                                   for a in range(2)])
                else:
                    carry(f"e.{n}", [(t[a * DH:(a + 1) * DH, a, :], lambda t_, a=a: t_[a * DH:(a + 1) * DH, 0:S])
                                     for a in range(2)])
                    carry("e.vw", [(nv[1][:, :, a, a * DH:(a + 1) * DH],
                                    lambda t_, a=a: t_[:, 0:256].rearrange("p (t c) -> p t c", t=2)[:, :, a * DH:(a + 1) * DH])
                                   for a in range(2)])
            whole(gates, "e.gates", ACT.Exp, scale=-1.0)
            for j, n in enumerate("kv"):
                whole(h1T[:, j, :, :], f"e.h1{n}", ACT.Gelu_apprx_tanh)
            carry("e.kc", [(kcz[a * DH:(a + 1) * DH, a, 0:N_CMP], lambda t, a=a: t[0:DH, a * N_CMP:(a + 1) * N_CMP])
                           for a in range(2)])
            carry("e.vc", [(vcz[0:N_CMP, a, a * DH:(a + 1) * DH], lambda t, a=a: t[0:N_CMP, a * DH:(a + 1) * DH])
                           for a in range(2)])
            attention(numbered(nsa_units(), ATT["nsa"]))
            for j in range(2):
                whole(mq[:, 2 * j:2 * j + 2, :], f"e.mq.{j}", scale=0.125)
            act.wait_ge(zeros_set, 2)
            for j in range(2):
                carry(f"e.mk.{j}", [(mk[a * DH:(a + 1) * DH, 4 * a + 2 * j:4 * a + 2 * j + 2, :],
                                     lambda t, a=a: t[a * DH:(a + 1) * DH, :].rearrange("p (i s) -> p i s", i=2))
                                    for a in range(2)])
            for T in range(NT):
                carry(f"e.mv.{T}", [(mv[:, T, 4 * a:4 * a + 4, a * DH:(a + 1) * DH],
                                     lambda t, a=a: t[:, :].rearrange("p (i c) -> p i c", i=4)[:, :, a * DH:(a + 1) * DH])
                                    for a in range(2)])
            attention(numbered(moba_units(), ATT["moba"]))
            modulated("e.turn1", 0, 24)
            act.wait_ge(router_in, 3)
            fn(rA, rA, ACT.Exp, scale=-1.0).then_inc(router_exp, 1)
            experts("e.moe")

            modulated("o.turn0", 1, 0)
            for T in range(NT):
                whole(cq[:, T, :], f"o.c.{T}")
            for j in range(2):
                whole(qn[:, 2 * j:2 * j + 2, :], f"o.qn.{j}", scale=MLA_SCALE)
                whole(kn[:, 2 * j:2 * j + 2, :], f"o.kn.{j}")
            for T in range(NT):
                whole(lv[:, T, :], f"o.v.{T}")
            whole(qrT, "o.qrT")
            attention(numbered(mla_units(), ATT["mla"]))
            for j in range(2):
                whole(swq[:, 2 * j:2 * j + 2, :], f"o.sq.{j}", scale=0.125)
            act.wait_ge(zeros_set, 3)
            carry("o.sk", [(swk[a * DH:(a + 1) * DH, a, :], lambda t, a=a: t[a * DH:(a + 1) * DH, 0:S]) for a in range(2)])
            carry("o.sv", [(swv[:, :, a, a * DH:(a + 1) * DH],
                            lambda t, a=a: t[:, 0:256].rearrange("p (t c) -> p t c", t=2)[:, :, a * DH:(a + 1) * DH])
                           for a in range(2)])
            attention(numbered(swa_units(), ATT["swa"]))
            modulated("o.turn1", 1, 24)
            act.wait_ge(router_in, 4)
            fn(rA, rA, ACT.Exp, scale=-1.0).then_inc(router_exp, 1)
            experts("o.moe")

        @block.vector
        def _(dve):
            v = nc.vector
            step = Steps(dve, dve_steps)
            users, stats = [0], [0]

            def drained(name, ins, it=None):
                ins.then_inc(banks.drained[banks.jobs[name][0]], 1)
                banks.wait_drained(dve, name, it)

            def bank(name, it=None):
                banks.wait_full(dve, name, it)
                return psum[banks.jobs[name][0]]

            cells = {}

            def tell(semaphore):
                k = cells.setdefault(str(semaphore), len(cells))
                v.memset(sm("sig")[:, k:k + 1], 0.0).then_inc(semaphore, 1)

            def tt(o, a, b, op):
                return v.tensor_tensor(o, a, b, op)

            def rstd(n):
                stats[0] += 1
                dve.wait_ge(rstd_ready, stats[0])

            def eps(cols, src, scale, e):
                return v.tensor_scalar(stat_in[:, cols], src, scale, e, ALU.mult, ALU.add)

            def vectors_loaded():
                users[0] += 1
                dve.wait_ge(vecs_loaded, 16 * users[0])

            def turned(tag, dest=None):
                dest = xT if dest is None else dest
                for q in (1, 3):
                    p_ = bank(f"{tag}.{q}")
                    drained(f"{tag}.{q}", v.tensor_copy(dest[:, 2 * q:2 * q + 2, :],
                                                        p_[:, :].rearrange("p (a b) -> p a b", a=2)))

            def layer_norm(src):
                bn, mv_ = sm("bn", 2, 2 * 6), sm("mv", 2, 2)
                for T in range(NT):
                    for q in range(2):
                        step(v.bn_stats(bn[:, T, 6 * q:6 * q + 6], src[:, T, q * 512:(q + 1) * 512]))
                    step(v.bn_aggr(mv_[:, T, :], bn[:, T, :]))
                eps(slice(0, 2), mv_[:, :, 1], 1.0, LN_EPS).then_inc(var_ready, 1)
                rstd(2)
                for T in range(NT):
                    step(v.tensor_scalar(x[:, T, :], src[:, T, :], mv_[:, T, 0:1], stat_out[:, T:T + 1],
                                         ALU.subtract, ALU.mult))
                vectors_loaded()
                step(tt(x[:, :, :], x[:, :, :], lnv[:, 0:1, :].broadcast_to([P, NT, D]), ALU.mult))
                step(tt(x[:, :, :], x[:, :, :], lnv[:, 1:2, :].broadcast_to([P, NT, D]), ALU.add))
                tell(vecs_used)

            def residual(tag):
                for T, q in OUTS:
                    p_ = bank(f"{tag}.{T}.{q}")
                    c = slice(q * 512, (q + 1) * 512)
                    drained(f"{tag}.{T}.{q}", v.scalar_tensor_tensor(
                        out=x[:, T, c], in0=x[:, T, c], scalar=ALPHA, in1=p_[:, :], op0=ALU.mult, op1=ALU.add))

            def tell_x():
                tell(x_ready)

            def attention(units):
                def biased_max(u):
                    i, nk_ = u["n"] % 2, u["nk"]
                    p_ = bank(u["name"] + ".s")
                    if u["bias"] is None:
                        v.tensor_reduce(nm[:, i, :], p_[:, :].rearrange("p (a s) -> p a s", a=2), AX.X, ALU.max,
                                        negate=True).then_inc(att_max, 1)
                        return
                    mx = sm("mx", 2, 2)[:, i, :]
                    for a in range(2):
                        ins = v.tensor_tensor_reduce(
                            out=aS[:, i, a, 0:nk_], in0=p_[:, a * S:a * S + nk_], in1=u["bias"][a], scale=1.0,
                            scalar=LOW, op0=ALU.add, op1=ALU.max, accum_out=mx[:, a:a + 1])
                        if a == 0:
                            step(ins)
                    drained(u["name"] + ".s", ins)
                    if u["sink"] is not None:
                        step(tt(mx, mx, u["sink"], ALU.max))
                        step(tt(sm("es", 2, 2)[:, i, :], u["sink"], mx, ALU.subtract))
                    v.tensor_scalar(nm[:, i, :], mx, -1.0, None, ALU.mult).then_inc(att_max, 1)

                def normalise(u):
                    i, nk_ = u["n"] % 2, u["nk"]
                    if u["bias"] is None:
                        banks.wait_drained(dve, u["name"] + ".s")
                    else:
                        exps[0] += 1
                        dve.wait_ge(att_exp, exps[0])
                    if u["sink"] is not None:
                        step(tt(den[:, i, :], den[:, i, :], sm("es", 2, 2)[:, i, :], ALU.add))
                    step(v.reciprocal(den[:, i, :], den[:, i, :]))
                    if u["gate"] is not None:
                        step(tt(den[:, i, :], den[:, i, :], u["gate"], ALU.mult))
                    tt(aP[:, i, :, 0:nk_], aP[:, i, :, 0:nk_],
                       den[:, i, :].unsqueeze(2).broadcast_to([P, 2, nk_]), ALU.mult).then_inc(att_prob, 1)

                def outputs(u):
                    if u["last"]:
                        p_ = bank(u["o"])
                        r = u["regions"]
                        drained(u["o"], v.tensor_copy(u["dest"], p_[:, 0:r * P].rearrange("p (a b) -> p a b", a=r)))

                n = len(units)
                for k in range(n + 2):
                    if k < n:
                        biased_max(units[k])
                    if 1 <= k <= n:
                        normalise(units[k - 1])
                    if k >= 2:
                        outputs(units[k - 2])

            exps = [0]

            def route(tag, bname, first):
                p_ = bank(f"{tag}.logits")
                lg = p_[:, 0:32].rearrange("p (t e) -> p t e", t=2)
                if first:
                    drained(f"{tag}.logits", tt(rA, lg, pr("b_router").unsqueeze(1).broadcast_to([P, 2, 16]), ALU.add))
                    step(v.tensor_reduce(r2a, rA, AX.X, ALU.max))
                    tt(rA, rA, r2a.unsqueeze(2).broadcast_to([P, 2, 16]), ALU.subtract).then_inc(router_in, 1)
                    routed[0] += 1
                    dve.wait_ge(router_exp, routed[0])
                    step(v.tensor_reduce(r2a, rA, AX.X, ALU.add))
                    step(v.reciprocal(r2a, r2a))
                    step(tt(rA, rA, r2a.unsqueeze(2).broadcast_to([P, 2, 16]), ALU.mult))
                    score = rA
                else:
                    banks_copy = v.tensor_copy(rA, lg)
                    drained(f"{tag}.logits", banks_copy)
                    tell(router_in)
                    routed[0] += 1
                    dve.wait_ge(router_exp, routed[0])
                    step(v.tensor_scalar(rA, rA, 1.0, None, ALU.add))
                    step(v.reciprocal(rA, rA))
                    step(tt(rB, rA, pr("router_b_2").unsqueeze(1).broadcast_to([P, 2, 16]), ALU.add))
                    score = rB
                four = score.rearrange("p t (g j) -> p (t g) j", g=4)
                step(tt(r_hi, four[:, :, 0:4:2], four[:, :, 1:4:2], ALU.max))
                step(tt(r_lo, four[:, :, 0:4:2], four[:, :, 1:4:2], ALU.min))
                step(tt(r8a, r_hi[:, :, 0], r_hi[:, :, 1], ALU.max))
                step(tt(r8b, r_hi[:, :, 0], r_hi[:, :, 1], ALU.min))
                step(tt(r8c, r_lo[:, :, 0], r_lo[:, :, 1], ALU.max))
                step(tt(r8b, r8b, r8c, ALU.max))
                step(tt(r8a, r8a, r8b, ALU.add))

                def first_best(o, values):
                    step(v.tensor_reduce(r2a, values, AX.X, ALU.max))
                    step(tt(o, values, r2a.unsqueeze(2).broadcast_to([P, 2, 4]), ALU.is_equal))
                    step(tt(o, o, cs("rank4").unsqueeze(1).broadcast_to([P, 2, 4]), ALU.mult))
                    step(v.tensor_reduce(r2a, o, AX.X, ALU.max))
                    step(tt(o, o, r2a.unsqueeze(2).broadcast_to([P, 2, 4]), ALU.is_equal))

                first_best(r_g, r8a.rearrange("p (t g) -> p t g", t=2))

                def in_group(o, values):
                    step(tt(r_tmp, values.rearrange("p t (g j) -> p t g j", g=4),
                            r_g.unsqueeze(3).broadcast_to([P, 2, 4, 4]), ALU.mult))
                    step(v.tensor_reduce(o, r_tmp.rearrange("p t g j -> p t j g"), AX.X, ALU.add))

                in_group(r_b, score)
                in_group(r_a, rA)
                first_best(r_1, r_b)
                step(v.scalar_tensor_tensor(out=r_b, in0=r_1, scalar=NEG, in1=r_b, op0=ALU.mult, op1=ALU.add))
                first_best(r_2, r_b)
                step(tt(r_1, r_1, r_2, ALU.add))
                step(tt(r_a, r_a, r_1, ALU.mult))
                step(v.tensor_reduce(r2a, r_a, AX.X, ALU.add))
                step(v.reciprocal(r2a, r2a))
                step(tt(r_a, r_a, r2a.unsqueeze(2).broadcast_to([P, 2, 4]), ALU.mult))
                step(tt(gate.rearrange("p t (g j) -> p t g j", g=4), r_g.unsqueeze(3).broadcast_to([P, 2, 4, 4]),
                        r_a.unsqueeze(2).broadcast_to([P, 2, 4, 4]), ALU.mult))

            routed = [0]

            def experts(tag, ada_layer):
                with dve.Fori(0, BODIES) as it:
                    step.enter(it, 14 if ada_layer is not None else 0)

                    def ada_sum(k):
                        n = 2 * BODIES * ada_layer + k
                        dve.wait_ge(ada_loaded, it * 32 + 16 * (n + 1))
                        for c in range(DC):
                            ins = v.scalar_tensor_tensor(
                                out=ada_acc, in0=ada_in[:, c, :], scalar=sm("sc")[:, c:c + 1],
                                in1=ada_in[:, DC, :] if c == 0 else ada_acc, op0=ALU.mult, op1=ALU.add)
                            if c < DC - 1:
                                step(ins)
                        ins.then_inc(ada_summed, 1)

                    def ada_out(k):
                        p_ = bank(f"{tag}.ada{k}", it)
                        drained(f"{tag}.ada{k}", v.tensor_copy(
                            sm("modc", 2, 48)[:, ada_layer, bass.ds(it * 6 + 3 * k, 3)], p_[:, 0:3]), it)

                    def h(k):
                        banks.wait_drained(dve, f"{tag}.g{k}", it)
                        p_ = bank(f"{tag}.u{k}", it)
                        tt(eh[:, k % 2, :], esig[:, k % 2, :], p_[:, :], ALU.mult).then_inc(
                            banks.drained[banks.jobs[f"{tag}.u{k}"][0]], 1)

                    def y(k):
                        e, T = divmod(k, 2)
                        for n in range(2):
                            if k >= 2:
                                banks.wait_drained(dve, f"{tag}.y{k - 2}.{n}", it)
                            else:
                                banks.wait_drained_round_before(dve, f"{tag}.y{k + 2}.{n}", it)
                            p_ = bank(f"{tag}.y{k}.{n}", it)
                            c = slice(n * 512, (n + 1) * 512)
                            v.scalar_tensor_tensor(
                                out=mix[:, T, c], in0=p_[:, :], scalar=gate[:, T, bass.ds(it * 2 + e, 1)],
                                in1=mix[:, T, c], op0=ALU.mult, op1=ALU.add).then_inc(
                                    banks.drained[banks.jobs[f"{tag}.y{k}.{n}"][0]], 1)

                    ada_on = ada_layer is not None
                    if ada_on:
                        ada_sum(0)
                    h(0)
                    h(1)
                    y(0)
                    if ada_on:
                        ada_out(0)
                        ada_sum(1)
                    h(2)
                    y(1)
                    h(3)
                    y(2)
                    if ada_on:
                        ada_out(1)
                    y(3)
                step.leave(BODIES)
                for k in (2, 3):
                    for n in range(2):
                        banks.wait_drained(dve, f"{tag}.y{k}.{n}", rounds=BODIES)

            def rms(src_scale, e, cols, parts, junk):
                for k, part in enumerate(parts):
                    step(v.tensor_tensor_reduce(out=junk(k), in0=part, in1=part, scale=1.0, scalar=0.0,
                                                op0=ALU.mult, op1=ALU.add, accum_out=stat_in[:, cols + k:cols + k + 1]))

            def adaptive_norm(tag, layer, gain, scale, shift):
                rms(None, None, 0, [x[:, T, :] for T in range(NT)], lambda T: mix[:, T, :])
                eps(slice(0, 2), stat_in[:, 0:2], 1.0 / D, RMS_EPS).then_inc(var_ready, 1)
                rstd(2)
                step(v.scalar_tensor_tensor(out=sm("modg")[:, 0:8], in0=sm("modc", 2, 48)[:, layer, scale:scale + 8],
                                            scalar=1.0, in1=gain, op0=ALU.add, op1=ALU.mult))
                for T in range(NT):
                    step(v.tensor_scalar(mix[:, T, :], x[:, T, :], stat_out[:, T:T + 1], None, ALU.mult))
                tell_x()
                for q in (1, 3):
                    p_ = bank(f"{tag}.{q}")
                    for j in range(2):
                        c = 2 * q + j
                        ins = v.tensor_scalar(xT[:, c, :], p_[:, j * S:(j + 1) * S], sm("modg")[:, c:c + 1],
                                              sm("modc", 2, 48)[:, layer, shift + c:shift + c + 1], ALU.mult, ALU.add)
                        if j == 0:
                            step(ins)
                    drained(f"{tag}.{q}", ins)

            def take_gate(tag):
                for q in range(2):
                    p_ = bank(f"{tag}.{q}")
                    drained(f"{tag}.{q}", v.tensor_copy(gate_row[:, q * 512:(q + 1) * 512], p_[:, :]))

            def gated_residual(tag):
                for T, q in OUTS:
                    p_ = bank(f"{tag}.{T}.{q}")
                    c = slice(q * 512, (q + 1) * 512)
                    drained(f"{tag}.{T}.{q}", tt(mix[:, T, c], p_[:, :], gate_row[:, c], ALU.mult))
                    step(tt(x[:, T, c], x[:, T, c], mix[:, T, c], ALU.add))

            def gated_sum():
                step(tt(mix[:, :, :], mix[:, :, :], gate_row.unsqueeze(1).broadcast_to([P, NT, D]), ALU.mult))
                step(tt(x[:, :, :], x[:, :, :], mix[:, :, :], ALU.add))

            step(v.memset(stat_in, 1.0))
            v.memset(alow[:, :], 1.0).then_inc(ones_set, 1)
            dve.wait_ge(setup_loaded, 32)
            pads, pad_max = sm("pads", 2 * NT, 8), sm("padmax", 2 * NT, 8)
            step(tt(pad_w, pr("rel_rows", 8, 33).unsqueeze(1).broadcast_to([P, 2 * NT, 8, 33]),
                    cs("lncount", 2 * NT, 33).unsqueeze(2).broadcast_to([P, 2 * NT, 8, 33]), ALU.add))
            step(v.tensor_reduce(pad_max, pad_w, AX.X, ALU.max))
            tt(pad_w, pad_w, pad_max.unsqueeze(3).broadcast_to([P, 2 * NT, 8, 33]), ALU.subtract).then_inc(pads_in, 1)
            dve.wait_ge(pads_fn, 1)
            v.tensor_reduce(pads, pad_w, AX.X, ALU.add).then_inc(pads_in, 1)
            dve.wait_ge(pads_fn, 2)
            step(tt(pads, pads, pad_max, ALU.add))
            for l in range(DEPTH):
                v.memset(pr("w_s", 2, 4, P)[64:P, l, :, 0:64], 0.0).then_inc(ws_masked, 1)
            dve.wait_ge(xT_loaded, 48)
            dve.wait_ge(silu_c, 1)

            for l in range(DEPTH):
                tg = f"{l}"
                if l:
                    turned(f"{l - 1}.turn3")
                p_ = bank(f"{tg}.k")
                drained(f"{tg}.k", v.tensor_copy(gk, p_[:, :].rearrange("p (t n) -> p t n", t=2)))
                if l == 0:
                    dve.wait_ge(rows_out, 128)
                p_ = bank(f"{tg}.z")
                z = p_[:, :].rearrange("p (t n) -> p t n", t=2)
                step(v.tensor_scalar(gg, z, 0.0, None, ALU.min))
                ins = v.scalar_tensor_tensor(out=gE, in0=gg, scalar=-2.0, in1=z, op0=ALU.mult, op1=ALU.add)
                drained(f"{tg}.z", ins)
                tell(gla_abs)
                dve.wait_ge(gla_log, l + 1)
                tt(gg, gg, gE, ALU.subtract).then_inc(gla_g, 1)
                banks.wait_drained(dve, f"{tg}.rem")
                for c in range(NCHUNK):
                    T = c // 2
                    ins = v.scalar_tensor_tensor(out=gkd[:, c, :], in0=gk[:, T, :], scalar=inch[:, c % 2:c % 2 + 1],
                                                 in1=gE[:, T, :], op0=ALU.mult, op1=ALU.mult)
                    if c < NCHUNK - 1:
                        step(ins)
                ins.then_inc(gla_kd, 1)
                banks.wait_drained(dve, f"{tg}.dec")
                for c in range(NCHUNK):
                    p_ = bank(f"{tg}.kv.{c}")
                    ins = tt(states[:, c, :, :], p_[:, :].rearrange("p (m n) -> p m n", m=2),
                             blocks.unsqueeze(1).broadcast_to([P, 2, 256]), ALU.mult)
                    drained(f"{tg}.kv.{c}", ins)
                    if c == 0:
                        tell(gla_state)
                    else:
                        dve.wait_ge(gla_state, NCHUNK * l + c)
                        for m in range(2):
                            ins = v.scalar_tensor_tensor(out=states[:, c, m, :], in0=states[:, c - 1, m, :],
                                                         scalar=decay[:, m, c:c + 1], in1=states[:, c, m, :],
                                                         op0=ALU.mult, op1=ALU.add)
                            if m == 0:
                                step(ins)
                        ins.then_inc(gla_state, 1)
                banks.wait_drained(dve, f"{tg}.sv.1")
                bnb, mvb = sm("bnb", 8, 6), sm("mvb", 8, 2)
                for k in range(8):
                    T, g = divmod(k, 4)
                    step(v.bn_stats(bnb[:, k, :], sv[:, T, g * P:(g + 1) * P]))
                    step(v.bn_aggr(mvb[:, k, :], bnb[:, k, :]))
                eps(slice(0, 8), mvb[:, :, 1], 1.0, LN_EPS).then_inc(var_ready, 1)
                rstd(8)
                for k in range(8):
                    T, g = divmod(k, 4)
                    part = sv[:, T, g * P:(g + 1) * P]
                    step(v.tensor_scalar(part, part, mvb[:, k, 0:1], stat_out[:, k:k + 1], ALU.subtract, ALU.mult))
                vectors_loaded()
                step(tt(sv, sv, mixv[:, 1:2, :].broadcast_to([P, NT, 512]), ALU.mult))
                tt(sv, sv, mixv[:, 2:3, :].broadcast_to([P, NT, 512]), ALU.add).then_inc(sgu_ready, 1)
                dve.wait_ge(sgu_ready, l + 1)
                for c in range(NCHUNK):
                    p_ = bank(f"{tg}.o.{c}")
                    rows = slice((c % 2) * 64, (c % 2) * 64 + 64)
                    drained(f"{tg}.o.{c}", v.tensor_copy(mix[rows, c // 2, 0:512], p_[rows, :]))
                sq = cut(oT[:, :, :].rearrange("p a b -> p (a b)"), 1024, NT, 512)
                o_ = mix[:, :, 0:512]
                step(tt(sq, o_, o_, ALU.mult))
                step(v.tensor_reduce(stat_in[:, 0:8], sq.rearrange("p t (h d) -> p (t h) d", h=4), AX.X, ALU.add))
                eps(slice(0, 8), stat_in[:, 0:8], 1.0 / P, RMS_EPS).then_inc(var_ready, 1)
                rstd(8)
                for T in range(NT):
                    oh = mix[:, T, 0:512].rearrange("p (h d) -> p h d", h=4)
                    step(tt(oh, oh, stat_out[:, 4 * T:4 * T + 4].unsqueeze(2).broadcast_to([P, 4, P]), ALU.mult))
                step(tt(o_, o_, mixv[:, 0:1, :].broadcast_to([P, NT, 512]), ALU.mult))
                tell(vecs_used)
                step(tt(o_, o_, gr, ALU.mult))
                for T in range(NT):
                    p_ = bank(f"{tg}.mix.{T}")
                    for g in range(SGU_GROUPS):
                        c = slice(g * P, (g + 1) * P)
                        ins = v.scalar_tensor_tensor(out=mix[:, T, 512 + g * P:512 + (g + 1) * P], in0=p_[:, c],
                                                     scalar=pr("b_s")[:, 4 * l + g:4 * l + g + 1],
                                                     in1=su[:, T, c], op0=ALU.add, op1=ALU.mult)
                        if g < SGU_GROUPS - 1:
                            step(ins)
                    drained(f"{tg}.mix.{T}", ins)
                turned(f"{tg}.turn0", oT)
                residual(f"{tg}.out")
                layer_norm(x)
                tell_x()
                turned(f"{tg}.turn1")
                attention(numbered(cross_units(f"{tg}.x"), ATT[f"{tg}.x"]))
                residual(f"{tg}.xo")
                layer_norm(x)
                tell_x()
                turned(f"{tg}.turn2")
                route(tg, "b_router", True)
                step(v.tensor_scalar(mix[:, :, :], x[:, :, :], ALPHA, None, ALU.mult))
                experts(f"{tg}.moe", l)
                layer_norm(mix)
                if l == 0:
                    tell_x()

            adaptive_norm("e.turn0", 0, pr("norm_mix")[:, 0:8], 8, 0)
            p_ = bank("e.c")
            for j, pos in enumerate(("pos_k", "pos_v")):
                for a in range(2):
                    view = p_[a * DH:(a + 1) * DH, j * S:(j + 1) * S].rearrange("p (b r) -> p r b", r=16)
                    for odd in range(2):
                        for half in range(2):
                            ins = tt(flat[odd * DH:(odd + 1) * DH, j, 8 * half:8 * half + 8, a * N_CMP:(a + 1) * N_CMP],
                                     view[:, odd:16:2, half:half + N_CMP],
                                     pr(pos)[odd * DH:(odd + 1) * DH, 8 * half:8 * half + 8].unsqueeze(2)
                                     .broadcast_to([DH, 8, N_CMP]), ALU.add)
                            if (j, a, odd, half) != (1, 1, 1, 1):
                                step(ins)
            drained("e.c", ins)
            banks.wait_drained(dve, "e.gates")
            step(v.tensor_scalar(gates, gates, 1.0, None, ALU.add))
            step(v.reciprocal(gates, gates))
            for T in range(NT):
                g0 = gates[:, T, 0:24:3]
                step(v.tensor_scalar(g0, g0, cs("valid")[:, T:T + 1], None, ALU.mult))
            dve.wait_ge(bias_back, 32)
            attention(numbered(nsa_units(), ATT["nsa"]))
            attention(numbered(moba_units(), ATT["moba"]))
            take_gate("e.gm")
            gated_residual("e.out")
            adaptive_norm("e.turn1", 0, pr("norm_ffn")[:, 0:8], 32, 24)
            route("e", "router_b_2", False)
            step(v.memset(mix[:, :, :], 0.0))
            experts("e.moe", None)
            take_gate("e.gf")
            gated_sum()

            adaptive_norm("o.turn0", 1, pr("norm_mix")[:, 8:16], 8, 0)
            banks.wait_drained(dve, "o.c.0")
            banks.wait_drained(dve, "o.c.1")
            rms(None, None, 0, [cq[:, T, 0:256] for T in range(NT)] + [cq[:, T, 256:384] for T in range(NT)],
                lambda k: rt[:, 0:256] if k < 2 else rt[:, 0:128])
            step(eps(slice(0, 2), stat_in[:, 0:2], 1.0 / 256, RMS_EPS))
            eps(slice(2, 4), stat_in[:, 2:4], 1.0 / 128, RMS_EPS).then_inc(var_ready, 1)
            rstd(4)
            for T in range(NT):
                step(v.tensor_scalar(cq[:, T, 0:256], cq[:, T, 0:256], stat_out[:, T:T + 1], None, ALU.mult))
                ins = v.tensor_scalar(cq[:, T, 256:384], cq[:, T, 256:384], stat_out[:, 2 + T:3 + T], None, ALU.mult)
                if T == 0:
                    step(ins)
            ins.then_inc(lat_ready, 1)
            dve.wait_ge(lat_ready, 1)
            cos, sin = cs("cos", NT, 32), cs("sin", NT, 32)

            def rotate(o1, o2, x1, x2, c, s_, t1, t2):
                step(tt(t1, x1, c, ALU.mult))
                step(tt(t2, x2, s_, ALU.mult))
                step(tt(o1, t1, t2, ALU.subtract))
                step(tt(t1, x1, s_, ALU.mult))
                step(tt(t2, x2, c, ALU.mult))
                step(tt(o2, t1, t2, ALU.add))

            t1, t2 = (rt[:, a:a + 64].rearrange("p (t n) -> p t n", t=2) for a in (0, 64))
            rotate(kr2[:, :, 0:32], kr2[:, :, 32:64], cq[:, :, 384:416], cq[:, :, 416:448], cos, sin, t1, t2)
            v.tensor_copy(kr2[:, :, 64:128], kr2[:, :, 0:64]).then_inc(rope_ready, 1)
            p_ = bank("o.cqT")
            for j in range(2):
                ins = v.tensor_scalar(cT[:, j, :], p_[:, j * S:(j + 1) * S], pr("q_norm")[:, j:j + 1], None, ALU.mult)
                if j == 0:
                    step(ins)
            drained("o.cqT", ins)
            p_ = bank("o.ckvT")
            drained("o.ckvT", v.tensor_scalar(cT[:, 2, :], p_[:, 0:S], pr("kv_norm")[:, 0:1], None, ALU.mult))
            p_ = bank("o.qr")
            drained("o.qr", v.tensor_scalar(qrn, p_[:, :].rearrange("p (t n) -> p t n", t=2), MLA_SCALE, None, ALU.mult))
            for T in range(NT):
                q4 = qrn[:, T, :].rearrange("p (h n) -> p h n", h=4)
                o4 = qro[:, T, :].rearrange("p (h n) -> p h n", h=4)
                c4, s4 = (t[:, T:T + 1, :].broadcast_to([P, 4, 32]) for t in (cos, sin))
                t1, t2 = (rt[:, a:a + 128].rearrange("p (h n) -> p h n", h=4) for a in (0, 128))
                rotate(o4[:, :, 0:32], o4[:, :, 32:64], q4[:, :, 0:32], q4[:, :, 32:64], c4, s4, t1, t2)
            tell(rope_ready)
            dve.wait_ge(zeros_set, 3)
            p_ = bank("o.krT")
            for a in range(2):
                ins = v.tensor_copy(krz[a * DH:(a + 1) * DH, a, :], p_[a * DH:(a + 1) * DH, 0:S])
                if a == 0:
                    step(ins)
            drained("o.krT", ins)
            attention(numbered(mla_units(), ATT["mla"]))
            dve.wait_ge(bias_ready, 1)
            attention(numbered(swa_units(), ATT["swa"]))
            take_gate("o.gm")
            gated_residual("o.out")
            adaptive_norm("o.turn1", 1, pr("norm_ffn")[:, 8:16], 32, 24)
            route("o", "router_b_2", False)
            step(v.memset(mix[:, :, :], 0.0))
            experts("o.moe", None)
            take_gate("o.gf")
            gated_sum()
            rms(None, None, 0, [x[:, T, :] for T in range(NT)], lambda T: mix[:, T, :])
            eps(slice(0, 2), stat_in[:, 0:2], 1.0 / D, RMS_EPS).then_inc(var_ready, 1)
            rstd(2)
            vectors_loaded()
            for T in range(NT):
                v.scalar_tensor_tensor(out=mix[:, T, :], in0=x[:, T, :], scalar=stat_out[:, T:T + 1],
                                       in1=lnv[:, 0, :], op0=ALU.mult, op1=ALU.mult).then_inc(out_ready, 1)

        @block.gpsimd
        def _(pool):
            loads, stats = [0], [0]

            def load_vectors(dest, row, rows, after=None):
                if loads[0]:
                    pool.wait_ge(vecs_used, loads[0])
                loads[0] += 1
                pool.dma_start(dest, vecs[row:row + rows, :].rearrange("r n -> (r n)").partition_broadcast(P)) \
                    .then_inc(vecs_loaded, 16)

            def rstd():
                stats[0] += 1
                pool.wait_ge(var_ready, stats[0])
                nc.gpsimd.tensor_tensor(stat_out, stat_in, cs("half"), ALU.pow).then_inc(rstd_ready, 1)

            pool.wait_ge(setup_loaded, 32)
            for l in range(DEPTH):
                flat_v = work[:, LNV:LNV + 2048]
                load_vectors(flat_v, 8 * l, 2)
                rstd()
                rstd()
                load_vectors(flat_v, 8 * l + 2, 2)
                rstd()
                load_vectors(flat_v, 8 * l + 4, 2)
                rstd()
                load_vectors(flat_v, 8 * l + 6, 2)
                pool.wait_ge(x_ready, 3 * l + 2)
                with pool.Fori(0, NEXP) as it:
                    pool.wait_ge(ada_summed, it + NEXP * l)
                    pool.dma_start(ada_in, ada[l, bass.ds(it, 1), :, :].rearrange("e p (c n) -> p (e c) n", c=DC + 1)) \
                        .then_inc(ada_loaded, 16)
                rstd()
            rstd()
            pool.wait_ge(x_ready, 6)
            nc.gpsimd.memset(work[:, NS + 1024:NS + 3360], 0.0).then_inc(zeros_set, 1)
            banks.wait_drained(pool, "e.vc")
            nc.gpsimd.memset(work[:, MB + 1024:MB + 5120], 0.0).then_inc(zeros_set, 1)
            rstd()
            pool.wait_ge(x_ready, 7)
            w0 = bias[:, :, 1, 0:P]
            nc.gpsimd.affine_select(out=w0, in_=w0, pattern=[[0, 8], [1, P]], compare_op=ALU.is_gt, fill=NEG,
                                    base=0, channel_multiplier=-1).then_inc(bias_ready, 1)
            rstd()
            pool.wait_ge(x_ready, 8)
            nc.gpsimd.memset(work[:, NS + 7040:NS + 8576], 0.0).then_inc(zeros_set, 1)
            rstd()
            rstd()
            pool.wait_ge(x_ready, 9)
            load_vectors(work[:, LNV:LNV + D], 16, 1)
            rstd()

        @block.sync
        def _(sp):
            def load(g, j, static=False):
                src = weights[g * RING + j] if static else \
                    weights[bass.ds(g * RING + j, 1), :, :].rearrange("m p n -> p (m n)")
                sp.dma_start(ring[:, j, :], src).then_inc(slot_full[j], 16)

            for j in range(RING):
                load(0, j, True)
            rounds = NPIECES // RING
            with sp.Fori(1, rounds) as g:
                for j in range(RING):
                    sp.wait_ge(pieces_done, g * RING + (j - RING + 1))
                    load(g, j)
            for j in range(NPIECES - rounds * RING):
                sp.wait_ge(pieces_done, rounds * RING + j - RING + 1)
                load(rounds, j, True)
            for T in range(NT):
                sp.wait_ge(out_ready, T + 1)
                sp.dma_start(out[T * P:(T + 1) * P, :], mix[:, T, :]).then_inc(out_stored, 16)
            sp.wait_ge(out_stored, 16 * NT)


def chunks(w):
    k, n = w.shape
    return w.reshape(k // P, P, n).transpose(1, 0, 2).reshape(P, -1)


def pairs(w):
    return w.reshape(w.shape[0], 2, PAIRS, DH).transpose(0, 2, 1, 3).reshape(w.shape[0], -1)


def layouts(a):
    weights = np.zeros((NPIECES, P, PIECE), np.float32)
    at = [0]

    def put(*parts):
        col = 0
        for part in parts:
            weights[at[0], :, col:col + part.shape[1]] = part
            col += part.shape[1]
        at[0] += 1

    def put_cols(w):
        full = np.zeros((D, -(-w.shape[1] // 512) * 512), np.float32)
        full[:, :w.shape[1]] = w
        for q in range(full.shape[1] // 512):
            put(chunks(full[:, q * 512:(q + 1) * 512]))

    def put_experts(g, u, d):
        for e in range(NEXP):
            put(chunks(g[e]))
            put(chunks(u[e]))
            put(chunks(d[e]))

    for l in range(DEPTH):
        w = a["w_in"][l]
        put_cols(w[:, 0:512])
        put_cols(w[:, 512:1024])
        put_cols(w[:, 1024:1536])
        put_cols(w[:, 1552:2576])
        put_cols(a["wk_x"][l])
        put_cols(a["wv_x"][l])
        put_cols(a["w_out"][l])
        put_cols(a["wq_x"][l])
        put_cols(a["wo_x"][l])
        put_experts(a["w_gate"][l], a["w_up"][l], a["w_down"][l])

    def pair_rows(w):
        return pairs(w.T).T

    w = a["ev_w_in_2"][0]
    put_cols(pairs(w[:, 0:512]))
    put_cols(w[:, 512:1024])
    put_cols(w[:, 1024:1280])
    put(chunks(a["nsa_ck_w1_2"][0]))
    put(chunks(a["nsa_cv_w1_2"][0]))
    for q in range(3):
        put_cols(pairs(w[:, 1304 + 512 * q:1816 + 512 * q]))
    wo = a["ev_w_out_2"][0]
    put_cols(np.concatenate([pair_rows(wo[:512]), pair_rows(wo[512:])]))
    put_experts(a["moe_w_gate_2"][0], a["moe_w_up_2"][0], a["moe_w_down_2"][0])
    w = a["od_w_in_2"][0]
    put_cols(w[:, 0:448])
    put(chunks(a["mla_w_q_up_2"][0]), a["mla_w_kv_up_2"][0])
    put_cols(pairs(w[:, 448:960]))
    put_cols(w[:, 960:1216])
    wo = a["od_w_out_2"][0]
    put_cols(np.concatenate([wo[:512], pair_rows(wo[512:])]))
    put_experts(a["moe_w_gate_2"][1], a["moe_w_up_2"][1], a["moe_w_down_2"][1])
    assert at[0] == NPIECES, at

    ada = np.zeros((DEPTH, NEXP, P, DC + 1, ADA_COLS), np.float32)
    ada[:, :, :, 0:DC] = a["ada_w_2"].reshape(DEPTH, DC, P, NEXP, ADA_COLS).transpose(0, 3, 2, 1, 4)
    ada[:, :, 0, DC] = a["ada_b_2"].reshape(DEPTH, NEXP, ADA_COLS)

    prm = np.zeros((P, PARAM_N), np.float32)

    def param(name, v):
        lo, hi = PARAM[name]
        prm[:v.shape[0], lo:hi] = v.reshape(v.shape[0], hi - lo)

    def col(v):
        return v.reshape(-1, P).T

    def rows(v):
        return np.broadcast_to(v, (P, v.shape[0]))

    param("w_alow", np.concatenate([chunks(a["w_in"][l][:, 1536:1552]) for l in range(2)], 1))
    param("w_router", chunks(a["w_router"]))
    param("router_w_2", chunks(a["router_w_2"]))
    param("w_gates", chunks(a["ev_w_in_2"][0][:, 1280:1304]))
    param("b_s", a["b_s"].transpose(2, 0, 1).reshape(P, 8))
    param("w_s", a["w_s"].transpose(3, 0, 1, 2).reshape(P, -1))
    param("w_a2", np.concatenate([np.concatenate([a["w_a2"][l], a["b_a"][l][None]]) for l in range(2)], 1))
    param("c", col(a["c_2"]))
    param("norm_mix", np.concatenate([col(a["norm_mix_2"][l]) for l in range(2)], 1))
    param("norm_ffn", np.concatenate([col(a["norm_ffn_2"][l]) for l in range(2)], 1))
    param("q_norm", col(a["mla_q_norm_2"]))
    param("kv_norm", col(a["mla_kv_norm_2"]))
    for name, key in (("pos_k", "nsa_pos_k_2"), ("pos_v", "nsa_pos_v_2")):
        param(name, a[key][0].reshape(16, 2, DH).transpose(1, 2, 0).reshape(P, 16))
    param("ck_w2", chunks(a["nsa_ck_w2_2"][0]))
    param("cv_w2", chunks(a["nsa_cv_w2_2"][0]))
    param("rel_table", np.concatenate([a["rel_table_2"], np.ones((1, 8), np.float32)]))
    param("rel_rows", rows(np.concatenate([a["rel_table_2"].T, a["swa_sinks_2"][0][:, None]], 1).reshape(-1)))
    param("b_router", rows(a["b_router"]))
    param("router_b_2", rows(a["router_b_2"]))

    vecs = np.zeros((17, D), np.float32)
    for l in range(DEPTH):
        vecs[8 * l, :512] = a["gla_norm_g"][l]
        vecs[8 * l, 512:] = a["sgu_ln_g"][l]
        vecs[8 * l + 1, :512] = a["sgu_ln_b"][l]
        for k in range(3):
            vecs[8 * l + 2 + 2 * k] = a["ln_g"][l, k]
            vecs[8 * l + 3 + 2 * k] = a["ln_b"][l, k]
    vecs[16] = a["final_norm_2"]
    x = a["x"][0]
    return {
        "weights": weights, "ada": ada.reshape(DEPTH, NEXP, P, ADA_ROW), "cst": constants(), "prm": prm, "vecs": vecs,
        "x_in": np.ascontiguousarray(x.reshape(NT, P, D).transpose(1, 0, 2)),
        "xT_in": np.ascontiguousarray(x.T.reshape(DC, P, S).transpose(1, 0, 2)),
        "memT_in": np.ascontiguousarray(a["mem"][0].T.reshape(DC, P, S).transpose(1, 0, 2)),
    }


def kernel(**inputs):
    import concourse.bacc as bacc
    from concourse.bass_utils import run_bass_kernel_spmd

    arrays = layouts({k: np.asarray(v) for k, v in inputs.items()})
    nc = bacc.Bacc("TRN2", target_bir_lowering=False, num_devices=1)
    args = [nc.dram_tensor(f"in_{k}", v.shape, F32, kind="ExternalInput").ap() for k, v in arrays.items()]
    out = nc.dram_tensor("out", (S, D), F32, kind="ExternalOutput").ap()
    scratch = nc.dram_tensor("bias_rows", (8, P * (UROW + 1)), F32, kind="Internal").ap()
    program(nc, *args, out, scratch)
    r = run_bass_kernel_spmd(nc, [{f"in_{k}": v for k, v in arrays.items()}], core_ids=[0])
    return r.results[0]["out"].reshape(1, S, D)
```

```python
from contextlib import ExitStack

import numpy as np

import concourse.bass as bass
from concourse import mybir

F32 = mybir.dt.float32
F32R = mybir.dt.float32r
I32 = mybir.dt.int32
ALU = mybir.AluOpType
ACT = mybir.ActivationFunctionType
AX = mybir.AxisListType

P = 128
S = 256
NT = S // P
D = 1024
DC = D // P
DEPTH = 2
CHUNK = 64
NCHUNK = S // CHUNK
GLA_HEADS = 4
SGU_GROUPS = 4
GATE_RANK = 16
NEXP = 16
NGRP = 4
EPG = NEXP // NGRP
HID = 512
HC = HID // P
ALPHA = (2.0 * DEPTH) ** 0.25
LN_EPS = 1e-5
RMS_EPS = 1e-6
NEG = -1e30
LOW = -3.0e38

RING = 4
PIECE = 4096
HALF = PIECE // 2
HI_RING = 4
NBANK = 8
GROUPS = 4
PER_GROUP = NEXP // GROUPS
GROUPS_PER_BODY = 2
EXP_PER_BODY = GROUPS_PER_BODY * PER_GROUP
GATHERS = GROUPS + 1
BODIES = NEXP // EXP_PER_BODY

N_CMP = (S - 32) // 16 + 1
CMP_L = 32
DH = 64
PAIRS = 4
MLA_H = 4
MLA_SCALE = 192.0 ** -0.5
ADA_COLS = 6 * D // NEXP
ADA_PART = ADA_COLS // 2
ADA_ROW = (DC + 1) * ADA_PART
NLIN1 = 5 + 2 + 2 + 2 + 2 + 2
NLIN_EVEN = 8 + 2
NLIN_ODD = 4 + 2
NMOE = 3 * NEXP
NPIECES = 2 * (NLIN1 + NMOE) + NLIN_EVEN + NMOE + NLIN_ODD + NMOE
MOE_FIRST = {"0": NLIN1, "1": 2 * NLIN1 + NMOE, "e": 2 * NLIN1 + 2 * NMOE + NLIN_EVEN,
             "o": 2 * NLIN1 + 3 * NMOE + NLIN_EVEN + NLIN_ODD}
GROUP_ORDER = [("g", 0), ("u", 0), ("g", 1), ("d", 0), ("u", 1), ("g", 2), ("d", 1), ("u", 2), ("g", 3), ("d", 2),
               ("u", 3), ("d", 3)]
MOE_LAYER = {"0": 0, "1": 1, "e": 2, "o": 3}
UROW = 512


def layout(fields):
    at, out = 0, {}
    for name, n in fields:
        out[name] = (at, at + n)
        at += n
    return out, at


CONST, CONST_N = layout([
    ("ident", P), ("later", P), ("inch16", 2), ("inch", 2), ("blocks", 256), ("rank4", 4),
    ("valid", NT), ("causal", NT * S), ("cos", NT * 32), ("sin", NT * 32), ("onehot", UROW),
    ("lncount", 2 * NT * 33), ("before", P), ("iota", P), ("ones", 2), ("half", 16)])
PARAM, PARAM_N = layout([
    ("w_alow", 2 * DC * 16), ("w_router", DC * 16), ("router_w_2", DC * 16), ("w_gates", DC * 24),
    ("b_s", 8), ("w_s", 2 * 4 * P), ("w_a2", 2 * 256), ("c", DC), ("norm_mix", 2 * DC),
    ("norm_ffn", 2 * DC), ("q_norm", 2), ("kv_norm", 1), ("pos_k", 16), ("pos_v", 16),
    ("ck_w2", 2 * DH), ("cv_w2", 2 * DH), ("rel_table", 8), ("rel_rows", 8 * 33), ("b_router", 16),
    ("router_b_2", 16)])


NSA_WINDOW = 512
SWA_WINDOW = 128


def buckets(n):
    d = np.arange(n)
    bounds = [np.ceil(16 * 2.0 ** (3 * k / 8) - 1e-9) for k in range(16)]
    log_part = 15 + np.sum(d[:, None] >= np.array(bounds)[None, :], axis=1)
    return np.where(d < 16, d, np.minimum(log_part, 31))


def constants():
    c = np.zeros((P, CONST_N), np.float32)

    def put(name, a):
        a = np.asarray(a, np.float32)
        c[:a.shape[0], CONST[name][0]:CONST[name][1]] = a.reshape(a.shape[0], -1)

    p = np.arange(P)
    put("ident", np.eye(P))
    same = p[:, None] // CHUNK == p[None, :] // CHUNK
    put("later", np.where(same & (p[:, None] > p[None, :]), 1.0 / 16.0, 0.0))
    inch = p[:, None] // CHUNK == np.arange(2)[None, :]
    put("inch16", inch / 16.0)
    put("inch", inch)
    put("blocks", p[:, None] // 64 == np.arange(256)[None, :] // P)
    put("rank4", np.tile(np.array([4.0, 3.0, 2.0, 1.0]), (P, 1)))
    t = np.arange(NT)[None, :] * P + p[:, None]
    put("valid", t >= CMP_L - 1)
    put("causal", np.where(np.arange(S)[None, None, :] <= t[:, :, None], 0.0, NEG))
    ang = t[:, :, None].astype(np.float32) * (10000.0 ** (-np.arange(0, 64, 2) / 64.0)).astype(np.float32)
    put("cos", np.cos(ang))
    put("sin", np.sin(ang))
    u = np.arange(UROW)
    dist = 255 - u
    hot = np.zeros((33, UROW), np.float32)
    ok = (dist >= 0)
    hot[buckets(S)[dist[ok]], u[ok]] = 1.0
    hot[32, ~ok] = NEG
    put("onehot", hot)
    lncount = np.full((P, 2, NT, 33), NEG)
    for k, window in enumerate((NSA_WINDOW, SWA_WINDOW)):
        of = buckets(window)
        for b in range(32):
            n = np.sum((of == b) & (np.arange(window) > t[:, :, None]), axis=2)
            lncount[:, k, :, b] = np.where(n > 0, np.log(np.maximum(n, 1)), NEG)
    lncount[:, 1, :, 32] = 0.0
    put("lncount", lncount)
    put("before", p[:, None] < p[None, :])
    put("iota", np.tile(p + 1, (P, 1)))
    put("ones", np.ones((P, 2)))
    put("half", np.full((P, 16), -0.5))
    return c


class Banks:

    def __init__(self, full, drained):
        self.full, self.drained = full, drained
        self.count = [0] * NBANK
        self.next = 0
        self.jobs = {}

    def add(self, name):
        b = self.next % NBANK
        self.next += 1
        self.count[b] += 1
        self.jobs[name] = (b, self.count[b], 0)

    def add_loop(self, names, rounds):
        banks = [(self.next + k) % NBANK for k in range(len(names))]
        self.next += len(names)
        for k, (name, b) in enumerate(zip(names, banks)):
            self.jobs[name] = (b, self.count[b] + banks[:k + 1].count(b), banks.count(b))
        for b in range(NBANK):
            self.count[b] += rounds * banks.count(b)

    def number(self, name, it):
        b, n, per = self.jobs[name]
        return b, (n if it is None else it * per + n)

    def wait_full(self, eng, name, it=None, rounds=None):
        b, n = self.number(name, rounds if it is None else it)
        eng.wait_ge(self.full[b], n)

    def wait_drained(self, eng, name, it=None, rounds=None):
        b, n, per = self.jobs[name]
        if rounds is not None:
            n += (rounds - 1) * per
        eng.wait_ge(self.drained[b], n if it is None else it * per + n)

    def wait_drained_round_before(self, eng, name, it):
        b, n, per = self.jobs[name]
        assert n > per
        eng.wait_ge(self.drained[b], it * per + (n - per))

    def wait_free(self, eng, name, it=None):
        b, n, per = self.jobs[name]
        if it is not None:
            eng.wait_ge(self.drained[b], it * per + (n - 1))
        elif n > 1:
            eng.wait_ge(self.drained[b], n - 1)


class Steps:

    def __init__(self, eng, sem):
        self.eng, self.sem, self.n, self.it = eng, sem, 0, None

    def __call__(self, ins):
        self.n += 1
        ins.then_inc(self.sem, 1)
        self.eng.wait_ge(self.sem, self.n if self.it is None else self.it * self.per + self.n)

    def later(self, ins):
        self.n += 1
        ins.then_inc(self.sem, 1)

    def enter(self, it, per):
        self.it, self.per, self.start = it, per, self.n

    def leave(self, rounds):
        assert self.n - self.start == self.per, self.n - self.start
        self.n = self.start + rounds * self.per
        self.it = None


def program(nc, weights, ada, cst, prm, vecs, x_in, xT_in, memT_in, out, scratch):
    ctx = ExitStack()
    with ctx:
        def sb(name, *shape):
            return ctx.enter_context(nc.sbuf_tensor(name, [P, *shape], F32))

        def sem(name):
            return ctx.enter_context(nc.semaphore(name))

        def halves_view(name, *shape):
            plain = sb(name, *shape)
            base = nc.sbuf_base - 4 * int(np.prod(shape))
            return plain, nc.alloc_sbuf_tensor_at(f"{name}_parts", [P, *shape], F32R, offset=base)

        ring, ring_parts = halves_view("ring", RING, PIECE)
        hi_plain, hi_ring = halves_view("hi_ring", HI_RING, HALF)
        x = sb("x", NT, D)
        xT, xT_parts = halves_view("xT", DC, S)
        oT, oT_parts = halves_view("oT", DC, S)
        mix = sb("mix", NT, D)
        consts = sb("consts", CONST_N)
        params = sb("params", PARAM_N)
        work, work_parts = halves_view("work", 14336)
        small = sb("small", 560)
        psum = [ctx.enter_context(nc.psum_tensor(f"bank{b}", [P, 512], F32)) for b in range(NBANK)]

        def cut(t, at, *shape):
            n = int(np.prod(shape))
            ap = t[:, at:at + n]
            if len(shape) == 2:
                return ap.rearrange("p (a b) -> p a b", a=shape[0])
            if len(shape) == 3:
                return ap.rearrange("p (a b c) -> p a b c", a=shape[0], b=shape[1])
            return ap

        def cs(name, *shape):
            return cut(consts, CONST[name][0], *(shape or (CONST[name][1] - CONST[name][0],)))

        def pr(name, *shape):
            return cut(params, PARAM[name][0], *(shape or (PARAM[name][1] - PARAM[name][0],)))

        ident = cs("ident")
        later, inch16, inch = cs("later"), cs("inch16"), cs("inch")
        blocks = cs("blocks")

        memT = cut(work, 0, DC, S)
        xkT = cut(work, 2048, DC, S)
        xv = cut(work, 4096, NT, D)
        ada_in = [cut(work, 2048 + ADA_ROW * j, DC + 1, ADA_PART) for j in range(2)]
        GL = 6144
        gqT = cut(work, GL, 2, S)
        gk = cut(work, GL + 512, NT, 256)
        gv = cut(work, GL + 1024, NT, 512)
        gr = cut(work, GL + 2048, NT, 512)
        su = cut(work, GL + 3072, NT, 512)
        sv = cut(work, GL + 4096, NT, 512)
        xqT = cut(work, GL, DC, S)
        gg = cut(oT[:, :, :].rearrange("p a b -> p (a b)"), 0, NT, 256)
        gE = cut(oT[:, :, :].rearrange("p a b -> p (a b)"), 512, NT, 256)
        gkd = cut(oT[:, :, :].rearrange("p a b -> p (a b)"), 1024, NCHUNK, 256)
        states = cut(xT[:, :, :].rearrange("p a b -> p (a b)"), 0, NCHUNK, 2, 256)
        LNV = GL + 5120
        lnv = cut(work, LNV, 2, D)
        mixv = cut(work, LNV, 3, 512)
        EX = GL
        esig = cut(work, EX, 2, HID)
        eh = cut(work, EX + 1024, 2, HID)
        ehT = cut(work_parts, EX + 2048, 2, HC, P)
        ehT_lo = cut(work_parts, EX + 3968, 2, HC, P)
        ehT_plain = cut(work, EX + 2048, 2, HC, P)
        xg = [cut(t[:, :, :].rearrange("p a b -> p (a b)"), 0, DC, P) for t in (xT, oT)]
        xg_lo, xg_hi = ([cut(t[:, :, :].rearrange("p a b -> p (a b)"), at, DC, P) for t in (xT_parts, oT_parts)]
                        for at in (0, DC * P))
        pick = cut(work, 5504, NT, P)
        place = [cut(work, 5760, NT * P), cut(work, EX + 3712, NT * P)]
        ada_acc = cut(work, EX + 3072, ADA_COLS)
        gtmp = cut(work, EX + 3456, 256)
        aS = cut(mix[:, :, :].rearrange("p a b -> p (a b)"), 0, 2, 2, S)
        aP2 = cut(mix[:, :, :].rearrange("p a b -> p (a b)"), 1024, 2, 2, S)

        def aP(u):
            i = u["n"] % 3
            if i < 2:
                return aP2[:, i, :, :]
            return cut(work, EX + 3072 if u["name"][1] == "." else 12672, 2, S)

        aPT = cut(work, 13312, 2, 4, P)
        bias = cut(work, 0, 8, NT, S)
        NS = 4096
        nq = cut(work, NS, PAIRS, S)
        nk = [cut(work, NS + 1024 + 512 * j, 2, S) for j in range(2)]
        nv = [cut(work, NS + 2048 + 512 * j, NT, 2, P) for j in range(2)]
        kcz = cut(work, NS + 3072, 2, 16)
        vcz = cut(work, NS + 3104, 2, P)
        MB = NS + 3360
        mq = cut(work, MB, PAIRS, S)
        mk = cut(work, MB + 1024, 8, S)
        mv = cut(work, MB + 3072, NT, 8, P)
        flat = cut(work, MB + 1024, 2, 16, 2 * N_CMP)
        h1T = cut(work, MB + 2048, 2, 2, 2 * N_CMP)
        gate_row = cut(work, MB, D)
        rowbuf = [cut(t[:, :, :].rearrange("p a b -> p (a b)"), 0, 4, UROW) for t in (mix, oT)]
        cq = cut(work, NS, NT, 448)
        cT = cut(work, NS + 896, 3, S)
        kr2 = cut(work, NS + 1664, NT, P)
        rt = cut(work, NS + 1920, 512)
        swq = cut(work, NS, PAIRS, S)
        swk = cut(work, NS + 7552, 2, S)
        swv = cut(work, NS + 8064, NT, 2, P)
        qn = cut(work, NS + 2432, MLA_H, S)
        kn = cut(work, NS + 3456, MLA_H, S)
        lv = cut(work, NS + 4480, NT, 512)
        qrn = cut(work, NS + 5504, NT, 256)
        qro = cut(work, NS + 6016, NT, 256)
        qrT = cut(work, NS + 6528, 2, S)
        krz = cut(work, NS + 7040, 2, S)
        assert NS + 8576 <= 13312 and MB + 5120 <= 13312

        SM, _n = layout([("stat_in", 16), ("stat_out", 16), ("bn", 2 * 12), ("mv", 4), ("nm", 4),
                         ("den", 4), ("modc", 96), ("slot", NT * GATHERS), ("slot_gate", 2 * PER_GROUP), ("sc", 8), ("decay", 8), ("gates", 48),
                         ("modg", 16), ("bnb", 48), ("mvb", 16), ("es", 4), ("mx", 4), ("counts", GROUPS), ("over", 2), ("pads", 2 * NT * 8), ("padmax", 2 * NT * 8), ("sig", 8)])
        assert _n <= 560

        def sm(name, *shape):
            return cut(small, SM[name][0], *(shape or (SM[name][1] - SM[name][0],)))

        stat_in, stat_out = sm("stat_in"), sm("stat_out")
        slot = sm("slot", NT, GATHERS)
        slot_gate = sm("slot_gate", 2, PER_GROUP)
        control = ctx.enter_context(nc.sbuf_tensor("control", [P, 2 * 4], I32))
        gates = sm("gates", NT, 24)
        nm, den = sm("nm", 2, 2), sm("den", 2, 2)
        decay = sm("decay", 2, NCHUNK)
        alow = sb("alow", S)

        pad_w = cut(work, GL + 3072, 2 * NT, 8, 33)

        R, _n = layout([("A", 32), ("B", 32), ("hi", 16), ("lo", 16), ("8a", 8), ("8b", 8), ("8c", 8), ("2a", 2),
                        ("g", 8), ("a", 8), ("b", 8), ("1", 8), ("2", 8), ("tmp", 32)])

        def ro(name, *shape):
            return cut(gtmp, R[name][0], *(shape or (R[name][1] - R[name][0],)))

        rA, rB = ro("A", 2, 16), ro("B", 2, 16)
        r_hi, r_lo, r8a, r8b, r8c = ro("hi", 8, 2), ro("lo", 8, 2), ro("8a"), ro("8b"), ro("8c")
        r2a, r_g, r_a, r_b, r_1, r_2 = ro("2a"), ro("g", 2, 4), ro("a", 2, 4), ro("b", 2, 4), ro("1", 2, 4), ro("2", 2, 4)
        r_tmp = ro("tmp", 2, 4, 4)

        def skewed(first):
            flat_ = scratch[:, :]
            return bass.AP(flat_.tensor, flat_.offset + first, [[UROW, P], [P * (UROW + 1), 8], [1, S]])

        slot_full = [sem(f"slot_full{i}") for i in range(RING)]
        halves_done = sem("halves_done")
        hi_ready, lo_ready = sem("hi_ready"), sem("lo_ready")
        xhi_ready, xlo_ready = sem("xhi_ready"), sem("xlo_ready")
        group_ready = sem("group_ready")
        pick_ready = sem("pick_ready")
        control_ready = sem("control_ready")
        ov_loaded = [sem("ov_loaded0"), sem("ov_loaded1")]
        ov_pe, ov_act, ov_dve = sem("ov_pe"), sem("ov_act"), sem("ov_dve")
        hid_hi = sem("hid_hi")
        banks = Banks([sem(f"bank_full{i}") for i in range(NBANK)],
                      [sem(f"bank_drained{i}") for i in range(NBANK)])
        setup_loaded = sem("setup_loaded")
        xT_loaded, mem_loaded = sem("xT_loaded"), sem("mem_loaded")
        vecs_loaded = sem("vecs_loaded")
        vecs_used = sem("vecs_used")
        var_ready = sem("var_ready")
        rstd_ready = sem("rstd_ready")
        dve_steps, act_steps, pool_steps = sem("dve_steps"), sem("act_steps"), sem("pool_steps")
        att_max, att_exp, att_prob = sem("att_max"), sem("att_exp"), sem("att_prob")
        ada_loaded = [sem("ada_loaded0"), sem("ada_loaded1")]
        ada_summed = sem("ada_summed")
        x_half = sem("x_half")
        x_ready = sem("x_ready")
        gla_abs, gla_log, gla_g, gla_kd = sem("gla_abs"), sem("gla_log"), sem("gla_g"), sem("gla_kd")
        gla_state = sem("gla_state")
        sgu_ready = sem("sgu_ready")
        ws_masked = sem("ws_masked")
        silu_c = sem("silu_c")
        router_in, router_exp = sem("router_in"), sem("router_exp")
        ones_set = sem("ones_set")
        pads_in, pads_fn = sem("pads_in"), sem("pads_fn")
        rows_out, bias_back = sem("rows_out"), sem("bias_back")
        bias_ready = sem("bias_ready")
        zeros_set = sem("zeros_set")
        lat_ready = sem("lat_ready")
        rope_ready = sem("rope_ready")
        out_ready, out_stored = sem("out_ready"), sem("out_stored")

        OUTS = [(T, n) for n in range(2) for T in range(NT)]

        def cross_units(tag):
            out = []
            for hp in range(2):
                for T in range(NT):
                    t = slice(T * P, (T + 1) * P)
                    out.append(dict(
                        name=f"{tag}.{hp}.{T}", nk=S, tiles=2, kp=P, bias=None, sink=None, gate=None,
                        scores=[[(xqT[:, 4 * hp + 2 * a + j, t], xkT[:, 4 * hp + 2 * a + j, :])
                                 for j in range(2)] for a in range(2)],
                        pv=[(2 * a + j, a, kt, xv[:, kt, (4 * hp + 2 * a + j) * P:(4 * hp + 2 * a + j + 1) * P])
                            for a in range(2) for j in range(2) for kt in range(2)],
                        first=True, last=True, o=f"{tag}.o.{hp}.{T}", regions=4,
                        dest=oT[:, 4 * hp:4 * hp + 4, t]))
            return out

        def pair_units(tag, q, branches, chunk0):
            out = []
            for i in range(PAIRS):
                for T in range(NT):
                    t = slice(T * P, (T + 1) * P)
                    for b, (kf, vf, n, g, biases, sink) in enumerate(branches):
                        nk_ = n or (T + 1) * P
                        tiles = 1 if n else T + 1
                        out.append(dict(
                            name=f"{tag}.{i}.{T}.{b}", nk=nk_, tiles=tiles, kp=min(nk_, P),
                            bias=biases(i, T), sink=sink and sink(i, T),
                            gate=None if g is None else g(i, T),
                            scores=[[(q[:, i, t], kf(i, a)[:, 0:nk_])] for a in range(2)],
                            pv=[(0, a, kt, vf(i, a, kt)) for a in range(2) for kt in range(tiles)],
                            first=b == 0, last=b == len(branches) - 1, o=f"{tag}.o.{i}.{T}",
                            regions=1, dest=oT[:, chunk0 + i:chunk0 + i + 1, t]))
            return out

        def causal_bias(i, T):
            return [bias[:, i + 4 * a, T, 0:(T + 1) * P] for a in range(2)]

        def cmp_bias(i, T):
            return [bias[:, i + 4 * a, T, CMP_L - 1:S:16] for a in range(2)]

        def nsa_gate(b):
            return lambda i, T: gates[:, T, :].rearrange("p (a i b) -> p a i b", a=2, b=3)[:, :, i, b]

        def before(k):
            return lambda i, T: sm("pads", 2 * NT, 2, 4)[:, NT * k + T, :, i]

        def nsa_units():
            return pair_units("nsa", nq, [
                (lambda i, a: kcz[:, a, :], lambda i, a, kt: vcz[0:N_CMP, a, :], N_CMP, nsa_gate(0), cmp_bias, None),
                (lambda i, a: nk[0][:, a, :], lambda i, a, kt: nv[0][:, kt, a, :], None, nsa_gate(1), causal_bias, None),
                (lambda i, a: nk[1][:, a, :], lambda i, a, kt: nv[1][:, kt, a, :], None, nsa_gate(2), causal_bias,
                 before(0)),
            ], 0)

        def moba_units():
            return pair_units("moba", mq, [
                (lambda i, a: mk[:, i + 4 * a, :], lambda i, a, kt: mv[:, kt, i + 4 * a, :], None, None, causal_bias,
                 None),
            ], 4)

        def swa_units():
            return pair_units("swa", swq, [
                (lambda i, a: swk[:, a, :], lambda i, a, kt: swv[:, kt, a, :], None, None, causal_bias,
                 before(1)),
            ], 4)

        def mla_units():
            out = []
            for i in range(2):
                for T in range(NT):
                    t = slice(T * P, (T + 1) * P)
                    n = (T + 1) * P
                    out.append(dict(
                        name=f"mla.{i}.{T}", nk=n, tiles=T + 1, kp=P, sink=None, gate=None,
                        bias=[cs("causal", NT, S)[:, T, 0:n]] * 2,
                        scores=[[(qn[:, 2 * i + a, t], kn[:, 2 * i + a, 0:n]),
                                 (qrT[:, i, t], krz[:, a, 0:n])] for a in range(2)],
                        pv=[(a, a, kt, lv[:, kt, (2 * i + a) * P:(2 * i + a + 1) * P])
                            for a in range(2) for kt in range(T + 1)],
                        first=True, last=True, o=f"mla.o.{i}.{T}", regions=2,
                        dest=oT[:, 2 * i:2 * i + 2, t]))
            return out

        def numbered(units, first):
            for k, u in enumerate(units):
                u["n"] = first + k
            return units

        ATT = {"0.x": 0, "1.x": 4, "nsa": 8, "moba": 32, "mla": 40, "swa": 44}

        POS = {(w, e): j for j, (w, e) in enumerate(GROUP_ORDER)}

        def place_of(what, k):
            return len(GROUP_ORDER) * (k // PER_GROUP) + POS[what, k % PER_GROUP]

        def scatter_names(tag, g):
            return [(T, n, f"{tag}.sc{g}.{T}.{n}") for T in range(NT) for n in range(2)]

        def moe_jobs(tag, with_ada):
            out = []
            for g in range(GROUPS_PER_BODY):
                for e in range(PER_GROUP):
                    k = PER_GROUP * g + e
                    if e == 0:
                        out.append(f"{tag}.g{k}")
                        if g:
                            out += [name for _, _, name in scatter_names(tag, g - 1)]
                        out.append(f"{tag}.u{k}")
                    out.append(f"{tag}.g{k + 1}" if e < PER_GROUP - 1 else f"{tag}.xg{g + 1}.1")
                    out += [f"{tag}.hT{k}", f"{tag}.y{k}.0", f"{tag}.y{k}.1"]
                    if with_ada:
                        out.append(f"{tag}.ada{k}")
                    if e == 0:
                        out += [f"{tag}.at{g + 1}", f"{tag}.sg{g + 1}", f"{tag}.xg{g + 1}.0"]
                    if e < PER_GROUP - 1:
                        out.append(f"{tag}.u{k + 1}")
            return out + [name for _, _, name in scatter_names(tag, GROUPS_PER_BODY - 1)]

        class Half:

            def __init__(self, tag, j, h):
                m = MOE_FIRST[tag[0]] + j
                self.slot, self.full = m % RING, 16 * (m // RING + 1)
                self.free = 2 * m + h - HI_RING + 1
                self.n = 2 * NMOE * MOE_LAYER[tag[0]] + 2 * j + h + 1
                self.raw = ring[:, self.slot, h * HALF:(h + 1) * HALF]
                self.hi = hi_ring[:, (self.n - 1) % HI_RING, :]
                self.lo = ring_parts[:, self.slot, h * HALF:(h + 1) * HALF]

        def yacc(tag):
            return cut(work, 13312 if tag[0] in "01" else 4096, D)

        def ysum(tag):
            return mix[:, :, :] if tag[0] in "01" else cut(work, 12288, NT, D)

        OV_PE, OV_ACT, OV_DVE = 4 * PER_GROUP + 1, 2 * PER_GROUP, 1 + 2 * PER_GROUP + 1
        OV_LOADS = 16 * 3 * PER_GROUP // 2
        flat_hi = hi_plain[:, :, :].rearrange("p a b -> p (a b)")
        ov_w = [flat_hi[:, j * PIECE:(j + 1) * PIECE] for j in range(2)]
        PER_BODY = 3 * EXP_PER_BODY
        assert PER_BODY % RING == 0 and 2 * PER_BODY % HI_RING == 0

        block = ctx.enter_context(nc.Block())

        @block.tensor
        def _(pe):
            taken = [0]
            release = [0]
            owed = [0]

            def piece():
                m = taken[0]
                taken[0] += 1
                n = 16 * (m // RING + 1)
                pe.wait_ge(slot_full[m % RING], n)
                release[0] += owed[0]
                owed[0] = 2
                return ring[:, m % RING, :]

            def mm(o, lhsT, rhs, start, stop):
                ins = nc.tensor.matmul(o, lhsT, rhs, start=start, stop=stop)
                if release[0] and not stop:
                    ins.then_inc(halves_done, release[0])
                    release[0] = 0
                return ins

            def begin(name, it=None):
                if it is None:
                    banks.add(name)
                banks.wait_free(pe, name, it)
                return psum[banks.jobs[name][0]]

            def end(name, ins):
                ins.then_inc(banks.full[banks.jobs[name][0]], 1)

            def ready(name, it=None):
                banks.wait_drained(pe, name, it)

            def product(name, parts, it=None):
                bank = begin(name, it)
                for c0, c1, rows, pairs in parts:
                    for k, (a, b) in enumerate(pairs):
                        ins = mm(bank[0:rows, c0:c1], a, b, k == 0, k == len(pairs) - 1)
                end(name, ins)

            def transposes(name, pairs, it=None):
                bank = begin(name, it)
                for c0, c1, rows, src in pairs:
                    k = src.shape[0]
                    ins = nc.tensor.transpose(bank[0:rows, c0:c1], src, ident[0:k, 0:k])
                end(name, ins)

            def columns(w, n=512):
                return w[:, 0:DC * n].rearrange("p (c n) -> p c n", c=DC)

            def natural(name, T, rhs, src=xT, n=512, at=0):
                product(name, [(at, at + n, P, [(src[:, c, T * P:(T + 1) * P], rhs(c)) for c in range(DC)])])

            def transposed(name, cols, src=xT):
                product(name, [(k * S, (k + 1) * S, f(0).shape[-1] if len(f(0).shape) == 2 else P,
                                [(f(c), src[:, c, :]) for c in range(DC)]) for k, f in enumerate(cols)])

            def turn(tag, src, norm=None):
                for q in range(DC // 2):
                    if norm and q in (0, DC // 4):
                        pe.wait_ge(x_ready if q else x_half, norm)
                    transposes(f"{tag}.{q}", [(j * S + T * P, j * S + (T + 1) * P, P,
                                               src[:, T, (2 * q + j) * P:(2 * q + j + 1) * P])
                                              for j in range(2) for T in range(NT)])

            def project_out(tag):
                for q in range(2):
                    w = columns(piece())
                    for T in range(NT):
                        natural(f"{tag}.{T}.{q}", T, lambda c: w[:, c, :], src=oT)

            def attention(units):
                n = len(units)
                for k in range(n + 3):
                    if k < n:
                        u = units[k]
                        product(u["name"] + ".s", [(a * S, a * S + u["nk"], P, u["scores"][a]) for a in range(2)])
                    if 2 <= k <= n + 1:
                        u = units[k - 2]
                        pe.wait_ge(att_prob, u["n"] + 1)
                        src = aP(u)
                        transposes(u["name"] + ".t", [
                            ((2 * a + kt) * P, (2 * a + kt + 1) * P, u["kp"], src[:, a, kt * P:kt * P + u["kp"]])
                            for a in range(2) for kt in range(u["tiles"])])
                    if k >= 3:
                        u = units[k - 3]
                        if u["first"]:
                            begin(u["o"])
                        bank = psum[banks.jobs[u["o"]][0]]
                        ready(u["name"] + ".t")
                        src = aPT[:, u["n"] % 2, :, :]
                        for j, (r, a, kt, v) in enumerate(u["pv"]):
                            fresh = u["first"] and (j == 0 or u["pv"][j - 1][0] != r)
                            done = u["last"] and (j == len(u["pv"]) - 1 or u["pv"][j + 1][0] != r)
                            ins = mm(bank[:, r * P:(r + 1) * P], v, src[0:u["kp"], 2 * a + kt, :], fresh, done)
                        if u["last"]:
                            end(u["o"], ins)

            def experts(tag, with_ada, src):
                layer = MOE_LAYER[tag[0]]
                pe.wait_ge(group_ready, layer + 1)
                product(f"{tag}.rank", [
                    (0, 4, P, [(cs("before"), r_g[:, 0, :])]),
                    (4, 8, P, [(cs("ones")[:, 0:1].broadcast_to([P, P]), r_g[:, 0, :]), (cs("before"), r_g[:, 1, :])]),
                    (8, 12, P, [(cs("ones")[:, 0:1].broadcast_to([P, P]), r_g[:, T, :]) for T in range(NT)])])

                def gather_a(n, it=None):
                    count = GATHERS * layer + n + 1
                    pe.wait_ge(pick_ready, count if it is None else it * GROUPS_PER_BODY + count)
                    transposes(f"{tag}.at{n}", [(T * P, (T + 1) * P, P, pick[:, T, :]) for T in range(NT)], it)
                    product(f"{tag}.sg{n}", [(0, PER_GROUP, P, [(pick[:, T, :], r_a[:, T, :]) for T in range(NT)])], it)
                    gather_b(n, 0, it)

                def gather_b(n, half=1, it=None):
                    product(f"{tag}.xg{n}.{half}", [
                        (j * P, (j + 1) * P, P, [(src[:, T, (4 * half + j) * P:(4 * half + j + 1) * P], pick[:, T, :])
                                                 for T in range(NT)]) for j in range(4)], it)

                release[0] += 1
                gather_a(0)
                gather_b(0)
                banks.add_loop(moe_jobs(tag, with_ada), BODIES)
                with pe.Fori(0, BODIES) as it:
                    def split(j, h):
                        part = Half(tag, j, h)
                        pe.wait_ge(lo_ready, it * (2 * PER_BODY) + part.n)
                        return part.hi, part.lo

                    def three(o, a_hi, a_lo, b_hi, b_lo, start, stop):
                        mm(o, a_hi, b_hi, start, False)
                        mm(o, a_hi, b_lo, False, False)
                        return mm(o, a_lo, b_hi, False, stop)

                    def gate_up(what, k, halves=(0, 1)):
                        b = k // PER_GROUP % 2
                        name = f"{tag}.{what}{k}"
                        o = (begin(name, it) if halves[0] == 0 else psum[banks.jobs[name][0]])[:, :]
                        for h in halves:
                            hi, lo = (t.rearrange("p (c n) -> p c n", c=DC // 2) for t in split(place_of(what, k), h))
                            release[0] += 1
                            for c in range(DC // 2):
                                t = (slice(None), DC // 2 * h + c, slice(None))
                                ins = three(o, xg_hi[b][t], xg_lo[b][t], hi[:, c, :], lo[:, c, :],
                                            h == 0 and c == 0, h == 1 and c == DC // 2 - 1)
                        if halves[-1] == 1:
                            end(name, ins)

                    def turn_hidden(k):
                        ready(f"{tag}.u{k}", it)
                        transposes(f"{tag}.hT{k}", [(j * P, (j + 1) * P, P, eh[:, k % 2, j * P:(j + 1) * P])
                                                    for j in range(HC)], it)

                    def down(k):
                        ready(f"{tag}.hT{k}", it)
                        o = [begin(f"{tag}.y{k}.{n}", it)[:, :] for n in range(2)]
                        for h in range(2):
                            hi, lo = (t.rearrange("p (c n) -> p c n", c=HC // 2) for t in split(place_of("d", k), h))
                            release[0] += 1
                            for c in range(HC // 2):
                                t = (slice(None), k % 2, HC // 2 * h + c, slice(None))
                                for n in range(2):
                                    w = (slice(None), c, slice(n * 512, (n + 1) * 512))
                                    ins = three(o[n], ehT[t], ehT_lo[t], hi[w], lo[w],
                                                h == 0 and c == 0, h == 1 and c == HC // 2 - 1)
                                    if h == 1 and c == HC // 2 - 1:
                                        end(f"{tag}.y{k}.{n}", ins)

                    def scatter(g):
                        for n in range(2):
                            ready(f"{tag}.y{PER_GROUP * g + PER_GROUP - 1}.{n}", it)
                        for T, n, name in scatter_names(tag, g):
                            product(name, [(0, 512, P, [(place[g][:, T * P:(T + 1) * P], yacc(tag)[:, n * 512:(n + 1) * 512])])],
                                    it)

                    for g in range(GROUPS_PER_BODY):
                        for e in range(PER_GROUP):
                            k = PER_GROUP * g + e
                            if e == 0:
                                pe.wait_ge(xlo_ready, it * GROUPS_PER_BODY + (GATHERS * layer + g + 1))
                                gate_up("g", k)
                                if g:
                                    scatter(g - 1)
                                gate_up("u", k)
                            if e < PER_GROUP - 1:
                                gate_up("g", k + 1, (0,))
                                turn_hidden(k)
                                gate_up("g", k + 1, (1,))
                            else:
                                gather_b(g + 1, 1, it)
                                turn_hidden(k)
                            down(k)
                            if with_ada:
                                pe.wait_ge(ada_summed, it * (2 * EXP_PER_BODY) + 2 * (NEXP * with_ada[0] + k + 1))
                                product(f"{tag}.ada{k}", [(j, j + 1, P, [(ada_acc[:, j * P:(j + 1) * P], cs("ones")[:, 0:1])])
                                                          for j in range(ADA_COLS // P)], it)
                            if e == 0:
                                gather_a(g + 1, it)
                            if e < PER_GROUP - 1:
                                gate_up("u", k + 1)
                    scatter(GROUPS_PER_BODY - 1)
                assert release[0] == 0
                owed[0] = 1
                taken[0] += NMOE

                pe.wait_ge(control_ready, layer + 1)
                over = pe.value_load(control[0:1, 2 * layer:2 * layer + 1], min_val=0, max_val=GROUPS)
                with pe.If(over > 0):
                    pe.wait_ge(ov_dve, OV_DVE * layer + 1)
                    pieces = [0]

                    def weights_of(chunks_):
                        i = pieces[0]
                        pieces[0] += 1
                        pe.wait_ge(ov_loaded[i % 2], OV_LOADS * layer + 16 * (i // 2 + 1))
                        return ov_w[i % 2].rearrange("p (c n) -> p c n", c=chunks_)

                    for e in range(PER_GROUP):
                        if e:
                            pe.wait_ge(ov_dve, OV_DVE * layer + 1 + 2 * e)
                        for j in range(2):
                            w = weights_of(DC)
                            for c in range(DC):
                                ins = nc.tensor.matmul(psum[j][:, :], xg[0][:, c, :], w[:, c, :],
                                                       start=c == 0, stop=c == DC - 1)
                            ins.then_inc(ov_pe, 1)
                        pe.wait_ge(ov_dve, OV_DVE * layer + 2 + 2 * e)
                        for j in range(HC):
                            ins = nc.tensor.transpose(psum[2][:, j * P:(j + 1) * P], eh[:, 0, j * P:(j + 1) * P], ident)
                        ins.then_inc(ov_pe, 1)
                        pe.wait_ge(ov_act, OV_ACT * layer + 2 + 2 * e)
                        w = weights_of(HC)
                        for n in range(2):
                            for j in range(HC):
                                ins = nc.tensor.matmul(psum[3 + n][:, :], ehT_plain[:, 0, j, :],
                                                       w[:, j, n * 512:(n + 1) * 512], start=j == 0, stop=j == HC - 1)
                        ins.then_inc(ov_pe, 1)
                    pe.wait_ge(ov_dve, OV_DVE * layer + 1 + 2 * PER_GROUP)
                    for b, (T, n) in zip((5, 6, 7, 0), OUTS):
                        ins = nc.tensor.matmul(psum[b][:, :], place[0][:, T * P:(T + 1) * P],
                                               yacc(tag)[:, n * 512:(n + 1) * 512], start=True, stop=True)
                    ins.then_inc(ov_pe, 1)
                with pe.Else():
                    pe.sem_inc(ov_pe, OV_PE)
                pe.wait_ge(ov_dve, OV_DVE * (layer + 1))

            pe.wait_ge(setup_loaded, 32)
            for h in range(8):
                product(f"row.{h}", [(0, UROW, P, [(pr("rel_table")[0:33, h:h + 1].broadcast_to([33, P]), cs("onehot")[0:33, :])])])

            def first_layer(l):
                if l == 0:
                    pe.wait_ge(xT_loaded, 16)
                else:
                    for q in range(DC // 2):
                        ready(f"{l - 1}.turn3.{q}")
                tg = f"{l}"
                w = columns(piece())
                transposed(f"{tg}.q", [lambda c, m=m: w[:, c, m * P:(m + 1) * P] for m in range(2)])
                product(f"{tg}.k", [(T * 256, (T + 1) * 256, P, [(xT[:, c, T * P:(T + 1) * P], w[:, c, 256:512])
                                                               for c in range(DC)]) for T in range(NT)])
                wl = pr("w_alow", 2, DC * 16)[:, l, :].rearrange("p (c n) -> p c n", c=DC)
                product(f"{tg}.alow", [(0, S, GATE_RANK, [(wl[:, c, :], xT[:, c, :]) for c in range(DC)])])
                w = columns(piece())
                for T in range(NT):
                    natural(f"{tg}.v.{T}", T, lambda c: w[:, c, :])
                ready(f"{tg}.alow")
                wa = pr("w_a2", 2, 256)[0:GATE_RANK + 1, l, :]
                product(f"{tg}.z", [(T * 256, (T + 1) * 256, P, [(alow[0:GATE_RANK + 1, T * P:(T + 1) * P], wa)])
                                    for T in range(NT)])
                for n in ("r", "u", "sv"):
                    w = columns(piece())
                    for T in range(NT):
                        natural(f"{tg}.{n}.{T}", T, lambda c: w[:, c, :])
                pe.wait_ge(gla_g, l + 1)
                product(f"{tg}.rem", [(T * 256, (T + 1) * 256, P, [(later, gg[:, T, :])]) for T in range(NT)])
                product(f"{tg}.dec", [(m * 4 + 2 * T, m * 4 + 2 * T + 2, P,
                                       [(gg[:, T, m * P:(m + 1) * P], inch16)])
                                      for m in range(2) for T in range(NT)])
                if l == 0:
                    pe.wait_ge(mem_loaded, 32)
                for q in range(2):
                    w = columns(piece())
                    for j in range(2):
                        transposed(f"{tg}.xk.{2 * q + j}",
                                   [lambda c, m=m: w[:, c, m * P:(m + 1) * P] for m in (2 * j, 2 * j + 1)], src=memT)
                pe.wait_ge(gla_kd, l + 1)
                for T in range(NT):
                    ready(f"{tg}.v.{T}")
                for c in range(NCHUNK):
                    T = c // 2
                    product(f"{tg}.kv.{c}", [(m * 256, (m + 1) * 256, P,
                                              [(gkd[:, c, m * P:(m + 1) * P], gv[:, T, m * 256:(m + 1) * 256])])
                                             for m in range(2)])
                for q in range(2):
                    w = columns(piece())
                    for T in range(NT):
                        natural(f"{tg}.xv.{T}.{q}", T, lambda c: w[:, c, :], src=memT)
                ready(f"{tg}.q")
                for c in range(NCHUNK):
                    T = c // 2
                    pe.wait_ge(gla_state, NCHUNK * l + c + 1)
                    product(f"{tg}.o.{c}", [(m * 256, (m + 1) * 256, P,
                                             [(gqT[:, m, T * P:(T + 1) * P], states[:, c, m, :])]) for m in range(2)])
                pe.wait_ge(sgu_ready, l + 1)
                pe.wait_ge(ws_masked, 2)
                ws = pr("w_s", 2, 4, P)
                for T in range(NT):
                    product(f"{tg}.mix.{T}", [(g * P, (g + 1) * P, P, [(ws[:, l, g, :], sv[:, T, g * P:(g + 1) * P])])
                                              for g in range(SGU_GROUPS)])
                for T in range(NT):
                    ready(f"{tg}.mix.{T}")
                turn(f"{tg}.turn0", mix)
                for q in range(DC // 2):
                    ready(f"{tg}.turn0.{q}")
                project_out(f"{tg}.out")
                turn(f"{tg}.turn1", x, 3 * l + 1)
                for q in range(DC // 2):
                    ready(f"{tg}.turn1.{q}")
                for q in range(2):
                    w = columns(piece())
                    for j in range(2):
                        transposed(f"{tg}.xq.{2 * q + j}",
                                   [lambda c, m=m: w[:, c, m * P:(m + 1) * P] for m in (2 * j, 2 * j + 1)])
                for q in range(4):
                    ready(f"{tg}.xq.{q}")
                    ready(f"{tg}.xk.{q}")
                for q in range(2):
                    for T in range(NT):
                        ready(f"{tg}.xv.{T}.{q}")
                us = numbered(cross_units(f"{tg}.x"), ATT[f"{tg}.x"])
                attention(us)
                for u in us:
                    ready(u["o"])
                project_out(f"{tg}.xo")
                turn(f"{tg}.turn2", x, 3 * l + 2)
                for q in range(DC // 2):
                    ready(f"{tg}.turn2.{q}")
                route(f"{tg}.logits", "w_router")
                experts(f"{tg}.moe", (l,), x)
                if l == 0:
                    turn(f"{tg}.turn3", x, 3)

            def route(name, weights):
                wr = pr(weights, DC, 16)
                product(name, [(T * 16, (T + 1) * 16, P, [(xT[:, c, T * P:(T + 1) * P], wr[:, c, :])
                                                         for c in range(DC)]) for T in range(NT)])

            def gate_rows(tag, cols):
                for q in range(2):
                    product(f"{tag}.{q}", [(j * P, (j + 1) * P, P,
                                            [(cols[:, 4 * q + j:4 * q + j + 1].broadcast_to([P, P]), ident)])
                                           for j in range(4)])

            first_layer(0)
            first_layer(1)

            def normed(tag, n):
                pe.wait_ge(x_ready, n)
                turn(tag, mix)
                for q in range(DC // 2):
                    ready(f"{tag}.{q}")

            normed("e.turn0", 6)
            w = columns(piece())
            for j in range(2):
                transposed(f"e.q.{j}", [lambda c, i=i: w[:, c, i * P:(i + 1) * P] for i in (2 * j, 2 * j + 1)])
            w = columns(piece())
            transposed("e.c", [lambda c, i=i: w[:, c, i * P:(i + 1) * P] for i in range(2)])
            transposed("e.ks", [lambda c: w[:, c, 256:384]])
            product("e.vs", [(T * P, (T + 1) * P, P, [(xT[:, c, T * P:(T + 1) * P], w[:, c, 384:512])
                                                     for c in range(DC)]) for T in range(NT)])
            w = columns(piece())
            transposed("e.kw", [lambda c: w[:, c, 0:P]])
            product("e.vw", [(T * P, (T + 1) * P, P, [(xT[:, c, T * P:(T + 1) * P], w[:, c, P:2 * P])
                                                     for c in range(DC)]) for T in range(NT)])
            wg = pr("w_gates", DC, 24)
            product("e.gates", [(T * 24, (T + 1) * 24, P, [(xT[:, c, T * P:(T + 1) * P], wg[:, c, :])
                                                          for c in range(DC)]) for T in range(NT)])
            ready("e.c")
            for j, n in enumerate("kv"):
                w1 = piece().rearrange("p (c n) -> p c n", c=16)
                product(f"e.h1{n}", [(m * 2 * N_CMP, (m + 1) * 2 * N_CMP, P,
                                      [(w1[:, c, m * P:(m + 1) * P], flat[:, j, c, :]) for c in range(16)])
                                     for m in range(2)])
            ready("e.h1k")
            wk2 = pr("ck_w2", 2, DH)
            product("e.kc", [(0, 2 * N_CMP, DH, [(wk2[:, m, :], h1T[:, 0, m, :]) for m in range(2)])])
            ready("e.h1v")
            wv2 = pr("cv_w2", 2, DH)
            product("e.vc", [(a * DH, (a + 1) * DH, N_CMP,
                              [(h1T[:, 1, m, a * N_CMP:(a + 1) * N_CMP], wv2[:, m, :]) for m in range(2)])
                             for a in range(2)])
            for n in ("e.q.0", "e.q.1", "e.ks", "e.kw", "e.vs", "e.vw", "e.kc", "e.vc"):
                ready(n)
            attention(numbered(nsa_units(), ATT["nsa"]))
            w = columns(piece())
            for j in range(2):
                transposed(f"e.mq.{j}", [lambda c, i=i: w[:, c, i * P:(i + 1) * P] for i in (2 * j, 2 * j + 1)])
            w = columns(piece())
            for j in range(2):
                transposed(f"e.mk.{j}", [lambda c, i=i: w[:, c, i * P:(i + 1) * P] for i in (2 * j, 2 * j + 1)])
            w = columns(piece())
            for T in range(NT):
                natural(f"e.mv.{T}", T, lambda c: w[:, c, :])
            for n in ("e.mq.0", "e.mq.1", "e.mk.0", "e.mk.1", "e.mv.0", "e.mv.1"):
                ready(n)
            attention(numbered(moba_units(), ATT["moba"]))
            for i in range(PAIRS):
                for T in range(NT):
                    ready(f"nsa.o.{i}.{T}")
                    ready(f"moba.o.{i}.{T}")
            gate_rows("e.gm", sm("modc", 2, 48)[:, 0, 16:24])
            project_out("e.out")
            normed("e.turn1", 7)
            route("e.logits", "router_w_2")
            experts("e.moe", None, mix)
            gate_rows("e.gf", sm("modc", 2, 48)[:, 0, 40:48])

            normed("o.turn0", 8)
            w = columns(piece())
            for T in range(NT):
                natural(f"o.c.{T}", T, lambda c: w[:, c, 0:448], n=448)
            pe.wait_ge(lat_ready, 1)
            transposes("o.cqT", [(j * S + T * P, j * S + (T + 1) * P, P, cq[:, T, j * P:(j + 1) * P])
                                 for j in range(2) for T in range(NT)])
            transposes("o.ckvT", [(T * P, (T + 1) * P, P, cq[:, T, 2 * P:3 * P]) for T in range(NT)])
            w = piece()
            wq = w[:, 0:1536].rearrange("p (c n) -> p c n", c=2)
            wkv = w[:, 1536:2560]
            ready("o.cqT")
            ready("o.ckvT")
            for j in range(2):
                product(f"o.qn.{j}", [(a * S, (a + 1) * S, P,
                                       [(wq[:, c, (2 * j + a) * 192:(2 * j + a) * 192 + P], cT[:, c, :]) for c in range(2)])
                                      for a in range(2)])
                product(f"o.kn.{j}", [(a * S, (a + 1) * S, P, [(wkv[:, (2 * j + a) * 256:(2 * j + a) * 256 + P], cT[:, 2, :])])
                                      for a in range(2)])
            wqr = wq.rearrange("p c (h n) -> p c h n", h=MLA_H)
            wv_ = wkv.rearrange("p (h n) -> p h n", h=MLA_H)
            product("o.qr", [(T * 256, (T + 1) * 256, P, [(cT[:, c, T * P:(T + 1) * P], wqr[:, c, :, P:192]) for c in range(2)])
                             for T in range(NT)])
            for T in range(NT):
                product(f"o.v.{T}", [(0, 512, P, [(cT[:, 2, T * P:(T + 1) * P], wv_[:, :, P:256])])])
            pe.wait_ge(rope_ready, 1)
            transposes("o.krT", [(T * P, (T + 1) * P, P, kr2[:, T, :]) for T in range(NT)])
            pe.wait_ge(rope_ready, 2)
            transposes("o.qrT", [(i * S + T * P, i * S + (T + 1) * P, P, qro[:, T, i * P:(i + 1) * P])
                                 for i in range(2) for T in range(NT)])
            for n in ("o.qn.0", "o.qn.1", "o.kn.0", "o.kn.1", "o.v.0", "o.v.1", "o.krT", "o.qrT"):
                ready(n)
            attention(numbered(mla_units(), ATT["mla"]))
            w = columns(piece())
            for j in range(2):
                transposed(f"o.sq.{j}", [lambda c, i=i: w[:, c, i * P:(i + 1) * P] for i in (2 * j, 2 * j + 1)])
            w = columns(piece())
            transposed("o.sk", [lambda c: w[:, c, 0:P]])
            product("o.sv", [(T * P, (T + 1) * P, P, [(xT[:, c, T * P:(T + 1) * P], w[:, c, P:2 * P])
                                                     for c in range(DC)]) for T in range(NT)])
            for n in ("o.sq.0", "o.sq.1", "o.sk", "o.sv"):
                ready(n)
            attention(numbered(swa_units(), ATT["swa"]))
            for i in range(PAIRS):
                for T in range(NT):
                    ready(f"swa.o.{i}.{T}")
            for i in range(2):
                for T in range(NT):
                    ready(f"mla.o.{i}.{T}")
            gate_rows("o.gm", sm("modc", 2, 48)[:, 1, 16:24])
            project_out("o.out")
            normed("o.turn1", 9)
            route("o.logits", "router_w_2")
            experts("o.moe", None, mix)
            gate_rows("o.gf", sm("modc", 2, 48)[:, 1, 40:48])
            assert taken[0] == NPIECES, taken[0]

        @block.scalar
        def _(act):
            step = Steps(act, act_steps)

            def fn(o, i, f, **kw):
                return nc.scalar.activation(o, i, f, **kw)

            def carry(name, ops, f=ACT.Identity, it=None, **kw):
                banks.wait_full(act, name, it)
                b = banks.jobs[name][0]
                for k, (o, c) in enumerate(ops):
                    ins = fn(o, c(psum[b]), f, **kw)
                    if k < len(ops) - 1:
                        step(ins)
                ins.then_inc(banks.drained[b], 1)

            def whole(o, name, f=ACT.Identity, it=None, **kw):
                a, b = o.shape[1:] if len(o.shape) == 3 else (1, o.shape[1])
                n = a * b
                view = (lambda t: t[:, 0:n].rearrange("p (a b) -> p a b", a=a)) if len(o.shape) == 3 \
                    else (lambda t: t[0:o.shape[0], 0:n])
                carry(name, [(o, view)], f, it, **kw)

            def turned(tag):
                for q in (0, 2):
                    whole(xT[:, 2 * q:2 * q + 2, :], f"{tag}.{q}")

            def modulated(tag, layer, shift):
                for q in (0, 2):
                    banks.wait_full(act, f"{tag}.{q}")
                    b = banks.jobs[f"{tag}.{q}"][0]
                    for j in range(2):
                        c = 2 * q + j
                        ins = fn(xT[:, c, :], psum[b][:, j * S:(j + 1) * S], ACT.Identity,
                                 scale=sm("modg")[:, c:c + 1],
                                 bias=sm("modc", 2, 48)[:, layer, shift + c:shift + c + 1])
                        if j == 0:
                            step(ins)
                    ins.then_inc(banks.drained[b], 1)

            def attention(units):
                def exps(u):
                    act.wait_ge(att_max, u["n"] + 1)
                    i = u["n"] % 2
                    b = banks.jobs[u["name"] + ".s"][0]
                    for a in range(2):
                        src = psum[b][:, a * S:a * S + u["nk"]] if u["bias"] is None else aS[:, i, a, 0:u["nk"]]
                        ins = fn(aP(u)[:, a, 0:u["nk"]], src, ACT.Exp, bias=nm[:, i, a:a + 1],
                                 accum_out=den[:, i, a:a + 1])
                        if a == 0 or u["sink"] is not None:
                            step(ins)
                    if u["sink"] is not None:
                        es = sm("es", 2, 2)[:, i, :]
                        ins = fn(es, es, ACT.Exp)
                    if u["bias"] is None:
                        ins.then_inc(banks.drained[b], 1)
                    else:
                        ins.then_inc(att_exp, 1)

                def turned_probs(u):
                    o, kp = aPT[:, u["n"] % 2, :, :], u["kp"]
                    if u["tiles"] == 2:
                        carry(u["name"] + ".t", [(o[0:kp], lambda t: t[0:kp, :].rearrange("p (a b) -> p a b", a=4))])
                    else:
                        carry(u["name"] + ".t", [(o[0:kp, 0:4:2, :],
                                                  lambda t: t[0:kp, :].rearrange("p (a b) -> p a b", a=4)[:, 0:4:2, :])])

                for k in range(len(units) + 2):
                    if k < len(units):
                        exps(units[k])
                    if k >= 2:
                        turned_probs(units[k - 2])

            def experts(tag, mod=None):
                layer = MOE_LAYER[tag[0]]

                def gather(n, half, it=None):
                    name = f"{tag}.xg{n}.{half}"
                    banks.wait_full(act, name, it)
                    b = banks.jobs[name][0]
                    if mod is None:
                        ins = fn(xg[n % 2][:, 4 * half:4 * half + 4, :], psum[b][:, :].rearrange("p (c n) -> p c n", c=4),
                                 ACT.Identity)
                    else:
                        for j in range(4):
                            c = 4 * half + j
                            ins = fn(xg[n % 2][:, c, :], psum[b][:, j * P:(j + 1) * P], ACT.Identity,
                                     scale=sm("modg")[:, c:c + 1], bias=sm("modc", 2, 48)[:, mod, 24 + c:25 + c])
                            if j < 3:
                                step(ins)
                    ins.then_inc(banks.drained[b], 1)

                def gather_a(n, it=None):
                    whole(place[n % 2], f"{tag}.at{n}", it=it)
                    whole(slot_gate[:, n % 2, :], f"{tag}.sg{n}", it=it)
                    gather(n, 0, it)

                def gather_b(n, it=None):
                    gather(n, 1, it)
                    for half in range(2):
                        banks.wait_drained(act, f"{tag}.xg{n}.{half}", it)
                    fn(xg_hi[n % 2], xg[n % 2], ACT.Identity).then_inc(xhi_ready, 1)

                gather_a(0)
                gather_b(0)
                with act.Fori(0, BODIES) as it:
                    step.enter(it, 0 if mod is None else 6 * GROUPS_PER_BODY)

                    def split(g, j):
                        for h in range(2):
                            part = Half(tag, len(GROUP_ORDER) * g + j, h)
                            act.wait_ge(slot_full[part.slot], it * (16 * PER_BODY // RING) + part.full)
                            act.wait_ge(halves_done, it * (2 * PER_BODY) + part.free)
                            fn(part.hi, part.raw, ACT.Identity).then_inc(hi_ready, 1)

                    def sig(k):
                        whole(esig[:, k % 2, :], f"{tag}.g{k}", ACT.Silu, it)

                    def hidden(k):
                        banks.wait_full(act, f"{tag}.hT{k}", it)
                        p_ = psum[banks.jobs[f"{tag}.hT{k}"][0]]
                        fn(ehT[:, k % 2, :, :], p_[:, :].rearrange("p (c n) -> p c n", c=HC), ACT.Identity) \
                            .then_inc(hid_hi, 1)

                    for g in range(GROUPS_PER_BODY):
                        for e in range(PER_GROUP):
                            k = PER_GROUP * g + e
                            if e == 0:
                                for j in range(3):
                                    split(g, j)
                                sig(k)
                                split(g, 3)
                            else:
                                split(g, 3 * e + 1)
                                sig(k)
                                if e == 1:
                                    gather_a(g + 1, it)
                                split(g, 3 * e + 2)
                                if e < PER_GROUP - 1:
                                    split(g, 3 * e + 3)
                            hidden(k)
                        gather_b(g + 1, it)
                step.leave(BODIES)

                act.wait_ge(control_ready, layer + 1)
                over = act.value_load(control[0:1, 2 * layer:2 * layer + 1], min_val=0, max_val=GROUPS)
                with act.If(over > 0):
                    first = act.value_load(control[0:1, 2 * layer + 1:2 * layer + 2], min_val=0,
                                           max_val=NMOE - len(GROUP_ORDER))

                    def load(what, e):
                        i = 3 * e + "gud".index(what)
                        act.dma_start(ov_w[i % 2], weights[bass.ds(first + (MOE_FIRST[tag[0]] + POS[what, e]), 1), :, :]
                                      .rearrange("m p n -> p (m n)")).then_inc(ov_loaded[i % 2], 16)

                    act.wait_ge(ov_dve, OV_DVE * layer + 1)
                    load("g", 0)
                    load("u", 0)
                    for e in range(PER_GROUP):
                        act.wait_ge(ov_pe, OV_PE * layer + 4 * e + 1)
                        load("d", e)
                        fn(esig[:, 0, :], psum[0][:, :], ACT.Silu).then_inc(ov_act, 1)
                        act.wait_ge(ov_pe, OV_PE * layer + 4 * e + 2)
                        if e < PER_GROUP - 1:
                            load("g", e + 1)
                        act.wait_ge(ov_pe, OV_PE * layer + 4 * e + 3)
                        fn(ehT_plain[:, 0, :, :], psum[2][:, :].rearrange("p (c n) -> p c n", c=HC), ACT.Identity) \
                            .then_inc(ov_act, 1)
                        act.wait_ge(ov_pe, OV_PE * layer + 4 * e + 4)
                        if e < PER_GROUP - 1:
                            load("u", e + 1)
                with act.Else():
                    act.sem_inc(ov_act, OV_ACT)
                    for loaded in ov_loaded:
                        act.sem_inc(loaded, OV_LOADS)

            act.dma_start(consts[:, :], cst).then_inc(setup_loaded, 16)
            act.dma_start(params[:, :], prm).then_inc(setup_loaded, 16)
            act.dma_start(xT[:, :, :], xT_in).then_inc(xT_loaded, 16)
            act.dma_start(memT, memT_in).then_inc(mem_loaded, 16)
            act.dma_start(x[:, :, :], x_in).then_inc(mem_loaded, 16)
            act.wait_ge(setup_loaded, 32)
            fn(sm("sc"), pr("c"), ACT.Silu).then_inc(silu_c, 1)
            for h in range(8):
                whole(rowbuf[h // 4][:, h % 4, :], f"row.{h}")
                banks.wait_drained(act, f"row.{h}")
                act.dma_start(scratch[h, 0:P * (UROW + 1)].rearrange("(p u) -> p u", p=P)[:, 0:UROW],
                              rowbuf[h // 4][:, h % 4, :]).then_inc(rows_out, 16)
            act.wait_ge(pads_in, 1)
            fn(pad_w, pad_w, ACT.Exp).then_inc(pads_fn, 1)
            act.wait_ge(pads_in, 2)
            fn(sm("pads"), sm("pads"), ACT.Ln).then_inc(pads_fn, 1)
            act.wait_ge(ones_set, 1)

            for l in range(DEPTH):
                tg = f"{l}"
                if l:
                    turned(f"{l - 1}.turn3")
                whole(gqT, f"{tg}.q", scale=0.125)
                whole(alow[0:GATE_RANK, :], f"{tg}.alow")
                for T in range(NT):
                    whole(gv[:, T, :], f"{tg}.v.{T}")
                act.wait_ge(gla_abs, l + 1)
                step(fn(gE, gE, ACT.Exp, scale=-1.0))
                fn(gE, gE, ACT.Ln, bias=1.0).then_inc(gla_log, 1)
                for T in range(NT):
                    whole(gr[:, T, :], f"{tg}.r.{T}", ACT.Silu)
                for T in range(NT):
                    whole(su[:, T, :], f"{tg}.u.{T}", ACT.Gelu_apprx_tanh)
                for T in range(NT):
                    whole(sv[:, T, :], f"{tg}.sv.{T}", ACT.Gelu_apprx_tanh)
                whole(gE, f"{tg}.rem", ACT.Exp)
                whole(decay, f"{tg}.dec", ACT.Exp)
                for j in range(4):
                    whole(xkT[:, 2 * j:2 * j + 2, :], f"{tg}.xk.{j}")
                for T, q in OUTS:
                    whole(xv[:, T, q * 512:(q + 1) * 512], f"{tg}.xv.{T}.{q}")
                for q in (0, 2):
                    whole(oT[:, 2 * q:2 * q + 2, :], f"{tg}.turn0.{q}")
                turned(f"{tg}.turn1")
                for j in range(4):
                    whole(xqT[:, 2 * j:2 * j + 2, :], f"{tg}.xq.{j}", scale=0.0625)
                attention(numbered(cross_units(f"{tg}.x"), ATT[f"{tg}.x"]))
                turned(f"{tg}.turn2")
                act.wait_ge(router_in, l + 1)
                fn(rA, rA, ACT.Exp).then_inc(router_exp, 1)
                experts(f"{tg}.moe")

            act.wait_ge(rows_out, 128)
            act.wait_ge(x_ready, 6)
            for T in range(NT):
                act.dma_start(bias[:, :, T, :], skewed(255 - P * T)).then_inc(bias_back, 16)
            modulated("e.turn0", 0, 0)
            for j in range(2):
                whole(nq[:, 2 * j:2 * j + 2, :], f"e.q.{j}", scale=0.125)
            act.wait_ge(zeros_set, 1)
            for j, (keys, values) in enumerate((("e.ks", "e.vs"), ("e.kw", "e.vw"))):
                carry(keys, [(nk[j][a * DH:(a + 1) * DH, a, :], lambda t, a=a: t[a * DH:(a + 1) * DH, 0:S])
                             for a in range(2)])
                carry(values, [(nv[j][:, :, a, a * DH:(a + 1) * DH],
                                lambda t, a=a: t[:, 0:256].rearrange("p (t c) -> p t c", t=2)[:, :, a * DH:(a + 1) * DH])
                               for a in range(2)])
            whole(gates, "e.gates", ACT.Exp, scale=-1.0)
            for j, n in enumerate("kv"):
                whole(h1T[:, j, :, :], f"e.h1{n}", ACT.Gelu_apprx_tanh)
            carry("e.kc", [(kcz[a * DH:(a + 1) * DH, a, 0:N_CMP], lambda t, a=a: t[0:DH, a * N_CMP:(a + 1) * N_CMP])
                           for a in range(2)])
            carry("e.vc", [(vcz[0:N_CMP, a, a * DH:(a + 1) * DH], lambda t, a=a: t[0:N_CMP, a * DH:(a + 1) * DH])
                           for a in range(2)])
            attention(numbered(nsa_units(), ATT["nsa"]))
            for j in range(2):
                whole(mq[:, 2 * j:2 * j + 2, :], f"e.mq.{j}", scale=0.125)
            act.wait_ge(zeros_set, 2)
            for j in range(2):
                carry(f"e.mk.{j}", [(mk[a * DH:(a + 1) * DH, 4 * a + 2 * j:4 * a + 2 * j + 2, :],
                                     lambda t, a=a: t[a * DH:(a + 1) * DH, :].rearrange("p (i s) -> p i s", i=2))
                                    for a in range(2)])
            for T in range(NT):
                carry(f"e.mv.{T}", [(mv[:, T, 4 * a:4 * a + 4, a * DH:(a + 1) * DH],
                                     lambda t, a=a: t[:, :].rearrange("p (i c) -> p i c", i=4)[:, :, a * DH:(a + 1) * DH])
                                    for a in range(2)])
            attention(numbered(moba_units(), ATT["moba"]))
            modulated("e.turn1", 0, 24)
            act.wait_ge(router_in, 3)
            fn(rA, rA, ACT.Exp, scale=-1.0).then_inc(router_exp, 1)
            experts("e.moe", 0)

            modulated("o.turn0", 1, 0)
            for T in range(NT):
                whole(cq[:, T, :], f"o.c.{T}")
            for j in range(2):
                whole(qn[:, 2 * j:2 * j + 2, :], f"o.qn.{j}", scale=MLA_SCALE)
                whole(kn[:, 2 * j:2 * j + 2, :], f"o.kn.{j}")
            for T in range(NT):
                whole(lv[:, T, :], f"o.v.{T}")
            whole(qrT, "o.qrT")
            attention(numbered(mla_units(), ATT["mla"]))
            for j in range(2):
                whole(swq[:, 2 * j:2 * j + 2, :], f"o.sq.{j}", scale=0.125)
            act.wait_ge(zeros_set, 3)
            carry("o.sk", [(swk[a * DH:(a + 1) * DH, a, :], lambda t, a=a: t[a * DH:(a + 1) * DH, 0:S]) for a in range(2)])
            carry("o.sv", [(swv[:, :, a, a * DH:(a + 1) * DH],
                            lambda t, a=a: t[:, 0:256].rearrange("p (t c) -> p t c", t=2)[:, :, a * DH:(a + 1) * DH])
                           for a in range(2)])
            attention(numbered(swa_units(), ATT["swa"]))
            modulated("o.turn1", 1, 24)
            act.wait_ge(router_in, 4)
            fn(rA, rA, ACT.Exp, scale=-1.0).then_inc(router_exp, 1)
            experts("o.moe", 1)

        @block.vector
        def _(dve):
            v = nc.vector
            step = Steps(dve, dve_steps)
            users, stats = [0], [0]

            def drained(name, ins, it=None):
                ins.then_inc(banks.drained[banks.jobs[name][0]], 1)
                banks.wait_drained(dve, name, it)

            def bank(name, it=None):
                banks.wait_full(dve, name, it)
                return psum[banks.jobs[name][0]]

            cells = {}

            def tell(semaphore):
                k = cells.setdefault(str(semaphore), len(cells))
                v.memset(sm("sig")[:, k:k + 1], 0.0).then_inc(semaphore, 1)

            def tt(o, a, b, op):
                return v.tensor_tensor(o, a, b, op)

            def rstd(n):
                stats[0] += 1
                dve.wait_ge(rstd_ready, stats[0])

            def eps(cols, src, scale, e):
                return v.tensor_scalar(stat_in[:, cols], src, scale, e, ALU.mult, ALU.add)

            def vectors_loaded():
                users[0] += 1
                dve.wait_ge(vecs_loaded, 16 * users[0])

            def turned(tag, dest=None):
                dest = xT if dest is None else dest
                for q in (1, 3):
                    p_ = bank(f"{tag}.{q}")
                    drained(f"{tag}.{q}", v.tensor_copy(dest[:, 2 * q:2 * q + 2, :],
                                                        p_[:, :].rearrange("p (a b) -> p a b", a=2)))

            norms = [0]

            def layer_norm(src):
                bn, mv_ = sm("bn", 2, 2 * 6), sm("mv", 2, 2)
                for T in range(NT):
                    for q in range(2):
                        (step if T and q else step.later)(
                            v.bn_stats(bn[:, T, 6 * q:6 * q + 6], src[:, T, q * 512:(q + 1) * 512]))
                for T in range(NT):
                    (step if T else step.later)(v.bn_aggr(mv_[:, T, :], bn[:, T, :]))
                eps(slice(0, 2), mv_[:, :, 1], 1.0, LN_EPS).then_inc(var_ready, 1)
                rstd(2)
                for T in range(NT):
                    (step if T else step.later)(v.tensor_scalar(
                        x[:, T, :], src[:, T, :], mv_[:, T, 0:1], stat_out[:, T:T + 1], ALU.subtract, ALU.mult))
                vectors_loaded()
                for h in range(2):
                    c = slice(h * 512, (h + 1) * 512)
                    step(tt(x[:, :, c], x[:, :, c], lnv[:, 0:1, c].broadcast_to([P, NT, 512]), ALU.mult))
                    ins = tt(x[:, :, c], x[:, :, c], lnv[:, 1:2, c].broadcast_to([P, NT, 512]), ALU.add)
                    if h:
                        step(ins)
                    else:
                        ins.then_inc(x_half, 1)
                norms[0] += 1
                dve.wait_ge(x_half, norms[0])
                tell(vecs_used)

            def residual(tag):
                for T, q in OUTS:
                    p_ = bank(f"{tag}.{T}.{q}")
                    c = slice(q * 512, (q + 1) * 512)
                    drained(f"{tag}.{T}.{q}", v.scalar_tensor_tensor(
                        out=x[:, T, c], in0=x[:, T, c], scalar=ALPHA, in1=p_[:, :], op0=ALU.mult, op1=ALU.add))

            def tell_x():
                tell(x_ready)

            def attention(units):
                def biased_max(u):
                    i, nk_ = u["n"] % 2, u["nk"]
                    p_ = bank(u["name"] + ".s")
                    if u["bias"] is None:
                        v.tensor_reduce(nm[:, i, :], p_[:, :].rearrange("p (a s) -> p a s", a=2), AX.X, ALU.max,
                                        negate=True).then_inc(att_max, 1)
                        return
                    mx = sm("mx", 2, 2)[:, i, :]
                    for a in range(2):
                        ins = v.tensor_tensor_reduce(
                            out=aS[:, i, a, 0:nk_], in0=p_[:, a * S:a * S + nk_], in1=u["bias"][a], scale=1.0,
                            scalar=LOW, op0=ALU.add, op1=ALU.max, accum_out=mx[:, a:a + 1])
                        if a == 0:
                            step(ins)
                    drained(u["name"] + ".s", ins)
                    if u["sink"] is not None:
                        step(tt(mx, mx, u["sink"], ALU.max))
                        step(tt(sm("es", 2, 2)[:, i, :], u["sink"], mx, ALU.subtract))
                    v.tensor_scalar(nm[:, i, :], mx, -1.0, None, ALU.mult).then_inc(att_max, 1)

                def normalise(u):
                    i, nk_ = u["n"] % 2, u["nk"]
                    if u["bias"] is None:
                        banks.wait_drained(dve, u["name"] + ".s")
                    else:
                        exps[0] += 1
                        dve.wait_ge(att_exp, exps[0])
                    if u["sink"] is not None:
                        step(tt(den[:, i, :], den[:, i, :], sm("es", 2, 2)[:, i, :], ALU.add))
                    step(v.reciprocal(den[:, i, :], den[:, i, :]))
                    if u["gate"] is not None:
                        step(tt(den[:, i, :], den[:, i, :], u["gate"], ALU.mult))
                    tt(aP(u)[:, :, 0:nk_], aP(u)[:, :, 0:nk_],
                       den[:, i, :].unsqueeze(2).broadcast_to([P, 2, nk_]), ALU.mult).then_inc(att_prob, 1)

                def outputs(u):
                    if u["last"]:
                        p_ = bank(u["o"])
                        r = u["regions"]
                        drained(u["o"], v.tensor_copy(u["dest"], p_[:, 0:r * P].rearrange("p (a b) -> p a b", a=r)))

                n = len(units)
                for k in range(n + 3):
                    if k < n:
                        biased_max(units[k])
                    if 1 <= k <= n:
                        normalise(units[k - 1])
                    if k >= 3:
                        outputs(units[k - 3])

            exps = [0]

            def route(tag, bname, first):
                p_ = bank(f"{tag}.logits")
                lg = p_[:, 0:32].rearrange("p (t e) -> p t e", t=2)
                if first:
                    drained(f"{tag}.logits", tt(rA, lg, pr("b_router").unsqueeze(1).broadcast_to([P, 2, 16]), ALU.add))
                    step(v.tensor_reduce(r2a, rA, AX.X, ALU.max))
                    tt(rA, rA, r2a.unsqueeze(2).broadcast_to([P, 2, 16]), ALU.subtract).then_inc(router_in, 1)
                    routed[0] += 1
                    dve.wait_ge(router_exp, routed[0])
                    step(v.tensor_reduce(r2a, rA, AX.X, ALU.add))
                    step(v.reciprocal(r2a, r2a))
                    step(tt(rA, rA, r2a.unsqueeze(2).broadcast_to([P, 2, 16]), ALU.mult))
                    score = rA
                else:
                    drained(f"{tag}.logits", v.tensor_copy(rA, lg))
                    tell(router_in)
                    routed[0] += 1
                    dve.wait_ge(router_exp, routed[0])
                    step(v.tensor_scalar(rA, rA, 1.0, None, ALU.add))
                    step(v.reciprocal(rA, rA))
                    step(tt(rB, rA, pr("router_b_2").unsqueeze(1).broadcast_to([P, 2, 16]), ALU.add))
                    score = rB
                four = score.rearrange("p t (g j) -> p (t g) j", g=4)
                step.later(tt(r_hi, four[:, :, 0:4:2], four[:, :, 1:4:2], ALU.max))
                step(tt(r_lo, four[:, :, 0:4:2], four[:, :, 1:4:2], ALU.min))
                step.later(tt(r8a, r_hi[:, :, 0], r_hi[:, :, 1], ALU.max))
                step.later(tt(r8b, r_hi[:, :, 0], r_hi[:, :, 1], ALU.min))
                step(tt(r8c, r_lo[:, :, 0], r_lo[:, :, 1], ALU.max))
                step(tt(r8b, r8b, r8c, ALU.max))
                step(tt(r8a, r8a, r8b, ALU.add))

                def first_best(o, values, tell_done=None):
                    step(v.tensor_reduce(r2a, values, AX.X, ALU.max))
                    step(tt(o, values, r2a.unsqueeze(2).broadcast_to([P, 2, 4]), ALU.is_equal))
                    step(tt(o, o, cs("rank4").unsqueeze(1).broadcast_to([P, 2, 4]), ALU.mult))
                    step(v.tensor_reduce(r2a, o, AX.X, ALU.max))
                    ins = tt(o, o, r2a.unsqueeze(2).broadcast_to([P, 2, 4]), ALU.is_equal)
                    if tell_done is None:
                        step(ins)
                    else:
                        ins.then_inc(tell_done, 1)
                        dve.wait_ge(tell_done, MOE_LAYER[tag] + 1)

                first_best(r_g, r8a.rearrange("p (t g) -> p t g", t=2), group_ready)

                def in_group(o, values):
                    step(tt(r_tmp, values.rearrange("p t (g j) -> p t g j", g=4),
                            r_g.unsqueeze(3).broadcast_to([P, 2, 4, 4]), ALU.mult))
                    step(v.tensor_reduce(o, r_tmp.rearrange("p t g j -> p t j g"), AX.X, ALU.add))

                in_group(r_a, rA)
                if first:
                    step(v.tensor_copy(r_b, r_a))
                else:
                    in_group(r_b, score)
                first_best(r_1, r_b)
                step(v.scalar_tensor_tensor(out=r_b, in0=r_1, scalar=NEG, in1=r_b, op0=ALU.mult, op1=ALU.add))
                first_best(r_2, r_b)
                step(tt(r_1, r_1, r_2, ALU.add))
                step(tt(r_a, r_a, r_1, ALU.mult))
                step(v.tensor_reduce(r2a, r_a, AX.X, ALU.add))
                step(v.reciprocal(r2a, r2a))
                step(tt(r_a, r_a, r2a.unsqueeze(2).broadcast_to([P, 2, 4]), ALU.mult))
                p_ = bank(f"{tag}.moe.rank")
                step.later(v.tensor_copy(sm("counts", GROUPS), p_[:, 8:12]))
                drained(f"{tag}.moe.rank", tt(r_1, p_[:, 0:8].rearrange("p (t g) -> p t g", t=NT), r_g, ALU.mult))
                step(v.tensor_reduce(r2a, r_1, AX.X, ALU.add))
                step.later(v.tensor_scalar(slot[:, :, GROUPS], r2a, float(1 - P), None, ALU.add))
                step(v.scalar_tensor_tensor(out=slot[:, :, 0:GROUPS], in0=r2a.unsqueeze(2).broadcast_to([P, NT, GROUPS]),
                                            scalar=1.0, in1=r_g, op0=ALU.add, op1=ALU.mult))

            def overflow_control(layer):
                counts, over, begin_ = sm("counts", GROUPS), sm("over", 2)[:, 0:1], sm("over", 2)[:, 1:2]
                step(v.tensor_scalar(counts, counts, float(P), None, ALU.is_gt))
                step(tt(counts, counts, cs("rank4"), ALU.mult))
                step(v.tensor_reduce(over, counts, AX.X, ALU.add))
                step(v.tensor_scalar(begin_, over, float(-len(GROUP_ORDER)), float(NMOE), ALU.mult, ALU.add))
                v.tensor_copy(control[:, 2 * layer:2 * layer + 2], sm("over", 2)).then_inc(control_ready, 1)
                dve.wait_ge(control_ready, layer + 1)

            routed = [0]

            def experts(tag, ada_layer):
                layer = MOE_LAYER[tag[0]]
                total, acc = ysum(tag), yacc(tag)

                def slots(n, it=None):
                    for T in range(NT):
                        at = slot[:, T, n:n + 1] if it is None else slot[:, T, bass.ds(it * GROUPS_PER_BODY + n, 1)]
                        ins = v.tensor_scalar(pick[:, T, :], cs("iota"), at, None, ALU.is_equal)
                        if T == 0:
                            step(ins)
                    ins.then_inc(pick_ready, 1)

                def low_tokens(n, it=None):
                    count = GATHERS * layer + n + 1
                    dve.wait_ge(xhi_ready, count if it is None else it * GROUPS_PER_BODY + count)
                    tt(xg_lo[n % 2], xg[n % 2], xg_hi[n % 2], ALU.subtract).then_inc(xlo_ready, 1)

                slots(0)
                overflow_control(layer)
                low_tokens(0)
                with dve.Fori(0, BODIES) as it:
                    step.enter(it, GROUPS_PER_BODY)

                    def ada_out(k):
                        if ada_layer is None:
                            return
                        p_ = bank(f"{tag}.ada{k}", it)
                        v.tensor_copy(sm("modc", 2, 48)[:, ada_layer, bass.ds(it * (3 * EXP_PER_BODY) + 3 * k, 3)],
                                      p_[:, 0:3]).then_inc(banks.drained[banks.jobs[f"{tag}.ada{k}"][0]], 1)

                    def h(k):
                        banks.wait_drained(dve, f"{tag}.g{k}", it)
                        p_ = bank(f"{tag}.u{k}", it)
                        tt(eh[:, k % 2, :], esig[:, k % 2, :], p_[:, :], ALU.mult).then_inc(
                            banks.drained[banks.jobs[f"{tag}.u{k}"][0]], 1)

                    def split(g, j, halves=(0, 1)):
                        for half in halves:
                            part = Half(tag, len(GROUP_ORDER) * g + j, half)
                            dve.wait_ge(hi_ready, it * (2 * PER_BODY) + part.n)
                            tt(part.lo, part.raw, part.hi, ALU.subtract).then_inc(lo_ready, 1)

                    def hidden(k):
                        dve.wait_ge(hid_hi, it * EXP_PER_BODY + (NEXP * layer + k + 1))
                        p_ = bank(f"{tag}.hT{k}", it)
                        tt(ehT_lo[:, k % 2, :, :], p_[:, :].rearrange("p (c n) -> p c n", c=HC), ehT[:, k % 2, :, :],
                           ALU.subtract).then_inc(banks.drained[banks.jobs[f"{tag}.hT{k}"][0]], 1)

                    def y(k):
                        e = k % PER_GROUP
                        for n in range(2):
                            name = f"{tag}.y{k}.{n}"
                            c = slice(n * 512, (n + 1) * 512)
                            g_ = slot_gate[:, k // PER_GROUP, e:e + 1]
                            if e:
                                banks.wait_drained(dve, f"{tag}.y{k - 1}.{n}", it)
                            p_ = bank(name, it)
                            if e:
                                ins = v.scalar_tensor_tensor(out=acc[:, c], in0=p_[:, :], scalar=g_, in1=acc[:, c],
                                                             op0=ALU.mult, op1=ALU.add)
                            else:
                                ins = v.tensor_scalar(acc[:, c], p_[:, :], g_, None, ALU.mult)
                            ins.then_inc(banks.drained[banks.jobs[name][0]], 1)
                        ada_out(k)

                    def scattered(g):
                        for T, n, name in scatter_names(tag, g):
                            if g:
                                banks.wait_drained(dve, f"{tag}.sc{g - 1}.{T}.{n}", it)
                            else:
                                banks.wait_drained_round_before(dve, f"{tag}.sc{GROUPS_PER_BODY - 1}.{T}.{n}", it)
                            p_ = bank(name, it)
                            part = total[:, T, n * 512:(n + 1) * 512]
                            tt(part, p_[:, :], part, ALU.add).then_inc(banks.drained[banks.jobs[name][0]], 1)

                    for g in range(GROUPS_PER_BODY):
                        for e in range(PER_GROUP):
                            k = PER_GROUP * g + e
                            if e == 0:
                                split(g, 0)
                                if g:
                                    y(k - 1)
                                split(g, 1)
                                split(g, 2)
                                if g:
                                    scattered(g - 1)
                                h(k)
                                slots(g + 1, it)
                                down = 3
                                split(g, down, (0,))
                            elif e < PER_GROUP - 1:
                                split(g, 3 * e + 1)
                                y(k - 1)
                                split(g, 3 * e + 2)
                                h(k)
                                down = 3 * e + 3
                                split(g, down, (0,))
                            else:
                                split(g, 3 * e + 1)
                                y(k - 1)
                                down = 3 * e + 2
                                split(g, down, (0,))
                                h(k)
                            hidden(k)
                            split(g, down, (1,))
                        low_tokens(g + 1, it)
                    y(EXP_PER_BODY - 1)
                    scattered(GROUPS_PER_BODY - 1)
                step.leave(BODIES)
                for T, n, name in scatter_names(tag, GROUPS_PER_BODY - 1):
                    banks.wait_drained(dve, name, rounds=BODIES)
                for n in range(2):
                    banks.wait_drained(dve, f"{tag}.y{EXP_PER_BODY - 1}.{n}", rounds=BODIES)

                over = dve.value_load(control[0:1, 2 * layer:2 * layer + 1], min_val=0, max_val=GROUPS)
                with dve.If(over > 0):
                    v.memset(acc, 0.0)
                    dve.wait_ge(xlo_ready, GATHERS * (layer + 1))
                    tt(xg[0], xg_lo[0], xg_hi[0], ALU.add).then_inc(ov_dve, 1)
                    dve.wait_ge(ov_dve, OV_DVE * layer + 1)
                    with dve.Fori(0, PER_GROUP) as it:
                        dve.wait_ge(ov_act, it * 2 + (OV_ACT * layer + 1))
                        dve.wait_ge(ov_pe, it * 4 + (OV_PE * layer + 2))
                        tt(eh[:, 0, :], esig[:, 0, :], psum[1][:, :], ALU.mult).then_inc(ov_dve, 1)
                        dve.wait_ge(ov_pe, it * 4 + (OV_PE * layer + 4))
                        dve.wait_ge(ov_dve, it * 2 + (OV_DVE * layer + 2))
                        ov_steps = [v.scalar_tensor_tensor(
                            out=acc[:, n * 512:(n + 1) * 512], in0=psum[3 + n][:, :],
                            scalar=slot_gate[:, 0, bass.ds(it, 1)], in1=acc[:, n * 512:(n + 1) * 512],
                            op0=ALU.mult, op1=ALU.add) for n in range(2)]
                        ov_steps[1].then_inc(ov_dve, 1)
                    dve.wait_ge(ov_pe, OV_PE * (layer + 1))
                    for b, (T, n) in zip((5, 6, 7, 0), OUTS):
                        part = total[:, T, n * 512:(n + 1) * 512]
                        ins = tt(part, psum[b][:, :], part, ALU.add)
                    ins.then_inc(ov_dve, 1)
                with dve.Else():
                    dve.sem_inc(ov_dve, OV_DVE)
                dve.wait_ge(ov_dve, OV_DVE * (layer + 1))

            def sum_squares(cols, parts, junk):
                for k, part in enumerate(parts):
                    step(v.tensor_tensor_reduce(out=junk(k), in0=part, in1=part, scale=1.0, scalar=0.0,
                                                op0=ALU.mult, op1=ALU.add, accum_out=stat_in[:, cols + k:cols + k + 1]))

            def adaptive_norm(tag, layer, gain, scale, shift):
                sum_squares(0, [x[:, T, :] for T in range(NT)], lambda T: mix[:, T, :])
                eps(slice(0, 2), stat_in[:, 0:2], 1.0 / D, RMS_EPS).then_inc(var_ready, 1)
                rstd(2)
                step(v.scalar_tensor_tensor(out=sm("modg")[:, 0:8], in0=sm("modc", 2, 48)[:, layer, scale:scale + 8],
                                            scalar=1.0, in1=gain, op0=ALU.add, op1=ALU.mult))
                for T in range(NT):
                    step(v.tensor_scalar(mix[:, T, :], x[:, T, :], stat_out[:, T:T + 1], None, ALU.mult))
                tell_x()
                for q in (1, 3):
                    p_ = bank(f"{tag}.{q}")
                    for j in range(2):
                        c = 2 * q + j
                        ins = v.tensor_scalar(xT[:, c, :], p_[:, j * S:(j + 1) * S], sm("modg")[:, c:c + 1],
                                              sm("modc", 2, 48)[:, layer, shift + c:shift + c + 1], ALU.mult, ALU.add)
                        if j == 0:
                            step(ins)
                    drained(f"{tag}.{q}", ins)

            def take_gate(tag):
                for q in range(2):
                    p_ = bank(f"{tag}.{q}")
                    drained(f"{tag}.{q}", v.tensor_copy(gate_row[:, q * 512:(q + 1) * 512], p_[:, :]))

            def gated_residual(tag):
                for T, q in OUTS:
                    p_ = bank(f"{tag}.{T}.{q}")
                    c = slice(q * 512, (q + 1) * 512)
                    drained(f"{tag}.{T}.{q}", tt(mix[:, T, c], p_[:, :], gate_row[:, c], ALU.mult))
                    step(tt(x[:, T, c], x[:, T, c], mix[:, T, c], ALU.add))

            def gated_sum(tag):
                total = ysum(tag)
                step(tt(total, total, gate_row.unsqueeze(1).broadcast_to([P, NT, D]), ALU.mult))
                step(tt(x[:, :, :], x[:, :, :], total, ALU.add))

            step(v.memset(stat_in, 1.0))
            v.memset(alow[:, :], 1.0).then_inc(ones_set, 1)
            dve.wait_ge(setup_loaded, 32)
            pads, pad_max = sm("pads", 2 * NT, 8), sm("padmax", 2 * NT, 8)
            step(tt(pad_w, pr("rel_rows", 8, 33).unsqueeze(1).broadcast_to([P, 2 * NT, 8, 33]),
                    cs("lncount", 2 * NT, 33).unsqueeze(2).broadcast_to([P, 2 * NT, 8, 33]), ALU.add))
            step(v.tensor_reduce(pad_max, pad_w, AX.X, ALU.max))
            tt(pad_w, pad_w, pad_max.unsqueeze(3).broadcast_to([P, 2 * NT, 8, 33]), ALU.subtract).then_inc(pads_in, 1)
            dve.wait_ge(pads_fn, 1)
            v.tensor_reduce(pads, pad_w, AX.X, ALU.add).then_inc(pads_in, 1)
            dve.wait_ge(pads_fn, 2)
            step(tt(pads, pads, pad_max, ALU.add))
            for l in range(DEPTH):
                v.memset(pr("w_s", 2, 4, P)[64:P, l, :, 0:64], 0.0).then_inc(ws_masked, 1)
            dve.wait_ge(mem_loaded, 32)
            dve.wait_ge(silu_c, 1)

            for l in range(DEPTH):
                tg = f"{l}"
                if l:
                    turned(f"{l - 1}.turn3")
                p_ = bank(f"{tg}.k")
                drained(f"{tg}.k", v.tensor_copy(gk, p_[:, :].rearrange("p (t n) -> p t n", t=2)))
                if l == 0:
                    dve.wait_ge(rows_out, 128)
                p_ = bank(f"{tg}.z")
                z = p_[:, :].rearrange("p (t n) -> p t n", t=2)
                step(v.tensor_scalar(gg, z, 0.0, None, ALU.min))
                ins = v.scalar_tensor_tensor(out=gE, in0=gg, scalar=-2.0, in1=z, op0=ALU.mult, op1=ALU.add)
                drained(f"{tg}.z", ins)
                tell(gla_abs)
                dve.wait_ge(gla_log, l + 1)
                tt(gg, gg, gE, ALU.subtract).then_inc(gla_g, 1)
                banks.wait_drained(dve, f"{tg}.rem")
                for c in range(NCHUNK):
                    T = c // 2
                    ins = v.scalar_tensor_tensor(out=gkd[:, c, :], in0=gk[:, T, :], scalar=inch[:, c % 2:c % 2 + 1],
                                                 in1=gE[:, T, :], op0=ALU.mult, op1=ALU.mult)
                    if c < NCHUNK - 1:
                        step(ins)
                ins.then_inc(gla_kd, 1)
                banks.wait_drained(dve, f"{tg}.dec")
                for c in range(NCHUNK):
                    p_ = bank(f"{tg}.kv.{c}")
                    ins = tt(states[:, c, :, :], p_[:, :].rearrange("p (m n) -> p m n", m=2),
                             blocks.unsqueeze(1).broadcast_to([P, 2, 256]), ALU.mult)
                    drained(f"{tg}.kv.{c}", ins)
                    if c == 0:
                        tell(gla_state)
                    else:
                        dve.wait_ge(gla_state, NCHUNK * l + c)
                        for m in range(2):
                            ins = v.scalar_tensor_tensor(out=states[:, c, m, :], in0=states[:, c - 1, m, :],
                                                         scalar=decay[:, m, c:c + 1], in1=states[:, c, m, :],
                                                         op0=ALU.mult, op1=ALU.add)
                            if m == 0:
                                step(ins)
                        ins.then_inc(gla_state, 1)
                banks.wait_drained(dve, f"{tg}.sv.1")
                bnb, mvb = sm("bnb", 8, 6), sm("mvb", 8, 2)
                for k in range(8):
                    T, g = divmod(k, 4)
                    step(v.bn_stats(bnb[:, k, :], sv[:, T, g * P:(g + 1) * P]))
                    step(v.bn_aggr(mvb[:, k, :], bnb[:, k, :]))
                eps(slice(0, 8), mvb[:, :, 1], 1.0, LN_EPS).then_inc(var_ready, 1)
                rstd(8)
                for k in range(8):
                    T, g = divmod(k, 4)
                    part = sv[:, T, g * P:(g + 1) * P]
                    step(v.tensor_scalar(part, part, mvb[:, k, 0:1], stat_out[:, k:k + 1], ALU.subtract, ALU.mult))
                vectors_loaded()
                step(tt(sv, sv, mixv[:, 1:2, :].broadcast_to([P, NT, 512]), ALU.mult))
                tt(sv, sv, mixv[:, 2:3, :].broadcast_to([P, NT, 512]), ALU.add).then_inc(sgu_ready, 1)
                dve.wait_ge(sgu_ready, l + 1)
                for c in range(NCHUNK):
                    p_ = bank(f"{tg}.o.{c}")
                    rows = slice((c % 2) * 64, (c % 2) * 64 + 64)
                    drained(f"{tg}.o.{c}", v.tensor_copy(mix[rows, c // 2, 0:512], p_[rows, :]))
                sq = cut(oT[:, :, :].rearrange("p a b -> p (a b)"), 1024, NT, 512)
                o_ = mix[:, :, 0:512]
                step(tt(sq, o_, o_, ALU.mult))
                step(v.tensor_reduce(stat_in[:, 0:8], sq.rearrange("p t (h d) -> p (t h) d", h=4), AX.X, ALU.add))
                eps(slice(0, 8), stat_in[:, 0:8], 1.0 / P, RMS_EPS).then_inc(var_ready, 1)
                rstd(8)
                for T in range(NT):
                    oh = mix[:, T, 0:512].rearrange("p (h d) -> p h d", h=4)
                    step(tt(oh, oh, stat_out[:, 4 * T:4 * T + 4].unsqueeze(2).broadcast_to([P, 4, P]), ALU.mult))
                step(tt(o_, o_, mixv[:, 0:1, :].broadcast_to([P, NT, 512]), ALU.mult))
                tell(vecs_used)
                step(tt(o_, o_, gr, ALU.mult))
                for T in range(NT):
                    p_ = bank(f"{tg}.mix.{T}")
                    for g in range(SGU_GROUPS):
                        c = slice(g * P, (g + 1) * P)
                        ins = v.scalar_tensor_tensor(out=mix[:, T, 512 + g * P:512 + (g + 1) * P], in0=p_[:, c],
                                                     scalar=pr("b_s")[:, 4 * l + g:4 * l + g + 1],
                                                     in1=su[:, T, c], op0=ALU.add, op1=ALU.mult)
                        if g < SGU_GROUPS - 1:
                            step(ins)
                    drained(f"{tg}.mix.{T}", ins)
                turned(f"{tg}.turn0", oT)
                residual(f"{tg}.out")
                layer_norm(x)
                tell_x()
                turned(f"{tg}.turn1")
                attention(numbered(cross_units(f"{tg}.x"), ATT[f"{tg}.x"]))
                residual(f"{tg}.xo")
                layer_norm(x)
                tell_x()
                turned(f"{tg}.turn2")
                route(tg, "b_router", True)
                step(v.tensor_scalar(mix[:, :, :], x[:, :, :], ALPHA, None, ALU.mult))
                experts(f"{tg}.moe", l)
                layer_norm(mix)
                if l == 0:
                    tell_x()

            adaptive_norm("e.turn0", 0, pr("norm_mix")[:, 0:8], 8, 0)
            p_ = bank("e.c")
            for j, pos in enumerate(("pos_k", "pos_v")):
                for a in range(2):
                    view = p_[a * DH:(a + 1) * DH, j * S:(j + 1) * S].rearrange("p (b r) -> p r b", r=16)
                    for odd in range(2):
                        for half in range(2):
                            ins = tt(flat[odd * DH:(odd + 1) * DH, j, 8 * half:8 * half + 8, a * N_CMP:(a + 1) * N_CMP],
                                     view[:, odd:16:2, half:half + N_CMP],
                                     pr(pos)[odd * DH:(odd + 1) * DH, 8 * half:8 * half + 8].unsqueeze(2)
                                     .broadcast_to([DH, 8, N_CMP]), ALU.add)
                            if (j, a, odd, half) != (1, 1, 1, 1):
                                step(ins)
            drained("e.c", ins)
            banks.wait_drained(dve, "e.gates")
            step(v.tensor_scalar(gates, gates, 1.0, None, ALU.add))
            step(v.reciprocal(gates, gates))
            for T in range(NT):
                g0 = gates[:, T, 0:24:3]
                step(v.tensor_scalar(g0, g0, cs("valid")[:, T:T + 1], None, ALU.mult))
            dve.wait_ge(bias_back, 32)
            attention(numbered(nsa_units(), ATT["nsa"]))
            attention(numbered(moba_units(), ATT["moba"]))
            take_gate("e.gm")
            gated_residual("e.out")
            adaptive_norm("e.turn1", 0, pr("norm_ffn")[:, 0:8], 32, 24)
            route("e", "router_b_2", False)
            step(v.memset(ysum("e.moe"), 0.0))
            experts("e.moe", None)
            take_gate("e.gf")
            gated_sum("e.moe")

            adaptive_norm("o.turn0", 1, pr("norm_mix")[:, 8:16], 8, 0)
            banks.wait_drained(dve, "o.c.0")
            banks.wait_drained(dve, "o.c.1")
            sum_squares(0, [cq[:, T, 0:256] for T in range(NT)] + [cq[:, T, 256:384] for T in range(NT)],
                lambda k: rt[:, 0:256] if k < 2 else rt[:, 0:128])
            step(eps(slice(0, 2), stat_in[:, 0:2], 1.0 / 256, RMS_EPS))
            eps(slice(2, 4), stat_in[:, 2:4], 1.0 / 128, RMS_EPS).then_inc(var_ready, 1)
            rstd(4)
            for T in range(NT):
                step(v.tensor_scalar(cq[:, T, 0:256], cq[:, T, 0:256], stat_out[:, T:T + 1], None, ALU.mult))
                ins = v.tensor_scalar(cq[:, T, 256:384], cq[:, T, 256:384], stat_out[:, 2 + T:3 + T], None, ALU.mult)
                if T == 0:
                    step(ins)
            ins.then_inc(lat_ready, 1)
            dve.wait_ge(lat_ready, 1)
            cos, sin = cs("cos", NT, 32), cs("sin", NT, 32)

            def rotate(o1, o2, x1, x2, c, s_, t1, t2):
                step(tt(t1, x1, c, ALU.mult))
                step(tt(t2, x2, s_, ALU.mult))
                step(tt(o1, t1, t2, ALU.subtract))
                step(tt(t1, x1, s_, ALU.mult))
                step(tt(t2, x2, c, ALU.mult))
                step(tt(o2, t1, t2, ALU.add))

            t1, t2 = (rt[:, a:a + 64].rearrange("p (t n) -> p t n", t=2) for a in (0, 64))
            rotate(kr2[:, :, 0:32], kr2[:, :, 32:64], cq[:, :, 384:416], cq[:, :, 416:448], cos, sin, t1, t2)
            v.tensor_copy(kr2[:, :, 64:128], kr2[:, :, 0:64]).then_inc(rope_ready, 1)
            p_ = bank("o.cqT")
            for j in range(2):
                ins = v.tensor_scalar(cT[:, j, :], p_[:, j * S:(j + 1) * S], pr("q_norm")[:, j:j + 1], None, ALU.mult)
                if j == 0:
                    step(ins)
            drained("o.cqT", ins)
            p_ = bank("o.ckvT")
            drained("o.ckvT", v.tensor_scalar(cT[:, 2, :], p_[:, 0:S], pr("kv_norm")[:, 0:1], None, ALU.mult))
            p_ = bank("o.qr")
            drained("o.qr", v.tensor_scalar(qrn, p_[:, :].rearrange("p (t n) -> p t n", t=2), MLA_SCALE, None, ALU.mult))
            for T in range(NT):
                q4 = qrn[:, T, :].rearrange("p (h n) -> p h n", h=4)
                o4 = qro[:, T, :].rearrange("p (h n) -> p h n", h=4)
                c4, s4 = (t[:, T:T + 1, :].broadcast_to([P, 4, 32]) for t in (cos, sin))
                t1, t2 = (rt[:, a:a + 128].rearrange("p (h n) -> p h n", h=4) for a in (0, 128))
                rotate(o4[:, :, 0:32], o4[:, :, 32:64], q4[:, :, 0:32], q4[:, :, 32:64], c4, s4, t1, t2)
            tell(rope_ready)
            dve.wait_ge(zeros_set, 3)
            p_ = bank("o.krT")
            for a in range(2):
                ins = v.tensor_copy(krz[a * DH:(a + 1) * DH, a, :], p_[a * DH:(a + 1) * DH, 0:S])
                if a == 0:
                    step(ins)
            drained("o.krT", ins)
            attention(numbered(mla_units(), ATT["mla"]))
            dve.wait_ge(bias_ready, 1)
            attention(numbered(swa_units(), ATT["swa"]))
            take_gate("o.gm")
            gated_residual("o.out")
            adaptive_norm("o.turn1", 1, pr("norm_ffn")[:, 8:16], 32, 24)
            route("o", "router_b_2", False)
            step(v.memset(ysum("o.moe"), 0.0))
            experts("o.moe", None)
            take_gate("o.gf")
            gated_sum("o.moe")
            sum_squares(0, [x[:, T, :] for T in range(NT)], lambda T: mix[:, T, :])
            eps(slice(0, 2), stat_in[:, 0:2], 1.0 / D, RMS_EPS).then_inc(var_ready, 1)
            rstd(2)
            vectors_loaded()
            for T in range(NT):
                v.scalar_tensor_tensor(out=mix[:, T, :], in0=x[:, T, :], scalar=stat_out[:, T:T + 1],
                                       in1=lnv[:, 0, :], op0=ALU.mult, op1=ALU.mult).then_inc(out_ready, 1)

        @block.gpsimd
        def _(pool):
            loads, stats = [0], [0]

            def load_vectors(dest, row, rows, after=None):
                if loads[0]:
                    pool.wait_ge(vecs_used, loads[0])
                loads[0] += 1
                pool.dma_start(dest, vecs[row:row + rows, :].rearrange("r n -> (r n)").partition_broadcast(P)) \
                    .then_inc(vecs_loaded, 16)

            def rstd():
                stats[0] += 1
                pool.wait_ge(var_ready, stats[0])
                nc.gpsimd.tensor_tensor(stat_out, stat_in, cs("half"), ALU.pow).then_inc(rstd_ready, 1)

            step = Steps(pool, pool_steps)

            pool.wait_ge(setup_loaded, 32)
            for l in range(DEPTH):
                flat_v = work[:, LNV:LNV + 2048]
                load_vectors(flat_v, 8 * l, 2)
                rstd()
                rstd()
                load_vectors(flat_v, 8 * l + 2, 2)
                rstd()
                load_vectors(flat_v, 8 * l + 4, 2)
                rstd()
                load_vectors(flat_v, 8 * l + 6, 2)
                pool.wait_ge(x_ready, 3 * l + 2)
                tag = f"{l}.moe"
                def load_ada(n):
                    pool.dma_start(ada_in[n % 2], ada[l, n:n + 1, :, :].rearrange("e p (c n) -> p (e c) n", c=DC + 1)) \
                        .then_inc(ada_loaded[n % 2], 16)

                load_ada(0)
                for n in range(2 * NEXP):
                    if n:
                        pool.wait_ge(ada_summed, 2 * NEXP * l + n)
                    if n < 2 * NEXP - 1:
                        load_ada(n + 1)
                    if n > 1 and n % 2 == 0:
                        before = n // 2 - 1
                        banks.wait_full(pool, f"{tag}.ada{before % EXP_PER_BODY}", rounds=before // EXP_PER_BODY)
                    pool.wait_ge(ada_loaded[n % 2], 16 * (NEXP * l + n // 2 + 1))
                    here = ada_in[n % 2]
                    part = here[:, 0:DC, :]
                    step(nc.gpsimd.tensor_tensor(part, part, sm("sc").unsqueeze(2).broadcast_to([P, DC, ADA_PART]), ALU.mult))
                    for c in (4, 2, 1):
                        step(nc.gpsimd.tensor_tensor(here[:, 0:c, :], here[:, 0:c, :], here[:, c:2 * c, :], ALU.add))
                    nc.gpsimd.tensor_tensor(ada_acc[:, n % 2 * ADA_PART:(n % 2 + 1) * ADA_PART], here[:, 0, :],
                                            here[:, DC, :], ALU.add).then_inc(ada_summed, 1)
                rstd()
            rstd()
            pool.wait_ge(x_ready, 6)
            nc.gpsimd.memset(work[:, NS + 1024:NS + 3360], 0.0).then_inc(zeros_set, 1)
            banks.wait_drained(pool, "e.vc")
            nc.gpsimd.memset(work[:, MB + 1024:MB + 5120], 0.0).then_inc(zeros_set, 1)
            rstd()
            pool.wait_ge(x_ready, 7)
            w0 = bias[:, :, 1, 0:P]
            nc.gpsimd.affine_select(out=w0, in_=w0, pattern=[[0, 8], [1, P]], compare_op=ALU.is_gt, fill=NEG,
                                    base=0, channel_multiplier=-1).then_inc(bias_ready, 1)
            rstd()
            pool.wait_ge(x_ready, 8)
            nc.gpsimd.memset(work[:, NS + 7040:NS + 8576], 0.0).then_inc(zeros_set, 1)
            rstd()
            rstd()
            pool.wait_ge(x_ready, 9)
            load_vectors(work[:, LNV:LNV + D], 16, 1)
            rstd()

        @block.sync
        def _(sp):
            def load(g, j, static=False):
                src = weights[g * RING + j] if static else \
                    weights[bass.ds(g * RING + j, 1), :, :].rearrange("m p n -> p (m n)")
                sp.dma_start(ring[:, j, :], src).then_inc(slot_full[j], 16)

            for j in range(RING):
                if j == 1:
                    sp.wait_ge(xT_loaded, 16)
                load(0, j, True)
            rounds = NPIECES // RING
            with sp.Fori(1, rounds) as g:
                for j in range(RING):
                    sp.wait_ge(halves_done, g * (2 * RING) + 2 * (j - RING + 1))
                    load(g, j)
            for j in range(NPIECES - rounds * RING):
                sp.wait_ge(halves_done, 2 * (rounds * RING + j - RING + 1))
                load(rounds, j, True)
            for T in range(NT):
                sp.wait_ge(out_ready, T + 1)
                sp.dma_start(out[T * P:(T + 1) * P, :], mix[:, T, :]).then_inc(out_stored, 16)
            sp.wait_ge(out_stored, 16 * NT)


def chunks(w):
    k, n = w.shape
    return w.reshape(k // P, P, n).transpose(1, 0, 2).reshape(P, -1)


def pairs(w):
    return w.reshape(w.shape[0], 2, PAIRS, DH).transpose(0, 2, 1, 3).reshape(w.shape[0], -1)


def layouts(a):
    weights = np.zeros((NPIECES, P, PIECE), np.float32)
    at = [0]

    def put(*parts):
        col = 0
        for part in parts:
            weights[at[0], :, col:col + part.shape[1]] = part
            col += part.shape[1]
        at[0] += 1

    def put_cols(w):
        full = np.zeros((D, -(-w.shape[1] // 512) * 512), np.float32)
        full[:, :w.shape[1]] = w
        for q in range(full.shape[1] // 512):
            put(chunks(full[:, q * 512:(q + 1) * 512]))

    def put_experts(g, u, d):
        of = {"g": g, "u": u, "d": d}
        for group in range(GROUPS):
            for what, e in GROUP_ORDER:
                put(chunks(of[what][PER_GROUP * group + e]))

    for l in range(DEPTH):
        w = a["w_in"][l]
        put_cols(w[:, 0:512])
        put_cols(w[:, 512:1024])
        put_cols(w[:, 1024:1536])
        put_cols(w[:, 1552:2576])
        put_cols(a["wk_x"][l])
        put_cols(a["wv_x"][l])
        put_cols(a["w_out"][l])
        put_cols(a["wq_x"][l])
        put_cols(a["wo_x"][l])
        put_experts(a["w_gate"][l], a["w_up"][l], a["w_down"][l])

    def pair_rows(w):
        return pairs(w.T).T

    w = a["ev_w_in_2"][0]
    put_cols(pairs(w[:, 0:512]))
    put_cols(w[:, 512:1024])
    put_cols(w[:, 1024:1280])
    put(chunks(a["nsa_ck_w1_2"][0]))
    put(chunks(a["nsa_cv_w1_2"][0]))
    for q in range(3):
        put_cols(pairs(w[:, 1304 + 512 * q:1816 + 512 * q]))
    wo = a["ev_w_out_2"][0]
    put_cols(np.concatenate([pair_rows(wo[:512]), pair_rows(wo[512:])]))
    put_experts(a["moe_w_gate_2"][0], a["moe_w_up_2"][0], a["moe_w_down_2"][0])
    w = a["od_w_in_2"][0]
    put_cols(w[:, 0:448])
    put(chunks(a["mla_w_q_up_2"][0]), a["mla_w_kv_up_2"][0])
    put_cols(pairs(w[:, 448:960]))
    put_cols(w[:, 960:1216])
    wo = a["od_w_out_2"][0]
    put_cols(np.concatenate([wo[:512], pair_rows(wo[512:])]))
    put_experts(a["moe_w_gate_2"][1], a["moe_w_up_2"][1], a["moe_w_down_2"][1])
    assert at[0] == NPIECES, at

    parts = 6 * D // ADA_PART
    ada = np.zeros((DEPTH, parts, P, DC + 1, ADA_PART), np.float32)
    ada[:, :, :, 0:DC] = a["ada_w_2"].reshape(DEPTH, DC, P, parts, ADA_PART).transpose(0, 3, 2, 1, 4)
    ada[:, :, 0, DC] = a["ada_b_2"].reshape(DEPTH, parts, ADA_PART)

    prm = np.zeros((P, PARAM_N), np.float32)

    def param(name, v):
        lo, hi = PARAM[name]
        prm[:v.shape[0], lo:hi] = v.reshape(v.shape[0], hi - lo)

    def col(v):
        return v.reshape(-1, P).T

    def rows(v):
        return np.broadcast_to(v, (P, v.shape[0]))

    param("w_alow", np.concatenate([chunks(a["w_in"][l][:, 1536:1552]) for l in range(2)], 1))
    param("w_router", chunks(a["w_router"]))
    param("router_w_2", chunks(a["router_w_2"]))
    param("w_gates", chunks(a["ev_w_in_2"][0][:, 1280:1304]))
    param("b_s", a["b_s"].transpose(2, 0, 1).reshape(P, 8))
    param("w_s", a["w_s"].transpose(3, 0, 1, 2).reshape(P, -1))
    param("w_a2", np.concatenate([np.concatenate([a["w_a2"][l], a["b_a"][l][None]]) for l in range(2)], 1))
    param("c", col(a["c_2"]))
    param("norm_mix", np.concatenate([col(a["norm_mix_2"][l]) for l in range(2)], 1))
    param("norm_ffn", np.concatenate([col(a["norm_ffn_2"][l]) for l in range(2)], 1))
    param("q_norm", col(a["mla_q_norm_2"]))
    param("kv_norm", col(a["mla_kv_norm_2"]))
    for name, key in (("pos_k", "nsa_pos_k_2"), ("pos_v", "nsa_pos_v_2")):
        param(name, a[key][0].reshape(16, 2, DH).transpose(1, 2, 0).reshape(P, 16))
    param("ck_w2", chunks(a["nsa_ck_w2_2"][0]))
    param("cv_w2", chunks(a["nsa_cv_w2_2"][0]))
    param("rel_table", np.concatenate([a["rel_table_2"], np.ones((1, 8), np.float32)]))
    param("rel_rows", rows(np.concatenate([a["rel_table_2"].T, a["swa_sinks_2"][0][:, None]], 1).reshape(-1)))
    param("b_router", rows(a["b_router"]))
    param("router_b_2", rows(a["router_b_2"]))

    vecs = np.zeros((17, D), np.float32)
    for l in range(DEPTH):
        vecs[8 * l, :512] = a["gla_norm_g"][l]
        vecs[8 * l, 512:] = a["sgu_ln_g"][l]
        vecs[8 * l + 1, :512] = a["sgu_ln_b"][l]
        for k in range(3):
            vecs[8 * l + 2 + 2 * k] = a["ln_g"][l, k]
            vecs[8 * l + 3 + 2 * k] = a["ln_b"][l, k]
    vecs[16] = a["final_norm_2"]
    x = a["x"][0]
    return {
        "weights": weights, "ada": ada.reshape(DEPTH, parts, P, ADA_ROW), "cst": constants(), "prm": prm, "vecs": vecs,
        "x_in": np.ascontiguousarray(x.reshape(NT, P, D).transpose(1, 0, 2)),
        "xT_in": np.ascontiguousarray(x.T.reshape(DC, P, S).transpose(1, 0, 2)),
        "memT_in": np.ascontiguousarray(a["mem"][0].T.reshape(DC, P, S).transpose(1, 0, 2)),
    }


def kernel(**inputs):
    import concourse.bacc as bacc
    from concourse.bass_utils import run_bass_kernel_spmd

    arrays = layouts({k: np.asarray(v) for k, v in inputs.items()})
    nc = bacc.Bacc("TRN2", target_bir_lowering=False, num_devices=1)
    args = [nc.dram_tensor(f"in_{k}", v.shape, F32, kind="ExternalInput").ap() for k, v in arrays.items()]
    out = nc.dram_tensor("out", (S, D), F32, kind="ExternalOutput").ap()
    scratch = nc.dram_tensor("bias_rows", (8, P * (UROW + 1)), F32, kind="Internal").ap()
    program(nc, *args, out, scratch)
    r = run_bass_kernel_spmd(nc, [{f"in_{k}": v for k, v in arrays.items()}], core_ids=[0])
    return r.results[0]["out"].reshape(1, S, D)
```
